# Optimizing a Trainium2 kernel written in Bass

```python
import math
import jax, jax.numpy as jnp
from jax import lax
import numpy as np

D_MODEL = 1024
BATCH = 1
SEQ = 2048
DEPTH = 1

GRID_W = 64
HEAD_DIM = 64
NA_HEADS = 8
NA_WIDTH = NA_HEADS * HEAD_DIM
NA_KH_MAX = 8
NA_KW = 16
NA_COL_BLOCK = 16
NA_KEY_COLS = 32
DIFF_HEADS = 4
DIFF_WIDTH = DIFF_HEADS * 2 * HEAD_DIM
MIX_WIDTH = NA_WIDTH + DIFF_WIDTH
IN_WIDTH = 3 * NA_WIDTH + 3 * DIFF_WIDTH
N_EXPERTS = 16
EC_CAPACITY_FACTOR = 2
D_FF_EXPERT = 1024
PLE_DIM = 256
Q_BLOCK = 128
EPS = 1e-6

kernel_name = "hybrid_na_diffattn_ec_moe_encoder"

def rmsnorm(x, g):
    xf = x.astype(jnp.float32)
    y = xf * lax.rsqrt(jnp.mean(xf * xf, axis=-1, keepdims=True) + EPS)
    return (y * g.astype(jnp.float32)).astype(x.dtype)

def alibi_slopes(n_heads):
    return jnp.exp2(-8.0 * jnp.arange(1, n_heads + 1, dtype=jnp.float32) / n_heads)

def neighbourhood_attention(q, k, v, rpb):
    B, S, H, dh = q.shape
    rows = S // GRID_W
    kh = min(NA_KH_MAX, rows)
    ncb = GRID_W // NA_COL_BLOCK
    qg = q.reshape(B, rows, ncb, NA_COL_BLOCK, H, dh)
    kg = k.reshape(B, rows, GRID_W, H, dh)
    vg = v.reshape(B, rows, GRID_W, H, dh)
    qcol = np.arange(GRID_W).reshape(ncb, NA_COL_BLOCK)
    kblk = np.clip(np.arange(ncb) * NA_COL_BLOCK - NA_KW // 2, 0, GRID_W - NA_KEY_COLS)
    kcol = kblk[:, None] + np.arange(NA_KEY_COLS)
    cstart = np.clip(qcol - NA_KW // 2, 0, GRID_W - NA_KW)
    kc = kcol[:, None, :]
    col_ok = (kc >= cstart[..., None]) & (kc < cstart[..., None] + NA_KW)
    dc = np.clip(kc - qcol[..., None] + NA_KW - 1, 0, 2 * NA_KW - 2)
    rpb_c = rpb[:, :, dc].astype(jnp.float32)
    mask = jnp.asarray(col_ok)[:, :, None, :]

    def row(r):
        rs = jnp.clip(r - kh // 2, 0, rows - kh)
        q_r = lax.dynamic_index_in_dim(qg, r, axis=1, keepdims=False)
        k_rows = lax.dynamic_slice_in_dim(kg, rs, kh, axis=1)
        v_rows = lax.dynamic_slice_in_dim(vg, rs, kh, axis=1)
        k_b = k_rows[:, :, kcol]
        v_b = v_rows[:, :, kcol]
        dr = rs + jnp.arange(kh) - r + NA_KH_MAX - 1
        bias = rpb_c[:, dr].transpose(0, 2, 3, 1, 4)
        s = jnp.einsum('bnqhd,brnjhd->bhnqrj', q_r, k_b).astype(jnp.float32)
        s = jnp.where(mask, s + bias[None], -jnp.inf)
        pr = jax.nn.softmax(s, axis=(-2, -1))
        o = jnp.einsum('bhnqrj,brnjhd->bnqhd', pr.astype(v.dtype), v_b)
        return o.reshape(B, GRID_W, H, dh)

    o = lax.map(row, jnp.arange(rows))
    return o.transpose(1, 0, 2, 3, 4).reshape(B, S, H, dh)

def differential_attention(q, k, v, lam, slopes):
    B, S, H, _, dh = q.shape
    nb = S // Q_BLOCK
    qb = q.reshape(B, nb, Q_BLOCK, H, 2, dh).transpose(1, 0, 2, 3, 4, 5)
    kpos = jnp.arange(S, dtype=jnp.float32)

    def block(args):
        q_i, i = args
        s = jnp.einsum('bqhcd,bkhcd->bhcqk', q_i, k).astype(jnp.float32)
        qpos = (i * Q_BLOCK + jnp.arange(Q_BLOCK)).astype(jnp.float32)
        dist = jnp.abs(qpos[:, None] - kpos[None, :])
        s = s - slopes[:, None, None, None] * dist
        pr = jax.nn.softmax(s, axis=-1)
        a = pr[:, :, 0] - lam * pr[:, :, 1]
        return jnp.einsum('bhqk,bkhe->bqhe', a.astype(v.dtype), v)

    o = lax.map(block, (qb, jnp.arange(nb)))
    return o.transpose(1, 0, 2, 3, 4).reshape(B, S, H, 2 * dh)

def expert_choice_moe(x, w_router, w_gate, w_up, w_down):
    B, S, D = x.shape
    cap = EC_CAPACITY_FACTOR * S // N_EXPERTS
    aff = jax.nn.softmax((x @ w_router).astype(jnp.float32), axis=-1)
    g, idx = lax.top_k(aff.transpose(0, 2, 1), cap)
    xs = jax.vmap(lambda xb, ib: xb[ib])(x, idx)
    hid = jax.nn.silu(jnp.einsum('becd,edf->becf', xs, w_gate)) * jnp.einsum('becd,edf->becf', xs, w_up)
    y = jnp.einsum('becf,efd->becd', hid, w_down) * g[..., None].astype(x.dtype)
    return jax.vmap(lambda yb, ib: jax.ops.segment_sum(
        yb.reshape(-1, D), ib.reshape(-1), num_segments=S))(y, idx)

def setup_inputs(seed: int = 0) -> dict:
    key = jax.random.key(seed)
    ks = jax.random.split(key, 24)
    f32 = jnp.float32
    nrm = lambda k, shape, scale: jax.random.normal(k, shape, f32) * scale
    gain = lambda k, shape: 1.0 + 0.05 * jax.random.normal(k, shape, f32)
    L, D, E, F = DEPTH, D_MODEL, N_EXPERTS, D_FF_EXPERT
    return {
        "x": nrm(ks[0], (BATCH, SEQ, D), 1.0),
        "p": nrm(ks[1], (L, BATCH, SEQ, PLE_DIM), 1.0),
        "g_mix": gain(ks[2], (L, D)),
        "w_in": nrm(ks[3], (L, D, IN_WIDTH), D ** -0.5),
        "na_rpb": nrm(ks[4], (L, NA_HEADS, 2 * NA_KH_MAX - 1, 2 * NA_KW - 1), 0.02),
        "g_na_out": gain(ks[5], (L, NA_HEADS, HEAD_DIM)),
        "lam_q1": nrm(ks[6], (L, HEAD_DIM), 0.1),
        "lam_k1": nrm(ks[7], (L, HEAD_DIM), 0.1),
        "lam_q2": nrm(ks[8], (L, HEAD_DIM), 0.1),
        "lam_k2": nrm(ks[9], (L, HEAD_DIM), 0.1),
        "g_diff_out": gain(ks[10], (L, 2 * HEAD_DIM)),
        "w_out": nrm(ks[11], (L, MIX_WIDTH, D), MIX_WIDTH ** -0.5),
        "g_moe": gain(ks[12], (L, D)),
        "w_router": nrm(ks[13], (L, D, E), D ** -0.5),
        "w_gate": nrm(ks[14], (L, E, D, F), D ** -0.5),
        "w_up": nrm(ks[15], (L, E, D, F), D ** -0.5),
        "w_down": nrm(ks[16], (L, E, F, D), F ** -0.5),
        "g_ple": gain(ks[17], (L, D)),
        "w_ple_gate": nrm(ks[18], (L, D, D), D ** -0.5),
        "w_ple_proj": nrm(ks[19], (L, PLE_DIM, D), PLE_DIM ** -0.5),
        "g_final": gain(ks[20], (D,)),
    }

def reference(x, p, g_mix, w_in, na_rpb, g_na_out, lam_q1, lam_k1, lam_q2, lam_k2,
              g_diff_out, w_out, g_moe, w_router, w_gate, w_up, w_down,
              g_ple, w_ple_gate, w_ple_proj, g_final):
    B, S, D = x.shape
    scale = HEAD_DIM ** -0.5
    slopes = alibi_slopes(DIFF_HEADS)
    splits = [NA_WIDTH, 2 * NA_WIDTH, 3 * NA_WIDTH,
              3 * NA_WIDTH + DIFF_WIDTH, 3 * NA_WIDTH + 2 * DIFF_WIDTH]
    h = x
    for i in range(DEPTH):
        hn = rmsnorm(h, g_mix[i])
        proj = hn @ w_in[i]
        q_na, k_na, v_na, q_df, k_df, v_df = jnp.split(proj, splits, axis=-1)

        o_na = neighbourhood_attention(
            q_na.reshape(B, S, NA_HEADS, HEAD_DIM) * scale,
            k_na.reshape(B, S, NA_HEADS, HEAD_DIM),
            v_na.reshape(B, S, NA_HEADS, HEAD_DIM),
            na_rpb[i])
        o_na = rmsnorm(o_na, g_na_out[i]).reshape(B, S, NA_WIDTH)

        lam_init = 0.8 - 0.6 * math.exp(-0.3 * i)
        lam = (jnp.exp(jnp.sum(lam_q1[i].astype(jnp.float32) * lam_k1[i].astype(jnp.float32)))
               - jnp.exp(jnp.sum(lam_q2[i].astype(jnp.float32) * lam_k2[i].astype(jnp.float32)))
               + lam_init)
        o_df = differential_attention(
            q_df.reshape(B, S, DIFF_HEADS, 2, HEAD_DIM) * scale,
            k_df.reshape(B, S, DIFF_HEADS, 2, HEAD_DIM),
            v_df.reshape(B, S, DIFF_HEADS, 2 * HEAD_DIM),
            lam, slopes)
        o_df = (rmsnorm(o_df, g_diff_out[i]) * (1.0 - lam_init)).reshape(B, S, DIFF_WIDTH)

        h = h + jnp.concatenate([o_na, o_df], axis=-1) @ w_out[i]

        h = h + expert_choice_moe(rmsnorm(h, g_moe[i]), w_router[i],
                                  w_gate[i], w_up[i], w_down[i])

        h = h + jax.nn.sigmoid(rmsnorm(h, g_ple[i]) @ w_ple_gate[i]) * (p[i] @ w_ple_proj[i])
    return rmsnorm(h, g_final)


_drawn_inputs = setup_inputs


def setup_inputs(seed=0):
    import zlib

    import numpy as np

    out = dict(_drawn_inputs(seed))
    spreads = {}
    factors = {'na_rpb': 4.686, 'lam_q1': 4.32, 'lam_k2': 8.0, 'g_moe': 2.827, 'g_ple': 126.27}
    for name, (base, spread) in spreads.items():
        noise = np.random.default_rng([zlib.crc32(name.encode()), seed]).standard_normal(out[name].shape)
        drawn = base * np.exp(spread * noise) if base else spread * noise
        out[name] = __import__('jax').numpy.asarray(drawn.astype(out[name].dtype))
    for name, factor in factors.items():
        out[name] = (out[name] * factor).astype(out[name].dtype)
    return out
```

```python
from contextlib import ExitStack

import concourse.bass as bass
from concourse import mybir

F32 = mybir.dt.float32
F32R = mybir.dt.float32r
BF16 = mybir.dt.bfloat16
U32 = mybir.dt.uint32
I32 = mybir.dt.int32
ALU = mybir.AluOpType
ACT = mybir.ActivationFunctionType
AX = mybir.AxisListType

P = 128
BANK = 512
SEQ = 2048
D = 1024
KB = D // P
TILES = SEQ // P
EPS = 1e-6

GRID_W = 64
ROWS = SEQ // GRID_W
DH = 64
NA_HEADS = 8
PAIRS = NA_HEADS // 2
KH = 8
KW = 16
NA_KEYS = KH * GRID_W
DIFF_HEADS = 4
LAM_INIT = 0.8 - 0.6
NEG = -1e30

E = 16
CAP = 2 * SEQ // E
F = 1024
PLE = 256
EXP_SCALE = DH ** -0.5


class Parts:

    def __init__(self, nc, name):
        self.nc, self.name, self.stack, self.sems = nc, name, ExitStack(), []

    def __enter__(self):
        self.stack.__enter__()
        return self

    def __exit__(self, *a):
        self.stack.__exit__(*a)
        if self.sems:
            self.nc.clear_and_free_semaphores(self.sems)
            self.nc.all_engine_barrier()

    def sb(self, name, shape, dt=F32):
        return self.stack.enter_context(self.nc.sbuf_tensor(f"{self.name}_{name}", shape, dt))

    def psum(self, name, shape, dt=F32):
        return self.stack.enter_context(self.nc.psum_tensor(f"{self.name}_{name}", shape, dt))

    def sem(self, name):
        self.sems.append(self.nc.alloc_semaphore(name=f"{self.name}_{name}"))
        return self.sems[-1]

    def block(self):
        return self.stack.enter_context(self.nc.Block())


def first_apart(eng, count, fn):
    fn(0)
    with eng.Fori(1, count) as g:
        fn(g)


def numbered(g, k):
    return isinstance(g, int) and g == k


def credit(eng, sem, n):
    eng.nop().then_inc(sem, n)


def identity_steps(pool, ident, sem):
    pool.memset(ident[:, :], 0.0).then_inc(sem, 1)
    pool.wait_ge(sem, 1)
    pool.affine_select(out=ident[:, :], in_=ident[:, :], compare_op=ALU.not_equal, fill=1.0, base=0,
                       pattern=[[-1, P]], channel_multiplier=1).then_inc(sem, 1)


def project(nc, x, g_mix, w_in, feat_t, v_tok):
    CW = 256
    GRP = 4
    HALF = 3 * D // 2
    UNITS = 8
    with Parts(nc, "pr") as m:
        xt = m.sb("xt", [P, GRP, D])
        junk = m.sb("junk", [P, D])
        ss = m.sb("ss", [P, GRP])
        ms = m.sb("ms", [P, GRP])
        rs = m.sb("rs", [P, GRP])
        mhalf = m.sb("mhalf", [P, GRP])
        gain = m.sb("gain", [P, KB])
        ident = m.sb("ident", [P, P])
        h_hi = m.sb("h_hi", [P, KB, SEQ], F32R)
        h_lo = m.sb("h_lo", [P, KB, SEQ], F32R)
        wst = [m.sb(f"wst{b}", [P, KB, CW]) for b in range(2)]
        w_hi = [m.sb(f"w_hi{b}", [P, KB, CW], F32R) for b in range(2)]
        w_lo = [m.sb(f"w_lo{b}", [P, KB, CW], F32R) for b in range(2)]
        stage = m.sb("stage", [P, 4, BANK])
        turned = m.psum("turned", [P, 4, BANK])
        out = m.psum("out", [P, 4, BANK])

        x_in = [m.sem(f"x_in{s}") for s in range(GRP)]
        gain_in = m.sem("gain_in")
        w_loaded = [m.sem(f"w_loaded{b}") for b in range(2)]
        consts = m.sem("consts")
        squares = m.sem("squares")
        pool_own = m.sem("pool_own")
        means = m.sem("means")
        rs_ready = m.sem("rs_ready")
        normed = m.sem("normed")
        turned_ready = m.sem("turned_ready")
        hi_ready = m.sem("hi_ready")
        lo_ready = m.sem("lo_ready")
        whi_ready = m.sem("whi_ready")
        wlo_ready = m.sem("wlo_ready")
        out_ready = m.sem("out_ready")
        out_free = m.sem("out_free")
        stored = [m.sem(f"stored{s}") for s in range(4)]

        x_v = x.rearrange("o (g s p) d -> (o g) s p d", s=GRP, p=P)
        w_v = w_in.rearrange("l (k p) c -> (l p) k c", p=P)
        block = m.block()

        @block.sync
        def _(sp):
            sp.dma_start(gain[:, :], g_mix.rearrange("l (k p) -> (l p) k", p=P),
                         allow_slow_non_contiguous=True).then_inc(gain_in, 16)
            for s in range(GRP):
                sp.dma_start(xt[:, s, :], x_v[0, s]).then_inc(x_in[s], 16)
            for b in range(2):
                sp.dma_start(wst[b][:, :, :], w_v[:, :, b * CW:(b + 1) * CW]).then_inc(w_loaded[b], 16)
            with sp.Fori(1, TILES // GRP) as g:
                sp.wait_ge(turned_ready, g * KB)
                for s in range(GRP):
                    sp.dma_start(xt[:, s, :], x_v[g, s]).then_inc(x_in[s], 16)

            def store(src_unit, dst, u):
                sp.wait_ge(out_free, src_unit + 5)
                sp.dma_start(dst, stage[:, u % 4, :]).then_inc(stored[u % 4], 16)

            with sp.Fori(0, 2) as half:
                with sp.Fori(0, 2) as j:
                    for b in range(2):
                        sp.wait_ge(wlo_ready, half * 6 + j * 2 + b + 1)
                        sp.dma_start(wst[b][:, :, :], w_v[:, :, bass.ds(half * HALF + j * 2 * CW + (b + 2) * CW, CW)]
                                     ).then_inc(w_loaded[b], 16)
                        for u in range(UNITS):
                            ft, tg = u // 4, u % 4
                            store(half * 48 + j * 16 + b * 8 + u,
                                  feat_t[half, bass.ds(j * 2 * CW + b * CW + ft * P, P), tg * BANK:(tg + 1) * BANK], u)
                for b in range(2):
                    sp.wait_ge(wlo_ready, half * 6 + 4 + b + 1)
                    sp.dma_start(wst[b][:, :, :], w_v[:, :, b * CW + HALF:(b + 1) * CW + HALF]).then_inc(w_loaded[b], 16)
                    for u in range(UNITS):
                        store(half * 48 + 32 + b * 8 + u,
                              v_tok[half, u * 2 * P:(u + 1) * 2 * P, b * CW:(b + 1) * CW].rearrange(
                                  "(a p) c -> p a c", p=P), u)
            for s in range(4):
                sp.wait_ge(stored[s], 16 * 24)
            for b in range(2):
                sp.wait_ge(w_loaded[b], 16 * 7)

        @block.gpsimd
        def _(pool):
            identity_steps(pool, ident, consts)
            pool.memset(mhalf[:, :], -0.5).then_inc(pool_own, 1)
            pool.wait_ge(pool_own, 1)

            def group(g):
                pool.wait_ge(means, g + 1)
                if not numbered(g, 0):
                    pool.wait_ge(normed, g * GRP)
                pool.tensor_tensor(rs[:, :], ms[:, :], mhalf[:, :], ALU.pow).then_inc(rs_ready, 1)

            first_apart(pool, TILES // GRP, group)
            with pool.Fori(0, 6) as c2:
                for b in range(2):
                    pool.wait_ge(whi_ready, c2 * 2 + b + 1)
                    pool.tensor_tensor(w_lo[b][:, :, :], wst[b][:, :, :], w_hi[b][:, :, :].bitcast(F32), ALU.subtract
                                       ).then_inc(wlo_ready, 1)

        @block.scalar
        def _(act):
            act.wait_ge(gain_in, 16)

            def group(g):
                for s in range(GRP):
                    act.wait_ge(x_in[s], g * 16 + 16)
                    if s == 0 and not numbered(g, 0):
                        act.wait_ge(rs_ready, g)
                    if not (s == 0 and numbered(g, 0)):
                        act.wait_ge(squares, g * GRP + s)
                    act.activation(junk[:, :], xt[:, s, :], ACT.Square, accum_out=ss[:, s:s + 1]).then_inc(squares, 1)
                for k in range(KB):
                    act.wait_ge(turned_ready, g * KB + k + 1)
                    act.activation(h_hi[:, k, bass.ds(g * BANK, BANK)], turned[:, k % 4, :], ACT.Copy,
                                   scale=gain[:, k:k + 1]).then_inc(hi_ready, 1)

            first_apart(act, TILES // GRP, group)
            for b in range(2):
                act.wait_ge(w_loaded[b], 16)
                act.activation(w_hi[b][:, :, :], wst[b][:, :, :], ACT.Copy).then_inc(whi_ready, 1)
            with act.Fori(1, 6) as c2:
                for b in range(2):
                    act.wait_ge(w_loaded[b], c2 * 16 + 16)
                    act.wait_ge(out_ready, (c2 * 2 + b - 1) * UNITS)
                    act.activation(w_hi[b][:, :, :], wst[b][:, :, :], ACT.Copy).then_inc(whi_ready, 1)

        @block.vector
        def _(dve):
            credit(dve, out_free, 4)
            dve.wait_ge(gain_in, 16)

            def group(g):
                dve.wait_ge(squares, g * GRP + GRP)
                dve.tensor_scalar(ms[:, :], ss[:, :], 1.0 / D, EPS, ALU.mult, ALU.add).then_inc(means, 1)
                dve.wait_ge(rs_ready, g + 1)
                for s in range(GRP):
                    dve.tensor_scalar(xt[:, s, :], xt[:, s, :], rs[:, s:s + 1], None, ALU.mult).then_inc(normed, 1)
                for k in range(KB):
                    dve.wait_ge(hi_ready, g * KB + k + 1)
                    dve.scalar_tensor_tensor(out=h_lo[:, k, bass.ds(g * BANK, BANK)], in0=turned[:, k % 4, :],
                                             scalar=gain[:, k:k + 1],
                                             in1=h_hi[:, k, bass.ds(g * BANK, BANK)].bitcast(F32),
                                             op0=ALU.mult, op1=ALU.subtract).then_inc(lo_ready, 1)

            def results(v):
                for s in range(4):
                    dve.wait_ge(out_ready, v * 4 + s + 1)
                    if not numbered(v, 0):
                        dve.wait_ge(stored[s], v * 16)
                    dve.tensor_copy(stage[:, s, :], out[:, s, :]).then_inc(out_free, 1)

            first_apart(dve, TILES // GRP, group)
            first_apart(dve, 24, results)

        @block.tensor
        def _(pe):
            pe.wait_ge(consts, 2)

            def group(g):
                pe.wait_ge(normed, g * GRP + GRP)
                for k in range(KB):
                    if k >= 4:
                        pe.wait_ge(lo_ready, g * KB + k - 3)
                    elif not numbered(g, 0):
                        pe.wait_ge(lo_ready, g * KB)
                    for s in range(GRP):
                        t = pe.transpose(turned[:, k % 4, s * P:(s + 1) * P], xt[:, s, k * P:(k + 1) * P], ident[:, :])
                    t.then_inc(turned_ready, 1)

            first_apart(pe, TILES // GRP, group)
            pe.wait_ge(lo_ready, TILES // GRP * KB)

            def unit(n, u):
                pe.wait_ge(out_free, n + u + 1)

            def products(dst, lhs, rhs):
                pairs = [(a, b) for a, b in ((0, 0), (0, 1), (1, 0))]
                for k in range(KB):
                    for a, b in pairs:
                        mm = pe.matmul(dst, lhs(a, k), rhs(b, k), start=(k == 0 and (a, b) == (0, 0)),
                                       stop=(k == KB - 1 and (a, b) == (1, 0)))
                return mm

            hs = (h_hi, h_lo)

            def features(n, b):
                ws = (w_hi[b], w_lo[b])
                for u in range(UNITS):
                    ft, tg = u // 4, u % 4
                    unit(n, u)
                    mm = products(out[:, u % 4, :], lambda a, k: ws[a][:, k, ft * P:(ft + 1) * P],
                                  lambda c, k: hs[c][:, k, tg * BANK:(tg + 1) * BANK])
                    mm.then_inc(out_ready, 1)

            def tokens(n, b):
                ws = (w_hi[b], w_lo[b])
                for u in range(UNITS):
                    unit(n, u)
                    for a2 in range(2):
                        t = 2 * u + a2
                        mm = products(out[:, u % 4, a2 * CW:(a2 + 1) * CW], lambda a, k: hs[a][:, k, t * P:(t + 1) * P],
                                      lambda c, k: ws[c][:, k, :])
                    mm.then_inc(out_ready, 1)

            with pe.Fori(0, 2) as half:
                with pe.Fori(0, 2) as j:
                    for b in range(2):
                        pe.wait_ge(wlo_ready, half * 6 + j * 2 + b + 1)
                        features(half * 48 + j * 16 + b * 8, b)
                for b in range(2):
                    pe.wait_ge(wlo_ready, half * 6 + 4 + b + 1)
                    tokens(half * 48 + 32 + b * 8, b)


def neighbourhood(nc, feat_t, v_tok, na_bias, o_cat):
    STEPS = PAIRS * ROWS
    UNROLL = 4
    LAG = 4
    with Parts(nc, "na") as m:
        ident = m.sb("ident", [P, P])
        own = m.sb("own", [P, 2, DH])
        q_raw = [m.sb(f"q_raw{i}", [P, SEQ]) for i in range(2)]
        k_st = m.sb("k_st", [P, SEQ])
        v_st = [m.sb(f"v_st{o}", [P, TILES, P]) for o in range(2)]
        k_hi = [m.sb(f"k_hi{i}", [P, SEQ], F32R) for i in range(2)]
        k_lo = [m.sb(f"k_lo{i}", [P, SEQ], F32R) for i in range(2)]
        v_parts = [[m.sb(f"v_parts{i}{o}", [P, TILES - o, 2, P], F32R) for o in range(2)] for i in range(2)]
        table = [m.sb(f"table{i}", [P, 2 * KH - 1, GRID_W]) for i in range(2)]
        q_own = [m.sb(f"q_own{b}", [P, P]) for b in range(2)]
        q_hi = [m.sb(f"q_hi{b}", [P, P], F32R) for b in range(2)]
        q_lo = [m.sb(f"q_lo{b}", [P, P], F32R) for b in range(2)]
        probs = [m.sb(f"probs{b}", [P, NA_KEYS]) for b in range(UNROLL)]
        nmax = [m.sb(f"nmax{b}", [P, 1]) for b in range(2)]
        sums = [m.sb(f"sums{b}", [P, 1]) for b in range(2)]
        recip = [m.sb(f"recip{b}", [P, 1]) for b in range(2)]
        t_hi = [m.sb(f"t_hi{b}", [P, BANK], F32R) for b in range(2)]
        t_lo = [m.sb(f"t_lo{b}", [P, BANK], F32R) for b in range(2)]
        o_part = [m.sb(f"o_part{b}", [P, P]) for b in range(2)]
        o_all = [m.sb(f"o_all{i}", [P, ROWS, DH]) for i in range(2)]
        s_ps = m.psum("s_ps", [P, 2, BANK])
        t_ps = m.psum("t_ps", [P, 2, BANK])
        o_ps = m.psum("o_ps", [P, 2, BANK])

        consts = m.sem("consts")
        own_ready = m.sem("own_ready")
        q_loaded = m.sem("q_loaded")
        k_loaded = m.sem("k_loaded")
        v_loaded = m.sem("v_loaded")
        table_loaded = m.sem("table_loaded")
        k_hi_ready = m.sem("k_hi_ready")
        k_lo_ready = m.sem("k_lo_ready")
        v_hi_ready = m.sem("v_hi_ready")
        v_lo_ready = m.sem("v_lo_ready")
        q_own_ready = m.sem("q_own_ready")
        q_hi_ready = m.sem("q_hi_ready")
        q_lo_ready = m.sem("q_lo_ready")
        s_ready = m.sem("s_ready")
        biased = m.sem("biased")
        exped = m.sem("exped")
        recips = m.sem("recips")
        t_ready = m.sem("t_ready")
        thi_ready = m.sem("thi_ready")
        tlo_ready = m.sem("tlo_ready")
        pv_done = m.sem("pv_done")
        o_part_ready = m.sem("o_part_ready")
        o_ready = m.sem("o_ready")
        o_stored = m.sem("o_stored")
        ticks = m.sem("ticks")
        block = m.block()

        q_dram = feat_t[0, 0:BANK, :].rearrange("(h d) t -> h d t", d=P)
        k_dram = feat_t[0, BANK:2 * BANK, :].rearrange("(h d) t -> h d t", d=P)
        v_dram = v_tok[0].rearrange("t (h e) -> h t e", e=P)

        def run(eng, fn):
            for h in range(PAIRS):
                for i in range(2 * UNROLL):
                    fn(h * ROWS + i, i % UNROLL, h, i)
                with eng.Fori(2, ROWS // UNROLL - 1) as j:
                    for s in range(UNROLL):
                        fn(j * UNROLL + (h * ROWS + s), s, h, (j, s))
                for i in range(ROWS - UNROLL, ROWS):
                    fn(h * ROWS + i, i % UNROLL, h, i)
            for i in range(LAG):
                fn(STEPS + i, i, PAIRS, i)

        def inner(i):
            return isinstance(i, tuple)

        def window(i):
            return min(max(i - KH // 2, 0), ROWS - KH)

        def at(i, k):
            return not inner(i) and i == k

        def has(n, i, lag):
            return inner(i) or 0 <= n - lag < STEPS

        def place(h, i, lag):
            if inner(i):
                return h, (i[0], i[1] - lag)
            return h + (i - lag) // ROWS, (i - lag) % ROWS

        def columns(row, off=0):
            if isinstance(row, tuple):
                return row[0] * (UNROLL * GRID_W) + (row[1] + off) * GRID_W
            return (row + off) * GRID_W

        @block.sync
        def _(sp):
            def load(h):
                if h >= 1:
                    sp.wait_ge(k_lo_ready, h)
                    sp.wait_ge(v_lo_ready, 2 * h)
                if h >= 2:
                    sp.wait_ge(q_own_ready, (h - 1) * ROWS)
                    sp.wait_ge(biased, (h - 1) * ROWS)
                sp.dma_start(k_st[:, :], k_dram[h]).then_inc(k_loaded, 16)
                sp.dma_start(q_raw[h % 2][:, :], q_dram[h]).then_inc(q_loaded, 16)
                sp.dma_start(table[h % 2][:, :, :].rearrange("p r c -> p (r c)"), na_bias[h]).then_inc(table_loaded, 16)
                for o in range(2):
                    sp.dma_start(v_st[o][:, 0:TILES - o, :],
                                 v_dram[h, o * GRID_W:SEQ - o * GRID_W, :].rearrange("(j p) e -> p j e", p=P)
                                 ).then_inc(v_loaded, 16)

            load(0)
            for h in range(PAIRS):
                if h < PAIRS - 1:
                    load(h + 1)
                sp.wait_ge(o_ready, 2 * ROWS * (h + 1))
                for hh in range(2):
                    sp.dma_start(o_cat.rearrange("(r q) f -> q r f", q=GRID_W)[:, :, h * P + hh * DH:h * P + (hh + 1) * DH],
                                 o_all[h % 2][hh * DH:(hh + 1) * DH, :, :]).then_inc(o_stored, 16)
            sp.wait_ge(o_stored, 16 * NA_HEADS)

        @block.gpsimd
        def _(pool):
            identity_steps(pool, ident, consts)
            pool.memset(own[:, :, :], 1.0).then_inc(own_ready, 1)
            pool.wait_ge(own_ready, 1)
            pool.affine_select(out=own[:, 0, :], in_=own[:, 0, :], compare_op=ALU.is_gt, fill=0.0, base=DH,
                               pattern=[[0, DH]], channel_multiplier=-1).then_inc(own_ready, 1)
            pool.affine_select(out=own[:, 1, :], in_=own[:, 1, :], compare_op=ALU.is_ge, fill=0.0, base=-DH,
                               pattern=[[0, DH]], channel_multiplier=1).then_inc(own_ready, 1)
            pool.wait_ge(own_ready, 3)

            def own_queries(m, b, h, row):
                if not isinstance(m, int) or m >= 2:
                    pool.wait_ge(q_lo_ready, m - 1)
                pool.wait_ge(q_loaded, 16 * (h + 1))
                pool.sem_inc(ticks, 1)
                pool.tensor_tensor(q_own[b][:, :].rearrange("p (a q) -> p a q", a=2),
                                   q_raw[h % 2][:, bass.ds(columns(row), GRID_W)].unsqueeze(1).to_broadcast([P, 2, GRID_W]),
                                   own[:, :, :], ALU.mult).then_inc(q_own_ready, 1)

            def queries_lo(m, b):
                pool.wait_ge(q_hi_ready, m + 1)
                pool.tensor_tensor(q_lo[b][:, :], q_own[b][:, :], q_hi[b][:, :].bitcast(F32), ALU.subtract
                                   ).then_inc(q_lo_ready, 1)

            def step(n, s, h, i):
                if has(n, i, -1):
                    queries_lo(n + 1, (s + 1) % 2)
                if has(n, i, -2):
                    own_queries(n + 2, s % 2, *place(h, i, -2))

            for m in range(2):
                own_queries(m, m, 0, m)
            queries_lo(0, 0)
            run(pool, step)

        @block.scalar
        def _(act):
            def split_k(h):
                act.wait_ge(k_loaded, 16 * (h + 1))
                act.activation(k_hi[h % 2][:, :], k_st[:, :], ACT.Copy, scale=EXP_SCALE).then_inc(k_hi_ready, 1)

            def split_v(h, o):
                act.wait_ge(v_loaded, 32 * (h + 1))
                act.activation(v_parts[h % 2][o][:, :, 0, :], v_st[o][:, 0:TILES - o, :], ACT.Copy).then_inc(v_hi_ready, 1)

            def queries_hi(m, b):
                act.wait_ge(q_own_ready, m + 1)
                if not isinstance(m, int) or m >= 2:
                    act.wait_ge(s_ready, m - 1)
                act.activation(q_hi[b][:, :], q_own[b][:, :], ACT.Copy).then_inc(q_hi_ready, 1)

            queries_hi(0, 0)
            split_k(0)
            split_v(0, 0)
            split_v(0, 1)

            def step(n, s, h, i):
                b = s % 2
                if has(n, i, 4):
                    act.wait_ge(pv_done, n - 3)
                    act.wait_ge(recips, n - 3)
                    if inner(i) or n >= 6:
                        act.wait_ge(o_ready, 2 * n - 10)
                    act.activation(o_part[b][:, :], o_ps[:, b, P:2 * P], ACT.Copy, scale=recip[b][:, :]
                                   ).then_inc(o_part_ready, 1)
                if has(n, i, 1):
                    act.wait_ge(biased, n)
                    if inner(i) or n >= 3:
                        act.wait_ge(recips, n - 2)
                    act.activation(probs[(s + 3) % UNROLL][:, :], probs[(s + 3) % UNROLL][:, :], ACT.Exp, bias=nmax[1 - b][:, :],
                                   scale=-1.0, accum_out=sums[1 - b][:, :]).then_inc(exped, 1)
                if has(n, i, -1):
                    queries_hi(n + 1, 1 - b)
                if has(n, i, 2):
                    act.wait_ge(t_ready, n - 1)
                    if inner(i) or n >= 4:
                        act.wait_ge(pv_done, n - 3)
                    act.activation(t_hi[b][:, :], t_ps[:, b, :], ACT.Copy).then_inc(thi_ready, 1)
                if h < PAIRS - 1:
                    if at(i, ROWS - 4):
                        split_k(h + 1)
                    if at(i, ROWS - 2):
                        split_v(h + 1, 0)
                if 1 <= h < PAIRS and at(i, 1):
                    split_v(h, 1)

            run(act, step)

        @block.vector
        def _(dve):
            def split_k(h):
                dve.wait_ge(k_hi_ready, h + 1)
                dve.scalar_tensor_tensor(out=k_lo[h % 2][:, :], in0=k_st[:, :], scalar=EXP_SCALE,
                                         in1=k_hi[h % 2][:, :].bitcast(F32), op0=ALU.mult, op1=ALU.subtract
                                         ).then_inc(k_lo_ready, 1)

            def split_v(h, o):
                dve.wait_ge(v_hi_ready, 2 * h + o + 1)
                dve.tensor_tensor(v_parts[h % 2][o][:, :, 1, :], v_st[o][:, 0:TILES - o, :],
                                  v_parts[h % 2][o][:, :, 0, :].bitcast(F32), ALU.subtract).then_inc(v_lo_ready, 1)

            split_k(0)
            split_v(0, 0)
            split_v(0, 1)

            def step(n, s, h, i):
                b = s % 2
                if has(n, i, 4):
                    ho, row = place(h, i, 4)
                    dve.wait_ge(o_part_ready, n - 3)
                    if ho >= 2 and at(row, 0):
                        dve.wait_ge(o_stored, 32 * (ho - 1))
                    row = row[0] * UNROLL + row[1] if isinstance(row, tuple) else row
                    for hh in range(2):
                        part = slice(hh * DH, (hh + 1) * DH)
                        dve.scalar_tensor_tensor(
                            out=o_all[ho % 2][part, bass.ds(row, 1), :].rearrange("p r d -> p (r d)"),
                            in0=o_ps[part, b, part], scalar=recip[b][part, :], in1=o_part[b][part, part],
                            op0=ALU.mult, op1=ALU.add).then_inc(o_ready, 1)
                if has(n, i, 0):
                    if at(i, 0):
                        dve.wait_ge(table_loaded, 16 * (h + 1))
                    dve.wait_ge(s_ready, n + 1)
                    if inner(i) or n >= 2:
                        dve.wait_ge(exped, n - 1)
                    if inner(i) or n >= 4:
                        dve.wait_ge(t_ready, n - 3)
                    dve.sem_inc(ticks, 1)
                    first = (KH - 1 - KH // 2 if inner(i) else window(i) - i + KH - 1) * GRID_W
                    dve.tensor_tensor_reduce(
                        probs[s][:, :], s_ps[:, b, :],
                        table[h % 2][:, :, :].rearrange("p r c -> p (r c)")[:, first:first + NA_KEYS],
                        -1.0, 3e38, ALU.add, ALU.min, nmax[b][:, :]).then_inc(biased, 1)
                if has(n, i, 2):
                    dve.wait_ge(exped, n - 1)
                    if inner(i) or n >= 4:
                        dve.wait_ge(o_ready, 2 * n - 6)
                    dve.reciprocal(recip[b][:, :], sums[b][:, :]).then_inc(recips, 1)
                    dve.wait_ge(thi_ready, n - 1)
                    dve.tensor_tensor(t_lo[b][:, :], t_ps[:, b, :], t_hi[b][:, :].bitcast(F32),
                                      ALU.subtract).then_inc(tlo_ready, 1)
                if h < PAIRS - 1:
                    if at(i, ROWS - 4):
                        split_k(h + 1)
                    if at(i, ROWS - 2):
                        split_v(h + 1, 0)
                if 1 <= h < PAIRS and at(i, 1):
                    split_v(h, 1)

            run(dve, step)

        @block.tensor
        def _(pe):
            pe.wait_ge(consts, 2)

            def scores(n, b, h, i):
                pe.wait_ge(q_lo_ready, n + 1)
                pe.wait_ge(k_lo_ready, h + 1)
                if inner(i) or n >= 2:
                    pe.wait_ge(biased, n - 1)
                cols = bass.ds(columns(i, -(KH // 2)) if inner(i) else columns(window(i)), NA_KEYS)
                pe.matmul(s_ps[:, b, :], q_hi[b][:, :], k_hi[h % 2][:, cols], start=True, stop=False)
                pe.matmul(s_ps[:, b, :], q_hi[b][:, :], k_lo[h % 2][:, cols], start=False, stop=False)
                pe.matmul(s_ps[:, b, :], q_lo[b][:, :], k_hi[h % 2][:, cols], start=False, stop=True).then_inc(s_ready, 1)

            def turn(n, s):
                b = s % 2
                pe.wait_ge(exped, n - 1)
                if not isinstance(n, int) or n >= 4:
                    pe.wait_ge(tlo_ready, n - 3)
                for k in range(4):
                    t = pe.transpose(t_ps[:, b, k * P:(k + 1) * P], probs[(s + 2) % UNROLL][:, k * P:(k + 1) * P], ident[:, :])
                t.then_inc(t_ready, 1)

            def values(n, s, h, i):
                c = 1 - s % 2
                hv, row = place(h, i, 3)
                pe.wait_ge(tlo_ready, n - 2)
                pe.wait_ge(v_lo_ready, 2 * hv + 2)
                if inner(i) or n >= 5:
                    pe.wait_ge(o_ready, 2 * n - 8)
                if inner(i):
                    off = row[1] - KH // 2
                    odd, first = off % 2, row[0] * (UNROLL // 2) + (off - off % 2) // 2
                else:
                    w = window(row)
                    odd, first = w % 2, w // 2
                for k in range(4):
                    blk = slice(k * P, (k + 1) * P)
                    pe.matmul(o_ps[:, c, 0:2 * P], t_hi[c][:, blk],
                              v_parts[hv % 2][odd][:, bass.ds(first + k, 1), :, :].rearrange("p r a e -> p (r a e)"),
                              start=(k == 0), stop=False, skip_group_check=True)
                    mm = pe.matmul(o_ps[:, c, 0:P], t_lo[c][:, blk],
                                   v_parts[hv % 2][odd][:, bass.ds(first + k, 1), 0, :].rearrange("p r e -> p (r e)"),
                                   start=False, stop=(k == 3), skip_group_check=True)
                mm.then_inc(pv_done, 1)

            def step(n, s, h, i):
                if has(n, i, 0):
                    scores(n, s % 2, h, i)
                if has(n, i, 2):
                    turn(n, s)
                if has(n, i, 3):
                    values(n, s, h, i)

            run(pe, step)


def tables(nc, na_rpb, alibi, rpb_rows, na_bias):
    WIDE = 2 * SEQ - P
    NR = 2 * KH - 1
    NC = 2 * KW - 1
    NPAD = 2 * GRID_W - 1
    with Parts(nc, "tb") as m:
        dist = m.sb("dist", [P, WIDE])
        absd = m.sb("absd", [P, WIDE])
        scaled = [m.sb(f"scaled{b}", [P, WIDE]) for b in range(2)]
        pad = m.sb("pad", [NA_HEADS * NR, NPAD])
        mirrored = m.sb("mirrored", [P, PAIRS, NR * GRID_W])
        mirror = m.sb("mirror", [P, P])
        tab = m.sb("tab", [P, PAIRS, NR, GRID_W])
        tab_ps = m.psum("tab_ps", [P, PAIRS, 2, BANK])
        made = m.sem("made")
        absed = m.sem("absed")
        scaled_ready = m.sem("scaled_ready")
        kept = [m.sem(f"kept{b}") for b in range(2)]
        pad_zero = m.sem("pad_zero")
        pad_in = m.sem("pad_in")
        pad_out = m.sem("pad_out")
        tab_in = m.sem("tab_in")
        mirror_ready = m.sem("mirror_ready")
        turned_round = m.sem("turned_round")
        tab_ready = m.sem("tab_ready")
        masked = m.sem("masked")
        tab_out = m.sem("tab_out")
        block = m.block()

        @block.gpsimd
        def _(pool):
            pool.memset(pad[:, :], 0.0).then_inc(pad_zero, 1)
            pool.iota(dist[:, :], pattern=[[-1, WIDE]], base=SEQ - P, channel_multiplier=1,
                      allow_small_or_imprecise_dtypes=True).then_inc(made, 1)
            pool.memset(mirror[:, :], 0.0).then_inc(mirror_ready, 1)
            for hh in range(2):
                pool.wait_ge(mirror_ready, hh + 1)
                pool.affine_select(out=mirror[:, :], in_=mirror[:, :], compare_op=ALU.not_equal, fill=1.0,
                                   base=1 - GRID_W - 2 * hh * GRID_W, pattern=[[1, P]], channel_multiplier=1
                                   ).then_inc(mirror_ready, 1)
            pool.wait_ge(tab_ready, PAIRS)
            n = 0
            for hh in range(2):
                part = tab[hh * GRID_W:(hh + 1) * GRID_W, :, :, :].rearrange("p a r c -> p (a r) c")
                low = part[:, :, 0:GRID_W - KW]
                pool.affine_select(out=low, in_=low, compare_op=ALU.is_ge, fill=NEG, base=KW // 2,
                                   pattern=[[0, PAIRS * NR], [1, GRID_W - KW]], channel_multiplier=-1).then_inc(masked, 1)
                n += 1
                pool.wait_ge(masked, n)
                high = part[:, :, KW:GRID_W]
                pool.affine_select(out=high, in_=high, compare_op=ALU.is_gt, fill=NEG, base=KW // 2 - KW,
                                   pattern=[[0, PAIRS * NR], [-1, GRID_W - KW]], channel_multiplier=1).then_inc(masked, 1)
                n += 1

        @block.tensor
        def _(pe):
            pe.wait_ge(mirror_ready, 3)
            pe.wait_ge(tab_in, 16 * NA_HEADS)
            for a in range(PAIRS):
                for half in range(2):
                    mm = pe.matmul(tab_ps[:, a, half, 0:NR * GRID_W // 2], mirror[:, :],
                                   mirrored[:, a, half * NR * GRID_W // 2:(half + 1) * NR * GRID_W // 2], start=True, stop=True)
                mm.then_inc(turned_round, 1)

        @block.scalar
        def _(act):
            act.wait_ge(made, 1)
            act.activation(absd[:, :], dist[:, :], ACT.Abs).then_inc(absed, 1)
            for a in range(PAIRS):
                act.wait_ge(turned_round, a + 1)
                act.activation(tab[:, a, :, :].rearrange("p r c -> p (r c)").rearrange("p (x n) -> p x n", x=2),
                               tab_ps[:, a, :, 0:NR * GRID_W // 2], ACT.Copy).then_inc(tab_ready, 1)

        @block.vector
        def _(dve):
            dve.wait_ge(absed, 1)
            for h in range(DIFF_HEADS):
                if h >= 2:
                    dve.wait_ge(kept[h % 2], 16)
                slope = 2.0 ** (-8.0 * (h + 1) / DIFF_HEADS)
                dve.tensor_scalar(scaled[h % 2][:, :], absd[:, :], -slope, None, ALU.mult).then_inc(scaled_ready, 1)

        @block.sync
        def _(sp):
            sp.wait_ge(pad_zero, 1)
            sp.dma_start(pad[:, GRID_W - KW:GRID_W - KW + NC], na_rpb.rearrange("l h r c -> (l h r) c")).then_inc(pad_in, 16)
            sp.wait_ge(pad_in, 16)
            sp.dma_start(rpb_rows, pad[:, :]).then_inc(pad_out, 16)
            sp.wait_ge(pad_out, 16)
            for h in range(NA_HEADS):
                src = bass.AP(rpb_rows.tensor, h * NR * NPAD, [[1, GRID_W], [NPAD, NR], [1, GRID_W]])
                hh = h % 2
                sp.dma_start(mirrored[hh * GRID_W:(hh + 1) * GRID_W, h // 2, :].rearrange("p (r c) -> p r c", c=GRID_W), src
                             ).then_inc(tab_in, 16)
            for h in range(DIFF_HEADS):
                sp.wait_ge(scaled_ready, h + 1)
                sp.dma_start(alibi[h], scaled[h % 2][:, :]).then_inc(kept[h % 2], 16)
            sp.wait_ge(masked, 4)
            sp.dma_start(na_bias.rearrange("a p n -> p a n"), tab[:, :, :, :].rearrange("p a r c -> p a (r c)")
                         ).then_inc(tab_out, 16)
            sp.wait_ge(tab_out, 16)
            for b in range(2):
                sp.wait_ge(kept[b], 32)


def differential(nc, feat_t, v_tok, alibi, lams, o_cat):
    QB = SEQ // P
    STEPS = DIFF_HEADS * QB
    CH = SEQ // BANK
    with Parts(nc, "df") as m:
        ident = m.sb("ident", [P, P])
        q_raw = [m.sb(f"q_raw{b}", [P, 2, P]) for b in range(2)]
        k_st = m.sb("k_st", [P, SEQ])
        v_st = m.sb("v_st", [P, TILES, P])
        k_hi = [m.sb(f"k_hi{i}", [P, 2, SEQ], F32R) for i in range(2)]
        k_lo = [m.sb(f"k_lo{i}", [P, 2, SEQ], F32R) for i in range(2)]
        v_parts = [m.sb(f"v_parts{i}", [P, TILES, 2, P], F32R) for i in range(2)]
        q_high = [m.sb(f"q_high{b}", [P, 2, P]) for b in range(2)]
        q_parts = [m.sb(f"q_parts{b}", [P, 2, P], F32R) for b in range(2)]
        bias = [m.sb(f"bias{b}", [P, SEQ]) for b in range(2)]
        probs = [m.sb(f"probs{b}", [P, 2, SEQ]) for b in range(2)]
        amap = [m.sb(f"amap{b}", [P, SEQ]) for b in range(2)]
        t_hi = [m.sb(f"t_hi{g}", [P, BANK], F32R) for g in range(CH)]
        t_lo = [m.sb(f"t_lo{g}", [P, BANK], F32R) for g in range(CH)]
        nmax = [m.sb(f"nmax{b}", [P, 2, CH]) for b in range(2)]
        sums = [m.sb(f"sums{b}", [P, 2]) for b in range(2)]
        recip = [m.sb(f"recip{b}", [P, 2]) for b in range(2)]
        ratio = [m.sb(f"ratio{b}", [P, 1]) for b in range(2)]
        o_part = m.sb("o_part", [P, P])
        o_sb = [m.sb(f"o_sb{b}", [P, P]) for b in range(2)]
        lam_sb = m.sb("lam_sb", [P, 4, DH])
        lam_exp = m.sb("lam_exp", [P, 2])
        lam_dot = m.sb("lam_dot", [P, 2])
        nlam = m.sb("nlam", [P, 1])
        s_ps = m.psum("s_ps", [P, 4, BANK])
        t_ps = m.psum("t_ps", [P, 2, BANK])
        o_ps = m.psum("o_ps", [P, 2, BANK])

        consts = m.sem("consts")
        lam_loaded = m.sem("lam_loaded")
        lam_steps = m.sem("lam_steps")
        q_loaded = [m.sem(f"q_loaded{b}") for b in range(2)]
        k_loaded = m.sem("k_loaded")
        v_loaded = m.sem("v_loaded")
        k_hi_ready = m.sem("k_hi_ready")
        k_lo_ready = m.sem("k_lo_ready")
        v_hi_ready = m.sem("v_hi_ready")
        v_lo_ready = m.sem("v_lo_ready")
        q_hi_ready = m.sem("q_hi_ready")
        q_ready = m.sem("q_ready")
        q_zeros = m.sem("q_zeros")
        bias_loaded = [m.sem(f"bias_loaded{b}") for b in range(2)]
        s_ready = m.sem("s_ready")
        biased = m.sem("biased")
        exped = m.sem("exped")
        recips = m.sem("recips")
        ratios = m.sem("ratios")
        p1_scaled = m.sem("p1_scaled")
        a_ready = m.sem("a_ready")
        t_ready = m.sem("t_ready")
        thi_ready = m.sem("thi_ready")
        tlo_ready = m.sem("tlo_ready")
        pv_groups = m.sem("pv_groups")
        o_part_ready = m.sem("o_part_ready")
        o_ready = m.sem("o_ready")
        o_stored = [m.sem(f"o_stored{b}") for b in range(2)]
        ticks = m.sem("ticks")
        block = m.block()

        q_dram = feat_t[1, 0:BANK, :].rearrange("(h c d) t -> h d c t", c=2, d=DH)
        k_dram = feat_t[1, BANK:2 * BANK, :].rearrange("(h c d) t -> h c d t", c=2, d=DH)
        v_dram = v_tok[1].rearrange("(j p) (h e) -> h p j e", p=P, e=P)

        def run(eng, fn):
            for h in range(DIFF_HEADS):
                for i in range(4):
                    fn(h * QB + i, i % 2, h, i)
                last = h == DIFF_HEADS - 1
                with eng.Fori(2, QB // 2 - last) as j:
                    for b in range(2):
                        fn(j * 2 + (h * QB + b), b, h, j * 2 + b)
                if last:
                    for i in range(QB - 2, QB):
                        fn(h * QB + i, i % 2, h, i)
            for i in range(4):
                fn(STEPS + i, i % 2, DIFF_HEADS, i)

        def inner(i):
            return not isinstance(i, int)

        def at(i, k):
            return isinstance(i, int) and i == k

        def has(n, i, lag):
            return inner(i) or 0 <= n - lag < STEPS

        def turn_of(n, b):
            return n * 8 + (16 - 8 * b)

        def head_of(n, h, i, lag):
            return h if inner(i) or i >= lag else h - 1

        @block.sync
        def _(sp):
            for i, lam in enumerate(lams):
                sp.dma_start(lam_sb[:, i, :], lam.partition_broadcast(P).rearrange("p l n -> p (l n)")
                             ).then_inc(lam_loaded, 16)

            def load_k(h, c):
                for half in range(2):
                    sp.dma_start(k_st[half * DH:(half + 1) * DH, :], k_dram[h, c]).then_inc(k_loaded, 16)

            def load_v(h):
                sp.dma_start(v_st[:, :, :], v_dram[h]).then_inc(v_loaded, 16)

            load_k(0, 0)
            load_v(0)
            sp.wait_ge(k_lo_ready, 1)
            load_k(0, 1)

            def step(n, b, h, i):
                if h < DIFF_HEADS:
                    if inner(i) or n >= 2:
                        sp.wait_ge(q_ready, n - 1)
                        sp.sem_inc(ticks, 1)
                    for half in range(2):
                        sp.dma_start(q_raw[b][half * DH:(half + 1) * DH, :, :], q_dram[h, :, :, bass.ds(i * P, P)]
                                     ).then_inc(q_loaded[b], 16)
                    if inner(i) or n >= 2:
                        sp.wait_ge(biased, n * 8 - 8)
                        sp.sem_inc(ticks, 1)
                    start = (SEQ - P) - i * P
                    sp.dma_start(bias[b][:, :], alibi[h, :, bass.ds(start, SEQ)]).then_inc(bias_loaded[b], 16)
                    if at(i, 0) and h < DIFF_HEADS - 1:
                        sp.wait_ge(k_lo_ready, 2 * h + 2)
                        load_k(h + 1, 0)
                    if at(i, 2) and h < DIFF_HEADS - 1:
                        sp.wait_ge(v_lo_ready, h + 1)
                        load_v(h + 1)
                    if at(i, 3) and h < DIFF_HEADS - 1:
                        sp.wait_ge(k_lo_ready, 2 * h + 3)
                        load_k(h + 1, 1)
                if inner(i) or n >= 4:
                    sp.wait_ge(o_ready, n - 3)
                    sp.sem_inc(ticks, 1)
                    if inner(i):
                        rows, hh = bass.ds((i - 4) * P, P), h
                    else:
                        hh, ii = (n - 4) // QB, (n - 4) % QB
                        rows = bass.ds(ii * P, P)
                    sp.dma_start(o_cat[rows, NA_HEADS * DH + hh * P:NA_HEADS * DH + (hh + 1) * P], o_sb[b][:, :]
                                 ).then_inc(o_stored[b], 16)

            run(sp, step)
            for b in range(2):
                sp.wait_ge(o_stored[b], 16 * STEPS // 2 + 16 * b)

        @block.gpsimd
        def _(pool):
            identity_steps(pool, ident, consts)

            pool.memset(q_high[0][0:DH, :, :], 0.0).then_inc(q_zeros, 1)
            pool.memset(q_high[1][0:DH, :, :], 0.0).then_inc(q_zeros, 1)
            pool.wait_ge(q_zeros, 2)

            def queries(m, b):
                pool.wait_ge(q_hi_ready, m + 1)
                if not isinstance(m, int) or m >= 2:
                    pool.wait_ge(s_ready, m * 8 - 8)
                pool.tensor_tensor(q_parts[b][:, :, :], q_raw[b][:, :, :], q_high[b][:, :, :],
                                   ALU.subtract).then_inc(q_ready, 1)

            def step(n, b, h, i):
                if has(n, i, -1):
                    queries(n + 1, 1 - b)
                if has(n, i, 1):
                    pool.wait_ge(ratios, n)
                    pool.sem_inc(ticks, 1)
                    for g in range(CH):
                        cols = slice(g * BANK, (g + 1) * BANK)
                        pool.tensor_scalar(probs[1 - b][:, 1, cols], probs[1 - b][:, 1, cols], ratio[1 - b][:, 0:1], 1.0,
                                           ALU.mult, ALU.mult).then_inc(p1_scaled, 1)
                    for g in range(CH):
                        cols = slice(g * BANK, (g + 1) * BANK)
                        if inner(i) or n >= 3:
                            pool.wait_ge(t_ready, n * CH + (g + 1 - 3 * CH))
                        pool.wait_ge(p1_scaled, n * CH + (g + 1 - CH))
                        pool.tensor_tensor(amap[1 - b][:, cols], probs[1 - b][:, 0, cols], probs[1 - b][:, 1, cols],
                                           ALU.add).then_inc(a_ready, 1)

            queries(0, 0)
            run(pool, step)

        @block.scalar
        def _(act):
            def split_k(h, c):
                n = 2 * h + c
                act.wait_ge(k_loaded, 32 * (n + 1))
                act.activation(k_hi[h % 2][:, c, :], k_st[:, :], ACT.Copy, scale=EXP_SCALE).then_inc(k_hi_ready, 1)

            act.wait_ge(lam_steps, 2)
            act.activation(lam_exp[:, :], lam_dot[:, :], ACT.Exp).then_inc(lam_steps, 1)
            split_k(0, 0)
            split_k(0, 1)

            def queries_high(m, b):
                act.wait_ge(q_loaded[b], 2 * turn_of(m, b))
                if not isinstance(m, int) or m >= 2:
                    act.wait_ge(q_ready, m - 1)
                act.activation(q_high[b][DH:P, :, :].bitcast(F32R), q_raw[b][DH:P, :, :], ACT.Copy).then_inc(q_hi_ready, 1)

            def exponentials(n, b, c):
                act.wait_ge(biased, n * 8 + (c - 1))
                if c == 0 and not (isinstance(n, int) and n < 3):
                    act.wait_ge(ratios, n - 2)
                act.activation(probs[1 - b][:, c, :], probs[1 - b][:, c, :], ACT.Exp, bias=nmax[1 - b][:, c, CH - 1:CH],
                               scale=-1.0, accum_out=sums[1 - b][:, c:c + 1]).then_inc(exped, 1)

            def turned_high(n, g):
                act.wait_ge(t_ready, n * CH + (g + 1 - 2 * CH))
                if not (isinstance(n, int) and n < 3):
                    act.wait_ge(pv_groups, n * CH + (g + 1 - 3 * CH))
                act.activation(t_hi[g][:, :], t_ps[:, g % 2, :], ACT.Copy).then_inc(thi_ready, 1)

            queries_high(0, 0)

            def step(n, b, h, i):
                if h < DIFF_HEADS and at(i, 0):
                    act.wait_ge(v_loaded, 16 * (h + 1))
                    if h >= 2:
                        act.wait_ge(pv_groups, (h - 1) * QB * CH)
                    act.activation(v_parts[h % 2][:, :, 0, :], v_st[:, :, :], ACT.Copy).then_inc(v_hi_ready, 1)
                if has(n, i, 1):
                    exponentials(n, b, 0)
                if has(n, i, -1):
                    queries_high(n + 1, 1 - b)
                if has(n, i, 2):
                    turned_high(n, 0)
                if has(n, i, 1):
                    exponentials(n, b, 1)
                if has(n, i, 2):
                    turned_high(n, 1)
                if has(n, i, 3):
                    act.wait_ge(pv_groups, n * CH - 2 * CH)
                    if inner(i) or n >= 4:
                        act.wait_ge(o_ready, n - 3)
                    act.activation(o_part[:, :], o_ps[:, 1 - b, P:2 * P], ACT.Copy, scale=recip[1 - b][:, 0:1]
                                   ).then_inc(o_part_ready, 1)
                if has(n, i, 2):
                    turned_high(n, 2)
                    turned_high(n, 3)
                if h < DIFF_HEADS - 1 and (at(i, 1) or at(i, 3)):
                    if h >= 1 and at(i, 1):
                        act.wait_ge(s_ready, h * QB * 8)
                    split_k(h + 1, i // 2)

            run(act, step)

        @block.vector
        def _(dve):
            def split_k(h, c):
                n = 2 * h + c
                dve.wait_ge(k_hi_ready, n + 1)
                dve.scalar_tensor_tensor(out=k_lo[h % 2][:, c, :], in0=k_st[:, :], scalar=EXP_SCALE,
                                         in1=k_hi[h % 2][:, c, :].bitcast(F32), op0=ALU.mult, op1=ALU.subtract
                                         ).then_inc(k_lo_ready, 1)

            credit(dve, o_stored[1], 16)
            dve.wait_ge(lam_loaded, 16 * 4)
            dve.tensor_tensor(lam_sb[:, 0::2, :], lam_sb[:, 0::2, :], lam_sb[:, 1::2, :], ALU.mult).then_inc(lam_steps, 1)
            dve.wait_ge(lam_steps, 1)
            dve.tensor_reduce(lam_dot[:, :], lam_sb[:, 0::2, :], AX.X, ALU.add).then_inc(lam_steps, 1)
            dve.wait_ge(lam_steps, 3)
            dve.scalar_tensor_tensor(out=nlam[:, :], in0=lam_exp[:, 1:2], scalar=-LAM_INIT, in1=lam_exp[:, 0:1],
                                     op0=ALU.add, op1=ALU.subtract).then_inc(lam_steps, 1)
            split_k(0, 0)
            split_k(0, 1)

            def bias_scores(n, b, g):
                for c in range(2):
                    u = n * 8 + (2 * g + c)
                    if g == 0 and c == 0:
                        dve.wait_ge(bias_loaded[b], turn_of(n, b))
                    dve.wait_ge(s_ready, u + 1)
                    if g >= 1:
                        dve.wait_ge(biased, u - 1)
                    dve.sem_inc(ticks, 1)
                    dve.tensor_tensor_reduce(
                        probs[b][:, c, g * BANK:(g + 1) * BANK], s_ps[:, 2 * (g % 2) + c, :],
                        bias[b][:, g * BANK:(g + 1) * BANK], -1.0,
                        3e38 if g == 0 else nmax[b][:, c, g - 1:g], ALU.add, ALU.min, nmax[b][:, c, g:g + 1]
                    ).then_inc(biased, 1)

            def step(n, b, h, i):
                if h < DIFF_HEADS and at(i, 0):
                    dve.wait_ge(v_hi_ready, h + 1)
                    dve.tensor_tensor(v_parts[h % 2][:, :, 1, :], v_st[:, :, :],
                                      v_parts[h % 2][:, :, 0, :].bitcast(F32), ALU.subtract).then_inc(v_lo_ready, 1)
                for g in range(CH):
                    if has(n, i, 0):
                        if inner(i) or n >= 2:
                            dve.wait_ge(a_ready, n * CH + (g + 1 - 2 * CH))
                            if g == 0:
                                dve.wait_ge(exped, n * 2 - 2)
                        bias_scores(n, b, g)
                    if has(n, i, 3) and g == 2:
                        dve.wait_ge(o_part_ready, n - 2)
                        if inner(i) or n >= 5:
                            dve.wait_ge(o_stored[1 - b], o_turn(n, b))
                        dve.scalar_tensor_tensor(out=o_sb[1 - b][:, :], in0=o_ps[:, 1 - b, 0:P], scalar=recip[1 - b][:, 0:1],
                                                 in1=o_part[:, :], op0=ALU.mult, op1=ALU.add).then_inc(o_ready, 1)
                    if has(n, i, 1) and g == 2:
                        dve.wait_ge(exped, n * 2)
                        if inner(i) or n >= 3:
                            dve.wait_ge(o_ready, n - 2)
                            dve.wait_ge(a_ready, n * CH - 2 * CH)
                        dve.reciprocal(recip[1 - b][:, :], sums[1 - b][:, :]).then_inc(recips, 1)
                        dve.wait_ge(recips, n)
                        dve.tensor_scalar(ratio[1 - b][:, :], recip[1 - b][:, 1:2], sums[1 - b][:, 0:1], nlam[:, 0:1],
                                          ALU.mult, ALU.mult).then_inc(ratios, 1)
                    if has(n, i, 2):
                        dve.wait_ge(thi_ready, n * CH + (g + 1 - 2 * CH))
                        dve.tensor_tensor(t_lo[g][:, :], t_ps[:, g % 2, :], t_hi[g][:, :].bitcast(F32),
                                          ALU.subtract).then_inc(tlo_ready, 1)
                if h + 1 < DIFF_HEADS and (at(i, 1) or at(i, 3)):
                    split_k(h + 1, i // 2)

            def o_turn(n, b):
                if isinstance(n, int):
                    return 16 * ((n - 5) // 2 + 1 + (1 - b))
                return n * 8 + (-24 if b else -16)

            dve.wait_ge(lam_steps, 4)
            run(dve, step)

        @block.tensor
        def _(pe):
            pe.wait_ge(consts, 2)

            def scores(n, b, h, g):
                for c in range(2):
                    u = n * 8 + (2 * g + c)
                    if g == 0 and c == 0:
                        pe.wait_ge(q_ready, n + 1)
                        pe.wait_ge(k_lo_ready, 2 * h + 2)
                    if not isinstance(n, int) or u >= 4:
                        pe.wait_ge(biased, u - 3)
                    rows = slice(g * BANK, (g + 1) * BANK)
                    pe.matmul(s_ps[:, 2 * (g % 2) + c, :], q_parts[b][:, c, :], k_hi[h % 2][:, c, rows],
                              start=True, stop=False)
                    pe.matmul(s_ps[:, 2 * (g % 2) + c, :], q_parts[b][:, c, :], k_lo[h % 2][:, c, rows],
                              start=False, stop=True).then_inc(s_ready, 1)

            def turn(n, b, g):
                pe.wait_ge(a_ready, n * CH + (g + 1 - 2 * CH))
                if not isinstance(n, int) or n >= 3 or g >= 2:
                    pe.wait_ge(tlo_ready, n * CH + (g - 1 - 2 * CH))
                for j in range(4):
                    t = pe.transpose(t_ps[:, g % 2, j * P:(j + 1) * P], amap[b][:, (4 * g + j) * P:(4 * g + j + 1) * P],
                                     ident[:, :])
                t.then_inc(t_ready, 1)

            def values(n, b, m_lag, hv, g):
                c = (b + m_lag) % 2
                pe.wait_ge(tlo_ready, n * CH + (g + 1 - m_lag * CH))
                if g == 0:
                    pe.wait_ge(v_lo_ready, hv + 1)
                    if not isinstance(n, int) or n >= 4:
                        pe.wait_ge(o_ready, n - 3)
                for j in range(4):
                    k = 4 * g + j
                    blk = slice(j * P, (j + 1) * P)
                    pe.matmul(o_ps[:, c, 0:2 * P], t_hi[g][:, blk], v_parts[hv % 2][:, k, :, :],
                              start=(k == 0), stop=False, skip_group_check=True)
                    mm = pe.matmul(o_ps[:, c, 0:P], t_lo[g][:, blk], v_parts[hv % 2][:, k, 0, :],
                                   start=False, stop=(k == TILES - 1), skip_group_check=True)
                mm.then_inc(pv_groups, 1)

            def step(n, b, h, i):
                for g in range(CH):
                    if has(n, i, 0):
                        scores(n, b, h, g)
                    if has(n, i, 2):
                        turn(n, b, g)
                    if g == 0 and has(n, i, 3):
                        values(n, b, 3, head_of(n, h, i, 3), CH - 1)
                    if g >= 1 and has(n, i, 2):
                        values(n, b, 2, head_of(n, h, i, 2), g - 1)

            run(pe, step)


def mix_out(nc, x, o_cat, g_na_out, g_diff_out, w_out, g_moe, w_router, h_res, hn_moe, logits):
    NG = D // DH
    NA_W = NA_HEADS * DH
    with Parts(nc, "mo") as m:
        ident = m.sb("ident", [P, P])
        w_st = [m.sb(f"w_st{b}", [P, D]) for b in range(2)]
        w_hi = m.sb("w_hi", [P, KB, D], F32R)
        w_lo = m.sb("w_lo", [P, KB, D], F32R)
        w_r = m.sb("w_r", [P, KB, E])
        g_heads = m.sb("g_heads", [P, D])
        g_next = m.sb("g_next", [P, D])
        mhalf = m.sb("mhalf", [P, NG])
        o_in = [m.sb(f"o_in{b}", [P, D]) for b in range(2)]
        x_in = [m.sb(f"x_in{b}", [P, D]) for b in range(2)]
        o_sq = m.sb("o_sq", [P, D])
        o_ss = m.sb("o_ss", [P, NG])
        o_pair = m.sb("o_pair", [P, NG // 4])
        o_ms = m.sb("o_ms", [P, NG])
        o_rs = m.sb("o_rs", [P, NG])
        ot_hi = [m.sb(f"ot_hi{b}", [P, KB, P], F32R) for b in range(2)]
        ot_lo = [m.sb(f"ot_lo{b}", [P, KB, P], F32R) for b in range(2)]
        h_sb = [m.sb(f"h_sb{b}", [P, D]) for b in range(2)]
        h_sq = m.sb("h_sq", [P, D])
        h_ss = m.sb("h_ss", [P, 1])
        h_ms = m.sb("h_ms", [P, 1])
        h_rs = m.sb("h_rs", [P, 1])
        hn_sb = [m.sb(f"hn_sb{b}", [P, D]) for b in range(2)]
        hnt = [m.sb(f"hnt{b}", [P, KB, P]) for b in range(2)]
        t_ps = m.psum("t_ps", [P, 2, BANK])
        out_ps = m.psum("out_ps", [P, 2, D])
        l_ps = m.psum("l_ps", [P, 2, BANK])

        sem = m.sem
        consts, mhalf_ready = sem("consts"), sem("mhalf_ready")
        gains_loaded, gains_ready = sem("gains_loaded"), sem("gains_ready")
        w_loaded = [sem(f"w_loaded{b}") for b in range(2)]
        whi_ready, wlo_ready, wr_loaded = sem("whi_ready"), sem("wlo_ready"), sem("wr_loaded")
        o_loaded = [sem(f"o_loaded{b}") for b in range(2)]
        x_loaded = [sem(f"x_loaded{b}") for b in range(2)]
        o_squared, o_summed, o_steps, o_means, o_rsqrt = (sem(n) for n in ("o_squared", "o_summed", "o_steps", "o_means", "o_rsqrt"))
        o_scaled, o_normed, turned = sem("o_scaled"), sem("o_normed"), sem("turned")
        othi_ready, otlo_ready, out_ready = sem("othi_ready"), sem("otlo_ready"), sem("out_ready")
        h_ready, h_squared, h_means, h_rsqrt, hn_ready = (sem(n) for n in ("h_ready", "h_squared", "h_means", "h_rsqrt", "hn_ready"))
        hnt_ready, l_ready, l_copied = sem("hnt_ready"), sem("l_ready"), sem("l_copied")
        h_stored = [sem(f"h_stored{b}") for b in range(2)]
        hn_stored = [sem(f"hn_stored{b}") for b in range(2)]
        block = m.block()

        def run(eng, fn):
            for n in range(4):
                fn(n, n % 2, n)
            with eng.Fori(2, TILES // 2 - 1) as j:
                for b in range(2):
                    fn(j * 2 + b, b, None)
            for n in range(TILES - 2, TILES + 4):
                fn(n, n % 2, n)

        def has(i, lag):
            return i is None or 0 <= i - lag < TILES

        def turns(n, b, lag=0):
            return n * 8 + (16 - 8 * ((b - lag) % 2) - 8 * lag)

        @block.sync
        def _(sp):
            sp.dma_start(g_heads[:, 0:NA_W], g_na_out.rearrange("l h d -> l (h d)").partition_broadcast(P).rearrange(
                "p l n -> p (l n)")).then_inc(gains_loaded, 16)
            for h in range(DIFF_HEADS):
                sp.dma_start(g_heads[:, NA_W + h * P:NA_W + (h + 1) * P], g_diff_out.partition_broadcast(P).rearrange(
                    "p l n -> p (l n)")).then_inc(gains_loaded, 16)
            sp.dma_start(g_next[:, :], g_moe.partition_broadcast(P).rearrange("p l n -> p (l n)")).then_inc(gains_loaded, 16)
            for b in range(2):
                sp.dma_start(o_in[b][:, :], o_cat[b * P:(b + 1) * P, :]).then_inc(o_loaded[b], 16)
            for k in range(KB):
                if k >= 2:
                    sp.wait_ge(wlo_ready, k - 1)
                sp.dma_start(w_st[k % 2][:, :], w_out[0, k * P:(k + 1) * P, :]).then_inc(w_loaded[k % 2], 16)
            sp.dma_start(w_r[:, :, :], w_router.rearrange("l (k p) e -> (l p) k e", p=P)).then_inc(wr_loaded, 16)

            def step(n, b, i):
                if has(i, 0):
                    if i is None or i >= 2:
                        sp.wait_ge(turned, 4 * n - 10 if i is None else 2 * n - 2)
                        sp.dma_start(o_in[b][:, :], o_cat[bass.ds(n * P, P), :]).then_inc(o_loaded[b], 16)
                        sp.wait_ge(h_ready, n - 1)
                    sp.dma_start(x_in[b][:, :], x[0, bass.ds(n * P, P), :]).then_inc(x_loaded[b], 16)
                if has(i, 3):
                    c = 1 - b
                    sp.wait_ge(hn_ready, n - 2)
                    sp.dma_start(h_res[bass.ds((n - 3) * P, P), :], h_sb[c][:, :]).then_inc(h_stored[c], 16)
                    sp.dma_start(hn_moe[bass.ds((n - 3) * P, P), :], hn_sb[c][:, :]).then_inc(hn_stored[c], 16)

            run(sp, step)
            for b in range(2):
                sp.wait_ge(h_stored[b], 8 * TILES)
                sp.wait_ge(hn_stored[b], 8 * TILES)

        def turned_o(n, g):
            return 4 * n + (g + 1 - 6) if not isinstance(n, int) or n >= 3 else 2 * n + g + 1

        def turned_hn(n, g):
            return 4 * n + (g + 3 - 6) if not isinstance(n, int) or n < TILES else 2 * n + (2 * TILES - 6) + g + 1

        @block.gpsimd
        def _(pool):
            identity_steps(pool, ident, consts)
            pool.memset(mhalf[:, :], -0.5).then_inc(mhalf_ready, 1)
            pool.wait_ge(mhalf_ready, 1)

            def norm_o(n):
                pool.wait_ge(o_means, n + 1)
                pool.tensor_tensor(o_rs[:, :], o_ms[:, :], mhalf[:, :], ALU.pow).then_inc(o_rsqrt, 1)

            def step(n, b, i):
                if i is None or i < TILES - 1:
                    norm_o(n + 1)
                if has(i, 2):
                    pool.wait_ge(h_means, n - 1)
                    pool.tensor_tensor(h_rs[:, :], h_ms[:, :], mhalf[:, 0:1], ALU.pow).then_inc(h_rsqrt, 1)

            norm_o(0)
            run(pool, step)

        @block.scalar
        def _(act):
            def square_o(n, b):
                act.wait_ge(o_loaded[b], turns(n, b))
                if not isinstance(n, int) or n >= 1:
                    act.wait_ge(o_summed, n)
                act.activation(o_sq[:, :], o_in[b][:, :], ACT.Square).then_inc(o_squared, 1)

            square_o(0, 0)
            for k in range(KB):
                act.wait_ge(w_loaded[k % 2], 16 * (k // 2 + 1))
                act.activation(w_hi[:, k, :], w_st[k % 2][:, :], ACT.Copy).then_inc(whi_ready, 1)

            def step(n, b, i):
                if has(i, 0):
                    for g in range(2):
                        act.wait_ge(turned, turned_o(n, g))
                        if g == 0 and (i is None or i >= 2):
                            act.wait_ge(out_ready, n - 1)
                        act.activation(ot_hi[b][:, 4 * g:4 * g + 4, :], t_ps[:, g, :].rearrange("p (k t) -> p k t", t=P),
                                       ACT.Copy).then_inc(othi_ready, 1)
                if has(i, 3):
                    c = 1 - b
                    for g in range(2):
                        act.wait_ge(turned, turned_hn(n, g))
                        if g == 0 and (i is None or i >= 5):
                            act.wait_ge(l_ready, n - 3)
                        act.activation(hnt[c][:, 4 * g:4 * g + 4, :], t_ps[:, g, :].rearrange("p (k t) -> p k t", t=P),
                                       ACT.Copy).then_inc(hnt_ready, 1)
                if i is None or i < TILES - 1:
                    square_o(n + 1, 1 - b)
                if has(i, 2):
                    act.wait_ge(h_ready, n - 1)
                    if i is None or i >= 3:
                        act.wait_ge(h_means, n - 2)
                        act.wait_ge(h_squared, n - 2)
                    act.activation(h_sq[:, :], h_sb[b][:, :], ACT.Square, accum_out=h_ss[:, :]).then_inc(h_squared, 1)

            run(act, step)

        @block.vector
        def _(dve):
            credit(dve, l_copied, 1)
            dve.wait_ge(gains_loaded, 16 * (2 + DIFF_HEADS))
            dve.tensor_scalar(g_heads[:, NA_W:D], g_heads[:, NA_W:D], 1.0 - LAM_INIT, None, ALU.mult).then_inc(gains_ready, 1)

            def norm_o(n, b):
                dve.wait_ge(o_squared, n + 1)
                if not isinstance(n, int) or n >= 1:
                    dve.wait_ge(o_means, n)
                dve.tensor_reduce(o_ss[:, :], o_sq[:, :].rearrange("p (g d) -> p g d", d=DH), AX.X, ALU.add
                                  ).then_inc(o_summed, 1)
                dve.wait_ge(o_summed, n + 1)
                dve.tensor_tensor(o_pair[:, :], o_ss[:, NG // 2::2], o_ss[:, NG // 2 + 1::2], ALU.add).then_inc(o_steps, 1)
                if not isinstance(n, int) or n >= 1:
                    dve.wait_ge(o_rsqrt, n)
                dve.tensor_scalar(o_ms[:, 0:NG // 2], o_ss[:, 0:NG // 2], 1.0 / DH, EPS, ALU.mult, ALU.add).then_inc(o_steps, 1)
                dve.wait_ge(o_steps, 2 * n + 2)
                dve.tensor_scalar(o_ms[:, NG // 2:NG].rearrange("p (h a) -> p h a", a=2),
                                  o_pair[:, :].unsqueeze(2).to_broadcast([P, NG // 4, 2]), 0.5 / DH, EPS, ALU.mult, ALU.add
                                  ).then_inc(o_means, 1)
                dve.wait_ge(o_rsqrt, n + 1)
                dve.tensor_tensor(o_in[b][:, :].rearrange("p (g d) -> p g d", d=DH),
                                  o_in[b][:, :].rearrange("p (g d) -> p g d", d=DH),
                                  o_rs[:, :].unsqueeze(2).to_broadcast([P, NG, DH]), ALU.mult).then_inc(o_scaled, 1)
                dve.wait_ge(o_scaled, n + 1)
                dve.tensor_tensor(o_in[b][:, :], o_in[b][:, :], g_heads[:, :], ALU.mult).then_inc(o_normed, 1)

            dve.wait_ge(gains_ready, 1)
            norm_o(0, 0)
            for k in range(KB):
                dve.wait_ge(whi_ready, k + 1)
                dve.tensor_tensor(w_lo[:, k, :], w_st[k % 2][:, :], w_hi[:, k, :].bitcast(F32), ALU.subtract
                                  ).then_inc(wlo_ready, 1)

            def step(n, b, i):
                if has(i, 0):
                    for g in range(2):
                        dve.wait_ge(othi_ready, 2 * n + (g + 1))
                        dve.tensor_tensor(ot_lo[b][:, 4 * g:4 * g + 4, :], t_ps[:, g, :].rearrange("p (k t) -> p k t", t=P),
                                          ot_hi[b][:, 4 * g:4 * g + 4, :].bitcast(F32), ALU.subtract).then_inc(otlo_ready, 1)
                if has(i, 2):
                    dve.wait_ge(out_ready, n - 1)
                    dve.wait_ge(x_loaded[b], turns(n, b, 2))
                    if i is None or i >= 4:
                        dve.wait_ge(h_stored[b], turns(n, b, 4))
                        dve.wait_ge(hn_stored[b], turns(n, b, 4))
                    dve.tensor_tensor(h_sb[b][:, :], out_ps[:, b, :], x_in[b][:, :], ALU.add).then_inc(h_ready, 1)
                if i is None or i < TILES - 1:
                    norm_o(n + 1, 1 - b)
                if has(i, 2):
                    dve.wait_ge(h_squared, n - 1)
                    if i is None or i >= 3:
                        dve.wait_ge(h_rsqrt, n - 2)
                    dve.tensor_scalar(h_ms[:, :], h_ss[:, :], 1.0 / D, EPS, ALU.mult, ALU.add).then_inc(h_means, 1)
                    dve.wait_ge(h_rsqrt, n - 1)
                    if i is None or i >= 4:
                        dve.wait_ge(turned, turned_hn(n - 1, 1))
                    dve.scalar_tensor_tensor(out=hn_sb[b][:, :], in0=h_sb[b][:, :], scalar=h_rs[:, 0:1], in1=g_next[:, :],
                                             op0=ALU.mult, op1=ALU.mult).then_inc(hn_ready, 1)
                if has(i, 4):
                    dve.wait_ge(l_ready, n - 2)
                    dve.tensor_copy(logits[:, bass.ds(n - 4, 1), :].rearrange("p a e -> p (a e)"), l_ps[:, b, 0:E]
                                    ).then_inc(l_copied, 1)

            run(dve, step)
            dve.wait_ge(l_copied, TILES + 1)

        @block.tensor
        def _(pe):
            credit(pe, l_ready, 1)
            pe.wait_ge(consts, 2)

            def step(n, b, i):
                if has(i, 0):
                    pe.wait_ge(o_normed, n + 1)
                    for g in range(2):
                        if g == 0 and (i is None or i >= 4):
                            pe.wait_ge(hnt_ready, 2 * n - 6)
                        elif g == 0 and i >= 1:
                            pe.wait_ge(otlo_ready, 2 * n)
                        for k in range(4 * g, 4 * g + 4):
                            t = pe.transpose(t_ps[:, g, (k % 4) * P:(k % 4 + 1) * P], o_in[b][:, k * P:(k + 1) * P], ident[:, :])
                        t.then_inc(turned, 1)
                if has(i, 3):
                    c = 1 - b
                    pe.wait_ge(hn_ready, n - 2)
                    for g in range(2):
                        if has(i, 0):
                            pe.wait_ge(otlo_ready, 2 * n + (g + 1))
                        else:
                            pe.wait_ge(hnt_ready, 2 * n - 6 + 0)
                            pe.wait_ge(otlo_ready, 2 * TILES)
                        for k in range(4 * g, 4 * g + 4):
                            t = pe.transpose(t_ps[:, g, (k % 4) * P:(k % 4 + 1) * P], hn_sb[c][:, k * P:(k + 1) * P], ident[:, :])
                        t.then_inc(turned, 1)
                if has(i, 1):
                    c = 1 - b
                    pe.wait_ge(otlo_ready, 2 * n)
                    if i is not None and i == 1:
                        pe.wait_ge(wlo_ready, KB)
                    if i is None or i >= 3:
                        pe.wait_ge(h_ready, n - 2)
                    for half in range(2):
                        cols = slice(half * BANK, (half + 1) * BANK)
                        for k in range(KB):
                            pe.matmul(out_ps[:, c, cols], ot_hi[c][:, k, :], w_hi[:, k, cols], start=(k == 0), stop=False)
                            pe.matmul(out_ps[:, c, cols], ot_hi[c][:, k, :], w_lo[:, k, cols], start=False, stop=False)
                            mm = pe.matmul(out_ps[:, c, cols], ot_lo[c][:, k, :], w_hi[:, k, cols], start=False,
                                           stop=(k == KB - 1))
                    mm.then_inc(out_ready, 1)
                if has(i, 3):
                    c = 1 - b
                    pe.wait_ge(hnt_ready, 2 * n - 4)
                    if i is not None and i == 3:
                        pe.wait_ge(wr_loaded, 16)
                    if i is None or i >= 5:
                        pe.wait_ge(l_copied, n - 3)
                    for k in range(KB):
                        mm = pe.matmul(l_ps[:, c, 0:E], hnt[c][:, k, :], w_r[:, k, :], start=(k == 0), stop=(k == KB - 1))
                    mm.then_inc(l_ready, 1)

            run(pe, step)


def route(nc, logits, slot_token, slot_gate):
    TE = TILES * E
    BITS = 30
    HALVES = CAP // P
    NPAY = 6
    RING = 4
    with Parts(nc, "ro") as m:
        aff = m.sb("aff", [P, TILES, E])
        per_tile = m.sb("per_tile", [P, TILES])
        thresh = m.sb("thresh", [P, E])
        cand = m.sb("cand", [P, E])
        kept = m.sb("kept", [P, E])
        bit = m.sb("bit", [P, E], I32)
        flags = m.sb("flags", [P, TILES, E])
        count = m.sb("count", [P, E])
        ones = m.sb("ones", [P, P])
        before = m.sb("before", [P, P])
        above = m.sb("above", [P, TILES, E])
        equal = m.sb("equal", [P, TILES, E])
        rank = m.sb("rank", [P, TILES, E])
        tiles_before = m.sb("tiles_before", [P, TILES, E])
        need = m.sb("need", [P, E])
        slot = m.sb("slot", [P, TILES, E])
        rest = m.sb("rest", [P, TILES, E])
        iota_s = m.sb("iota_s", [P, CAP], BF16)
        payload = m.sb("payload", [P, TILES, E, NPAY], BF16)
        hot = [m.sb(f"hot{r}", [P, CAP], BF16) for r in range(RING)]
        got = m.sb("got", [P, HALVES, E, NPAY])
        gate_part = m.sb("gate_part", [P, HALVES, E])
        token_f = m.sb("token_f", [P, HALVES, E])
        c_ps = m.psum("c_ps", [P, BANK])
        r_ps = m.psum("r_ps", [P, BANK])
        tot_ps = m.psum("tot_ps", [P, BANK])
        s_ps = m.psum("s_ps", [P, HALVES, BANK])

        consts = m.sem("consts")
        steps = m.sem("steps")
        exped = m.sem("exped")
        counted = m.sem("counted")
        counts_ready = m.sem("counts_ready")
        flags_ready = m.sem("flags_ready")
        sums_ready = m.sem("sums_ready")
        pay_ready = m.sem("pay_ready")
        hot_ready = m.sem("hot_ready")
        hot_used = m.sem("hot_used")
        block = m.block()

        @block.gpsimd
        def _(pool):
            pool.memset(ones[:, :], 1.0).then_inc(consts, 1)
            pool.memset(before[:, :], 1.0).then_inc(consts, 1)
            pool.wait_ge(consts, 2)
            pool.affine_select(out=before[:, :], in_=before[:, :], compare_op=ALU.is_gt, fill=0.0, base=0,
                               pattern=[[1, P]], channel_multiplier=-1).then_inc(consts, 1)
            pool.iota(iota_s[:, :], pattern=[[1, CAP]], base=0, channel_multiplier=0,
                      allow_small_or_imprecise_dtypes=True).then_inc(consts, 1)
            pool.memset(payload[:, :, :, :], 0.0).then_inc(consts, 1)
            pool.wait_ge(consts, 5)
            pool.iota(payload[:, :, :, 0], pattern=[[0, TILES], [0, E]], base=0, channel_multiplier=1,
                      allow_small_or_imprecise_dtypes=True).then_inc(consts, 1)
            pool.iota(payload[:, :, :, 1], pattern=[[1, TILES], [0, E]], base=0, channel_multiplier=0,
                      allow_small_or_imprecise_dtypes=True).then_inc(consts, 1)

        @block.scalar
        def _(act):
            act.wait_ge(steps, 2)
            act.activation(aff[:, :, :], aff[:, :, :], ACT.Exp).then_inc(exped, 1)

        @block.vector
        def _(dve):
            done = [0]

            def own(ins):
                done[0] += 1
                ins.then_inc(steps, 1)
                dve.wait_ge(steps, done[0])

            def over_tiles(a):
                return a.unsqueeze(1).to_broadcast([P, TILES, E])

            def over_experts(a):
                return a.unsqueeze(2).to_broadcast([P, TILES, E])

            own(dve.tensor_reduce(per_tile[:, :], logits[:, :, :], AX.X, ALU.max))
            own(dve.tensor_tensor(aff[:, :, :], logits[:, :, :], over_experts(per_tile[:, :]), ALU.subtract))
            dve.wait_ge(exped, 1)
            own(dve.tensor_reduce(per_tile[:, :], aff[:, :, :], AX.X, ALU.add))
            own(dve.reciprocal(per_tile[:, :], per_tile[:, :]))
            own(dve.tensor_tensor(aff[:, :, :], aff[:, :, :], over_experts(per_tile[:, :]), ALU.mult))
            own(dve.memset(thresh[:, :], 0.0))
            own(dve.memset(bit[:, :], 1 << (BITS - 1)))
            dve.wait_ge(consts, 7)
            base = done[0]
            with dve.Fori(0, BITS) as i:
                def mine(ins, k):
                    ins.then_inc(steps, 1)
                    dve.wait_ge(steps, i * 5 + (base + k))
                mine(dve.tensor_tensor(cand[:, :].bitcast(I32), thresh[:, :].bitcast(I32), bit[:, :], ALU.bitwise_or), 1)
                mine(dve.tensor_tensor(flags[:, :, :], aff[:, :, :], over_tiles(cand[:, :]), ALU.is_ge), 2)
                dve.tensor_reduce(count[:, :], flags[:, :, :].rearrange("p t e -> p e t"), AX.X, ALU.add).then_inc(counted, 1)
                mine(dve.tensor_scalar(bit[:, :], bit[:, :], 1, None, ALU.logical_shift_right), 3)
                dve.wait_ge(counts_ready, i + 1)
                mine(dve.scalar_tensor_tensor(out=kept[:, :], in0=c_ps[:, 0:E], scalar=CAP - 0.5, in1=cand[:, :],
                                              op0=ALU.is_ge, op1=ALU.mult), 4)
                mine(dve.tensor_tensor(thresh[:, :], thresh[:, :], kept[:, :], ALU.max), 5)
            done[0] = base + 5 * BITS

            def ranks(of, k):
                dve.nop().then_inc(flags_ready, 1)
                dve.wait_ge(sums_ready, k + 1)
                own(dve.memset(tiles_before[:, 0, :], 0.0))
                for t in range(1, TILES):
                    own(dve.tensor_tensor(tiles_before[:, t, :], tiles_before[:, t - 1, :],
                                          tot_ps[:, (t - 1) * E:t * E], ALU.add))
                own(dve.tensor_tensor(rank[:, :, :], r_ps[:, 0:TE].rearrange("p (t e) -> p t e", e=E),
                                      tiles_before[:, :, :], ALU.add))

            own(dve.tensor_tensor(above[:, :, :], aff[:, :, :], over_tiles(thresh[:, :]), ALU.is_gt))
            own(dve.tensor_tensor(equal[:, :, :], aff[:, :, :], over_tiles(thresh[:, :]), ALU.is_equal))
            dve.wait_ge(counts_ready, BITS)
            dve.tensor_reduce(count[:, :], above[:, :, :].rearrange("p t e -> p e t"), AX.X, ALU.add).then_inc(counted, 1)
            dve.wait_ge(counts_ready, BITS + 1)
            own(dve.tensor_scalar(need[:, :], c_ps[:, 0:E], -1.0, float(CAP), ALU.mult, ALU.add))
            ranks(equal, 0)
            own(dve.tensor_tensor(flags[:, :, :], rank[:, :, :], over_tiles(need[:, :]), ALU.is_lt))
            own(dve.tensor_tensor(equal[:, :, :], equal[:, :, :], flags[:, :, :], ALU.mult))
            own(dve.tensor_tensor(equal[:, :, :], equal[:, :, :], above[:, :, :], ALU.add))
            ranks(equal, 1)
            own(dve.scalar_tensor_tensor(out=slot[:, :, :], in0=rank[:, :, :], scalar=1.0, in1=equal[:, :, :],
                                         op0=ALU.add, op1=ALU.mult))
            own(dve.tensor_scalar(slot[:, :, :], slot[:, :, :], -1.0, None, ALU.add))
            own(dve.tensor_copy(payload[:, :, :, 2], aff[:, :, :]))
            own(dve.tensor_tensor(rest[:, :, :], aff[:, :, :], payload[:, :, :, 2], ALU.subtract))
            own(dve.tensor_copy(payload[:, :, :, 3], rest[:, :, :]))
            own(dve.tensor_tensor(rest[:, :, :], rest[:, :, :], payload[:, :, :, 3], ALU.subtract))
            own(dve.tensor_copy(payload[:, :, :, 4], rest[:, :, :]))
            credit(dve, pay_ready, 1)
            with dve.Fori(0, E) as e:
                for t in range(TILES):
                    dve.wait_ge(hot_used, e * TILES + (t + 1))
                    dve.tensor_scalar(hot[t % RING][:, :], iota_s[:, :],
                                      slot[:, t, bass.ds(e, 1)], None, ALU.is_equal).then_inc(hot_ready, 1)
            dve.wait_ge(hot_used, E * TILES + RING)
            own(dve.tensor_copy(got[:, :, :, :], s_ps[:, :, 0:E * NPAY].rearrange("p a (e n) -> p a e n", n=NPAY)))
            own(dve.scalar_tensor_tensor(out=token_f[:, :, :], in0=got[:, :, :, 1], scalar=float(P), in1=got[:, :, :, 0],
                                         op0=ALU.mult, op1=ALU.add))
            own(dve.tensor_copy(slot_token[:, :, :], token_f[:, :, :]))
            own(dve.tensor_tensor(gate_part[:, :, :], got[:, :, :, 3], got[:, :, :, 4], ALU.add))
            own(dve.tensor_tensor(slot_gate[:, :, :], gate_part[:, :, :], got[:, :, :, 2], ALU.add))

        @block.tensor
        def _(pe):
            credit(pe, hot_used, RING)
            pe.wait_ge(consts, 7)
            with pe.Fori(0, BITS + 1) as i:
                pe.wait_ge(counted, i + 1)
                pe.matmul(c_ps[:, 0:E], ones[:, :], count[:, :], start=True, stop=True).then_inc(counts_ready, 1)
            for k in range(2):
                pe.wait_ge(flags_ready, k + 1)
                flat = equal[:, :, :].rearrange("p t e -> p (t e)")
                pe.matmul(r_ps[:, 0:TE], before[:, :], flat, start=True, stop=True)
                pe.matmul(tot_ps[:, 0:TE], ones[:, :], flat, start=True, stop=True).then_inc(sums_ready, 1)
            pe.wait_ge(pay_ready, 1)
            with pe.Fori(0, E) as e:
                for t in range(TILES):
                    pe.wait_ge(hot_ready, e * TILES + (t + 1))
                    for a in range(HALVES):
                        mm = pe.matmul(s_ps[:, a, bass.ds(e * NPAY, NPAY)], hot[t % RING][:, a * P:(a + 1) * P],
                                       payload[:, t, bass.ds(e, 1), :].rearrange("p a n -> p (a n)"),
                                       start=(t == 0), stop=(t == TILES - 1))
                    mm.then_inc(hot_used, 1)


def experts(nc, hn_moe, w_gate, w_up, w_down, slot_token, slot_gate, h_res):
    CH = 2 * P
    NC = F // CH
    PER = 3 * NC
    RING = 3
    HALVES = CAP // P
    FB = CH // P
    with Parts(nc, "ex") as m:
        ident = m.sb("ident", [P, P])
        w_st = [m.sb(f"w_st{r}", [P, KB * CH]) for r in range(RING)]
        w_hi = [m.sb(f"w_hi{r}", [P, KB * CH], F32R) for r in range(RING)]
        w_lo = [m.sb(f"w_lo{r}", [P, KB * CH], F32R) for r in range(RING)]
        tokens = m.sb("tokens", [P, HALVES], U32)
        tokens_out = m.sb("tokens_out", [P, HALVES], U32)
        rows = m.sb("rows", [P, HALVES, D])
        xt_hi = m.sb("xt_hi", [P, KB, CAP], F32R)
        xt_lo = m.sb("xt_lo", [P, KB, CAP], F32R)
        silu = [m.sb(f"silu{b}", [P, FB * CAP]) for b in range(2)]
        hid = [m.sb(f"hid{b}", [P, FB * CAP]) for b in range(2)]
        hid_hi = m.sb("hid_hi", [P, NC, FB * CAP], F32R)
        hid_lo = m.sb("hid_lo", [P, NC, FB * CAP], F32R)
        y = m.sb("y", [P, HALVES, D])
        gu_ps = m.psum("gu_ps", [P, 4, BANK])
        y_ps = m.psum("y_ps", [P, HALVES, D])

        sem = m.sem
        consts = sem("consts")
        w_loaded = [sem(f"w_loaded{r}") for r in range(RING)]
        whi_ready, wlo_ready, w_used = sem("whi_ready"), sem("wlo_ready"), sem("w_used")
        tokens_ready, tokens_out_ready = sem("tokens_ready"), sem("tokens_out_ready")
        gathered, turned, xthi_ready, xtlo_ready = sem("gathered"), sem("turned"), sem("xthi_ready"), sem("xtlo_ready")
        silu_ready, hid_ready, hidhi_ready, hidlo_ready = sem("silu_ready"), sem("hid_ready"), sem("hidhi_ready"), sem("hidlo_ready")
        y_ready, y_scaled, y_free, added, ticks = sem("y_ready"), sem("y_scaled"), sem("y_free"), sem("added"), sem("ticks")
        block = m.block()

        def wide(t):
            return t[:, :].rearrange("p (k c) -> p k c", c=CH)

        def tall(t):
            return t[:, :].rearrange("p (k c) -> p k c", c=D)

        def all_experts(eng, fn, last=None):
            fn(0)
            with eng.Fori(1, E - 1) as e:
                fn(e)
            fn(E - 1)

        @block.sync
        def _(sp):
            def expert(e):
                for c in range(PER):
                    r = c % RING
                    first = isinstance(e, int) and e == 0 and c < RING
                    if not first:
                        sp.wait_ge(wlo_ready, e * PER + (c - RING + 1))
                    q, kind = (c // 2, c % 2) if c < 2 * NC else (c - 2 * NC, 2)
                    if kind < 2:
                        src = (w_gate, w_up)[kind][0].rearrange("e (k p) c -> e p k c", p=P)[
                            bass.ds(e, 1), :, :, q * CH:(q + 1) * CH].rearrange("e p k c -> (e p) k c")
                        dst = wide(w_st[r])
                    else:
                        src = w_down[0].rearrange("e (k p) c -> e p k c", p=P)[
                            bass.ds(e, 1), :, FB * q:FB * (q + 1), :].rearrange("e p k c -> (e p) k c")
                        dst = tall(w_st[r])
                    sp.dma_start(dst, src).then_inc(w_loaded[r], 16)

            all_experts(sp, expert)

        @block.gpsimd
        def _(pool):
            identity_steps(pool, ident, consts)
            credit(pool, y_free, 1)

            def gather(e):
                pool.tensor_copy(tokens[:, :], slot_token[:, :, bass.ds(e, 1)].rearrange("p a e -> p (a e)")
                                 ).then_inc(tokens_ready, 1)
                pool.wait_ge(tokens_ready, e + 1)
                pool.sem_inc(ticks, 1)
                for a in range(HALVES):
                    pool.indirect_dma_start(out=rows[:, a, :], out_offset=None, in_=hn_moe,
                                            in_offset=bass.IndirectOffsetOnAxis(ap=tokens[:, a:a + 1], axis=0)
                                            ).then_inc(gathered, 16)

            def expert(e):
                if not (isinstance(e, int) and e == E - 1):
                    pool.wait_ge(turned, e * 4 + 4)
                    pool.sem_inc(ticks, 1)
                    gather(e + 1)
                if not (isinstance(e, int) and e == 0):
                    pool.wait_ge(added, e * 32)
                    pool.sem_inc(y_free, 1)
                pool.tensor_copy(tokens_out[:, :], slot_token[:, :, bass.ds(e, 1)].rearrange("p a e -> p (a e)")
                                 ).then_inc(tokens_out_ready, 1)
                pool.wait_ge(tokens_out_ready, e + 1)
                pool.wait_ge(y_scaled, e * 2 + 2)
                pool.sem_inc(ticks, 1)
                for a in range(HALVES):
                    pool.indirect_dma_start(out=h_res, out_offset=bass.IndirectOffsetOnAxis(ap=tokens_out[:, a:a + 1], axis=0),
                                            in_=y[:, a, :], in_offset=None, compute_op=ALU.add).then_inc(added, 16)

            gather(0)
            all_experts(pool, expert)
            pool.wait_ge(added, 32 * E)

        @block.scalar
        def _(act):
            def split_w(e, c):
                r = c % RING
                act.wait_ge(w_loaded[r], (e * (PER // RING) + (c // RING + 1)) * 16)
                if not (isinstance(e, int) and e == 0 and c < RING):
                    act.wait_ge(w_used, e * PER + (c - RING + 1))
                act.activation(w_hi[r][:, :], w_st[r][:, :], ACT.Copy).then_inc(whi_ready, 1)

            def split_x(e, g):
                act.wait_ge(turned, e * 4 + (g + 1))
                act.activation(xt_hi[:, 2 * g:2 * g + 2, :], gu_ps[:, g, :].rearrange("p (k s) -> p k s", s=CAP), ACT.Copy
                               ).then_inc(xthi_ready, 1)

            def hidden(e, q):
                b = q % 2
                act.wait_ge(w_used, e * PER + (2 * q + 1))
                act.wait_ge(hid_ready, (e - 1) * NC + (NC + q - 1)) if not (isinstance(e, int) and e == 0 and q < 2) else None
                act.activation(silu[b][:, :], gu_ps[:, 2 * b, :], ACT.Silu).then_inc(silu_ready, 1)

            def hidden_hi(e, q):
                act.wait_ge(hid_ready, e * NC + (q + 1))
                if q == 0 and not (isinstance(e, int) and e == 0):
                    act.wait_ge(w_used, e * PER)
                act.activation(hid_hi[:, q, :], hid[q % 2][:, :], ACT.Copy).then_inc(hidhi_ready, 1)

            def expert(e):
                for q in range(NC):
                    for c in (2 * q, 2 * q + 1):
                        if not (isinstance(e, int) and e == 0 and c < 2):
                            split_w(e, c)
                    if q:
                        hidden(e, q - 1)
                        hidden_hi(e, q - 1)
                split_w(e, 2 * NC)
                hidden(e, NC - 1)
                hidden_hi(e, NC - 1)
                last = isinstance(e, int) and e == E - 1
                for q in range(1, NC):
                    split_w(e, 2 * NC + q)
                    if not last:
                        if q == 1:
                            for g in range(2):
                                split_x(e + 1, g)
                        if q == 2:
                            for g in range(2, 4):
                                split_x(e + 1, g)

            for c in range(2):
                split_w(0, c)
            for g in range(4):
                split_x(0, g)
            all_experts(act, expert)

        @block.vector
        def _(dve):
            def split_w(e, c):
                r = c % RING
                dve.wait_ge(whi_ready, e * PER + (c + 1))
                dve.tensor_tensor(w_lo[r][:, :], w_st[r][:, :], w_hi[r][:, :].bitcast(F32), ALU.subtract
                                  ).then_inc(wlo_ready, 1)

            def split_x(e, g):
                dve.wait_ge(xthi_ready, e * 4 + (g + 1))
                dve.tensor_tensor(xt_lo[:, 2 * g:2 * g + 2, :], gu_ps[:, g, :].rearrange("p (k s) -> p k s", s=CAP),
                                  xt_hi[:, 2 * g:2 * g + 2, :].bitcast(F32), ALU.subtract).then_inc(xtlo_ready, 1)

            def hidden(e, q):
                b = q % 2
                dve.wait_ge(w_used, e * PER + (2 * q + 2))
                dve.wait_ge(silu_ready, e * NC + (q + 1))
                if not (isinstance(e, int) and e == 0 and q < 2):
                    dve.wait_ge(hidlo_ready, e * NC + (q - 1))
                dve.tensor_tensor(hid[b][:, :], silu[b][:, :], gu_ps[:, 2 * b + 1, :], ALU.mult).then_inc(hid_ready, 1)

            def hidden_lo(e, q):
                dve.wait_ge(hidhi_ready, e * NC + (q + 1))
                dve.tensor_tensor(hid_lo[:, q, :], hid[q % 2][:, :], hid_hi[:, q, :].bitcast(F32), ALU.subtract
                                  ).then_inc(hidlo_ready, 1)

            def scale_y(e):
                dve.wait_ge(y_ready, e + 1)
                dve.wait_ge(y_free, e + 1)
                for a in range(HALVES):
                    dve.tensor_scalar(y[:, a, :], y_ps[:, a, :], slot_gate[:, a, bass.ds(e, 1)], None, ALU.mult
                                      ).then_inc(y_scaled, 1)

            def expert(e):
                for q in range(NC):
                    for c in (2 * q, 2 * q + 1):
                        if not (isinstance(e, int) and e == 0 and c < 2):
                            split_w(e, c)
                    if q == 1 and not (isinstance(e, int) and e == 0):
                        scale_y(e - 1)
                    if q:
                        hidden(e, q - 1)
                        hidden_lo(e, q - 1)
                split_w(e, 2 * NC)
                hidden(e, NC - 1)
                hidden_lo(e, NC - 1)
                last = isinstance(e, int) and e == E - 1
                for q in range(1, NC):
                    split_w(e, 2 * NC + q)
                    if not last:
                        if q == 1:
                            for g in range(2):
                                split_x(e + 1, g)
                        if q == 2:
                            for g in range(2, 4):
                                split_x(e + 1, g)

            for c in range(2):
                split_w(0, c)
            for g in range(4):
                split_x(0, g)
            all_experts(dve, expert)
            scale_y(E - 1)

        @block.tensor
        def _(pe):
            pe.wait_ge(consts, 2)

            def turn(e):
                pe.wait_ge(gathered, e * 32 + 32)
                if not (isinstance(e, int) and e == 0):
                    pe.wait_ge(hid_ready, e * NC - 1)
                for g in range(4):
                    if g == 2 and not (isinstance(e, int) and e == 0):
                        pe.wait_ge(hid_ready, e * NC)
                    for k in range(2 * g, 2 * g + 2):
                        for a in range(HALVES):
                            t = pe.transpose(gu_ps[:, g, (k % 2) * CAP + a * P:(k % 2) * CAP + (a + 1) * P],
                                             rows[:, a, k * P:(k + 1) * P], ident[:, :])
                    t.then_inc(turned, 1)

            def gate_up(e, c):
                r, q, kind = c % RING, c // 2, c % 2
                bank = 2 * (q % 2) + kind
                pe.wait_ge(wlo_ready, e * PER + (c + 1))
                if c == 0:
                    pe.wait_ge(xtlo_ready, e * 4 + 4)
                elif c >= 4:
                    pe.wait_ge(hid_ready, e * NC + (q - 1))
                hi, lo = wide(w_hi[r]), wide(w_lo[r])
                for f in range(FB):
                    dst, cols = gu_ps[:, bank, f * CAP:(f + 1) * CAP], slice(f * P, (f + 1) * P)
                    for k in range(KB):
                        pe.matmul(dst, hi[:, k, cols], xt_hi[:, k, :], start=(k == 0), stop=False)
                        pe.matmul(dst, hi[:, k, cols], xt_lo[:, k, :], start=False, stop=False)
                        mm = pe.matmul(dst, lo[:, k, cols], xt_hi[:, k, :], start=False, stop=(k == KB - 1))
                mm.then_inc(w_used, 1)

            def down(e, q):
                c = 2 * NC + q
                r = c % RING
                pe.wait_ge(wlo_ready, e * PER + (c + 1))
                pe.wait_ge(hidlo_ready, e * NC + (q + 1))
                if q == 0 and not (isinstance(e, int) and e == 0):
                    pe.wait_ge(y_scaled, e * 2)
                hi, lo = tall(w_hi[r]), tall(w_lo[r])
                for f in range(FB):
                    for a in range(HALVES):
                        slots = slice(f * CAP + a * P, f * CAP + (a + 1) * P)
                        for n in range(D // BANK):
                            cols = slice(n * BANK, (n + 1) * BANK)
                            dst = y_ps[:, a, cols]
                            first, last = q == 0 and f == 0, q == NC - 1 and f == FB - 1
                            pe.matmul(dst, hid_hi[:, q, slots], hi[:, f, cols], start=first, stop=False)
                            pe.matmul(dst, hid_hi[:, q, slots], lo[:, f, cols], start=False, stop=False)
                            mm = pe.matmul(dst, hid_lo[:, q, slots], hi[:, f, cols], start=False, stop=last)
                mm.then_inc(w_used, 1)
                if q == NC - 1:
                    pe.wait_ge(w_used, e * PER + PER)
                    pe.nop().then_inc(y_ready, 1)

            def expert(e):
                for c in range(2 * NC):
                    gate_up(e, c)
                if not (isinstance(e, int) and e == E - 1):
                    turn(e + 1)
                for q in range(NC):
                    down(e, q)

            turn(0)
            all_experts(pe, expert)


def gated_ple(nc, h_res, p_emb, g_ple, w_ple_gate, w_ple_proj, g_final, out):
    PB = PLE // P
    KT = KB + PB
    GROUPS = [(0, 4), (4, 8), (8, 10)]
    with Parts(nc, "pl") as m:
        ident = m.sb("ident", [P, P])
        w_st = [m.sb(f"w_st{b}", [P, D]) for b in range(2)]
        w_hi = m.sb("w_hi", [P, KT, D], F32R)
        w_lo = m.sb("w_lo", [P, KT, D], F32R)
        g_in = m.sb("g_in", [P, D])
        g_out = m.sb("g_out", [P, D])
        mhalf = m.sb("mhalf", [P, 1])
        h_in = [m.sb(f"h_in{i}", [P, D]) for i in range(4)]
        p_in = [m.sb(f"p_in{b}", [P, PLE]) for b in range(2)]
        sq = m.sb("sq", [P, D])
        ss, ms, rs = (m.sb(n, [P, 1]) for n in ("ss", "ms", "rs"))
        ss2, ms2, rs2 = (m.sb(n, [P, 1]) for n in ("ss2", "ms2", "rs2"))
        hn = [m.sb(f"hn{b}", [P, D]) for b in range(2)]
        t_hi = [m.sb(f"t_hi{b}", [P, KT, P], F32R) for b in range(2)]
        t_lo = [m.sb(f"t_lo{b}", [P, KT, P], F32R) for b in range(2)]
        gate = m.sb("gate", [P, D])
        mixed = m.sb("mixed", [P, D])
        out_sb = [m.sb(f"out_sb{b}", [P, D]) for b in range(2)]
        t_ps = m.psum("t_ps", [P, 3, BANK])
        g_ps = m.psum("g_ps", [P, D])
        p_ps = m.psum("p_ps", [P, D])

        sem = m.sem
        consts, mhalf_ready, gains_loaded = sem("consts"), sem("mhalf_ready"), sem("gains_loaded")
        w_loaded = [sem(f"w_loaded{b}") for b in range(2)]
        whi_ready, wlo_ready = sem("whi_ready"), sem("wlo_ready")
        h_loaded = [sem(f"h_loaded{i}") for i in range(4)]
        p_loaded = [sem(f"p_loaded{b}") for b in range(2)]
        squared, means, rsqrt, normed, turned, thi_ready, tlo_ready = (
            sem(n) for n in ("squared", "means", "rsqrt", "normed", "turned", "thi_ready", "tlo_ready"))
        g_ready, p_ready, gated, mixed_ready, h_ready, squared2, means2, rsqrt2, out_ready = (
            sem(n) for n in ("g_ready", "p_ready", "gated", "mixed_ready", "h_ready", "squared2", "means2", "rsqrt2", "out_ready"))
        out_stored = [sem(f"out_stored{b}") for b in range(2)]
        block = m.block()

        def run(eng, fn):
            for n in range(4):
                fn(n, n, n)
            with eng.Fori(1, TILES // 4 - 1) as j:
                for s in range(4):
                    fn(j * 4 + s, s, None)
            for n in range(TILES - 4, TILES + 2):
                fn(n, n % 4, n)

        def has(i, lag):
            return i is None or 0 <= i - lag < TILES

        def h_turns(n, s):
            return n * 4 + (16 - 4 * s)

        @block.sync
        def _(sp):
            for g, dst in ((g_ple, g_in), (g_final.rearrange("(l n) -> l n", l=1), g_out)):
                sp.dma_start(dst[:, :], g.partition_broadcast(P).rearrange("p l n -> p (l n)")).then_inc(gains_loaded, 16)
            for n in range(2):
                sp.dma_start(h_in[n][:, :], h_res[n * P:(n + 1) * P, :]).then_inc(h_loaded[n], 16)
                sp.dma_start(p_in[n][:, :], p_emb[0, 0, n * P:(n + 1) * P, :]).then_inc(p_loaded[n], 16)
            for k in range(KT):
                if k >= 2:
                    sp.wait_ge(wlo_ready, k - 1)
                src = w_ple_gate[0, k * P:(k + 1) * P, :] if k < KB else w_ple_proj[0, (k - KB) * P:(k - KB + 1) * P, :]
                sp.dma_start(w_st[k % 2][:, :], src).then_inc(w_loaded[k % 2], 16)

            def step(n, s, i):
                b = s % 2
                if i is None or 2 <= i < TILES:
                    if i is None or i >= 4:
                        sp.wait_ge(h_ready, n - 3)
                        sp.wait_ge(out_ready, n - 3)
                    sp.dma_start(h_in[s][:, :], h_res[bass.ds(n * P, P), :]).then_inc(h_loaded[s], 16)
                    sp.wait_ge(turned, 3 * (n - 1))
                    sp.dma_start(p_in[b][:, :], p_emb[0, 0, bass.ds(n * P, P), :]).then_inc(p_loaded[b], 16)
                if has(i, 2):
                    sp.wait_ge(out_ready, n - 1)
                    sp.dma_start(out[0, bass.ds((n - 2) * P, P), :], out_sb[b][:, :]).then_inc(out_stored[b], 16)

            run(sp, step)
            for b in range(2):
                sp.wait_ge(out_stored[b], 8 * TILES)

        @block.gpsimd
        def _(pool):
            identity_steps(pool, ident, consts)
            pool.memset(mhalf[:, :], -0.5).then_inc(mhalf_ready, 1)
            pool.wait_ge(mhalf_ready, 1)

            def norm(n):
                pool.wait_ge(means, n + 1)
                pool.tensor_tensor(rs[:, :], ms[:, :], mhalf[:, :], ALU.pow).then_inc(rsqrt, 1)

            def step(n, s, i):
                if i is None or i < TILES - 1:
                    norm(n + 1)
                if has(i, 1):
                    pool.wait_ge(means2, n)
                    pool.tensor_tensor(rs2[:, :], ms2[:, :], mhalf[:, :], ALU.pow).then_inc(rsqrt2, 1)

            norm(0)
            run(pool, step)

        @block.scalar
        def _(act):
            def square(n, s):
                act.wait_ge(h_loaded[s], h_turns(n, s))
                if not isinstance(n, int) or n >= 1:
                    act.wait_ge(means, n)
                    act.wait_ge(squared, n)
                if not isinstance(n, int) or n >= 3:
                    act.wait_ge(squared2, n - 2)
                act.activation(sq[:, :], h_in[s][:, :], ACT.Square, accum_out=ss[:, :]).then_inc(squared, 1)

            square(0, 0)
            for k in range(KT):
                act.wait_ge(w_loaded[k % 2], 16 * (k // 2 + 1))
                act.activation(w_hi[:, k, :], w_st[k % 2][:, :], ACT.Copy).then_inc(whi_ready, 1)

            def step(n, s, i):
                b = s % 2
                if has(i, 0):
                    for g, (lo, hi) in enumerate(GROUPS):
                        act.wait_ge(turned, 3 * n + (g + 1))
                        if g == 0 and (i is None or i >= 2):
                            act.wait_ge(p_ready, n - 1)
                        act.activation(t_hi[b][:, lo:hi, :], t_ps[:, g, 0:(hi - lo) * P].rearrange("p (k t) -> p k t", t=P),
                                       ACT.Copy).then_inc(thi_ready, 1)
                if i is None or i < TILES - 1:
                    square(n + 1, (s + 1) % 4)
                if has(i, 1):
                    act.wait_ge(g_ready, n)
                    if i is None or i >= 2:
                        act.wait_ge(mixed_ready, n - 1)
                    act.activation(gate[:, :], g_ps[:, :], ACT.Sigmoid).then_inc(gated, 1)
                    act.wait_ge(h_ready, n)
                    if i is None or i >= 2:
                        act.wait_ge(means2, n - 1)
                    if i is None or i < TILES - 1:
                        act.wait_ge(squared, n + 2)
                    else:
                        act.wait_ge(squared, TILES)
                    act.activation(sq[:, :], h_in[(s + 3) % 4][:, :], ACT.Square, accum_out=ss2[:, :]).then_inc(squared2, 1)

            run(act, step)

        @block.vector
        def _(dve):
            dve.wait_ge(gains_loaded, 32)

            def norm(n, s):
                b = s % 2
                dve.wait_ge(squared, n + 1)
                if not isinstance(n, int) or n >= 1:
                    dve.wait_ge(rsqrt, n)
                dve.tensor_scalar(ms[:, :], ss[:, :], 1.0 / D, EPS, ALU.mult, ALU.add).then_inc(means, 1)
                dve.wait_ge(rsqrt, n + 1)
                if not isinstance(n, int) or n >= 2:
                    dve.wait_ge(turned, 3 * n - 3)
                dve.scalar_tensor_tensor(out=hn[b][:, :], in0=h_in[s][:, :], scalar=rs[:, 0:1], in1=g_in[:, :],
                                         op0=ALU.mult, op1=ALU.mult).then_inc(normed, 1)

            norm(0, 0)
            for k in range(KT):
                dve.wait_ge(whi_ready, k + 1)
                dve.tensor_tensor(w_lo[:, k, :], w_st[k % 2][:, :], w_hi[:, k, :].bitcast(F32), ALU.subtract
                                  ).then_inc(wlo_ready, 1)

            def step(n, s, i):
                b = s % 2
                if has(i, 0):
                    for g, (lo, hi) in enumerate(GROUPS):
                        dve.wait_ge(thi_ready, 3 * n + (g + 1))
                        dve.tensor_tensor(t_lo[b][:, lo:hi, :], t_ps[:, g, 0:(hi - lo) * P].rearrange("p (k t) -> p k t", t=P),
                                          t_hi[b][:, lo:hi, :].bitcast(F32), ALU.subtract).then_inc(tlo_ready, 1)
                if i is None or i < TILES - 1:
                    norm(n + 1, (s + 1) % 4)
                if has(i, 1):
                    h = h_in[(s + 3) % 4]
                    dve.wait_ge(gated, n)
                    dve.wait_ge(p_ready, n)
                    dve.tensor_tensor(mixed[:, :], p_ps[:, :], gate[:, :], ALU.mult).then_inc(mixed_ready, 1)
                    dve.wait_ge(mixed_ready, n)
                    dve.tensor_tensor(h[:, :], h[:, :], mixed[:, :], ALU.add).then_inc(h_ready, 1)
                    dve.wait_ge(squared2, n)
                    if i is None or i >= 2:
                        dve.wait_ge(rsqrt2, n - 1)
                    dve.tensor_scalar(ms2[:, :], ss2[:, :], 1.0 / D, EPS, ALU.mult, ALU.add).then_inc(means2, 1)
                    dve.wait_ge(rsqrt2, n)
                    if i is None or i >= 3:
                        dve.wait_ge(out_stored[1 - b], n * 8 + (-16 if b == 0 else -8) + 0)
                    dve.scalar_tensor_tensor(out=out_sb[1 - b][:, :], in0=h[:, :], scalar=rs2[:, 0:1], in1=g_out[:, :],
                                             op0=ALU.mult, op1=ALU.mult).then_inc(out_ready, 1)

            run(dve, step)

        @block.tensor
        def _(pe):
            pe.wait_ge(consts, 2)

            def step(n, s, i):
                b = s % 2
                if has(i, 0):
                    pe.wait_ge(normed, n + 1)
                    pe.wait_ge(p_loaded[b], n * 8 + (16 - 8 * b))
                    for g, (lo, hi) in enumerate(GROUPS):
                        if i is None or i >= 1:
                            pe.wait_ge(tlo_ready, 3 * n + (g - 2))
                        for k in range(lo, hi):
                            src = hn[b][:, k * P:(k + 1) * P] if k < KB else p_in[b][:, (k - KB) * P:(k - KB + 1) * P]
                            t = pe.transpose(t_ps[:, g, (k - lo) * P:(k - lo + 1) * P], src, ident[:, :])
                        t.then_inc(turned, 1)
                if has(i, 1):
                    c = 1 - b
                    pe.wait_ge(tlo_ready, 3 * n)
                    if i is not None and i == 1:
                        pe.wait_ge(wlo_ready, KT)
                    for dst, lo, hi, done in ((g_ps, 0, KB, g_ready), (p_ps, KB, KT, p_ready)):
                        if i is None or i >= 2:
                            pe.wait_ge(gated if lo == 0 else mixed_ready, n - 1)
                        for half in range(2):
                            cols = slice(half * BANK, (half + 1) * BANK)
                            for k in range(lo, hi):
                                pe.matmul(dst[:, cols], t_hi[c][:, k, :], w_hi[:, k, cols], start=(k == lo), stop=False)
                                pe.matmul(dst[:, cols], t_hi[c][:, k, :], w_lo[:, k, cols], start=False, stop=False)
                                mm = pe.matmul(dst[:, cols], t_lo[c][:, k, :], w_hi[:, k, cols], start=False, stop=(k == hi - 1))
                        mm.then_inc(done, 1)

            run(pe, step)


def encoder_layer(nc, x, p, g_mix, w_in, na_rpb, g_na_out, lam_q1, lam_k1, lam_q2, lam_k2, g_diff_out, w_out, g_moe,
                  w_router, w_gate, w_up, w_down, g_ple, w_ple_gate, w_ple_proj, g_final, out):
    def dram(name, *shape):
        return nc.dram_tensor(name, shape, F32).ap()

    feat_t = dram("feat_t", 2, D, SEQ)
    v_tok = dram("v_tok", 2, SEQ, D // 2)
    alibi = dram("alibi", DIFF_HEADS, P, 2 * SEQ - P)
    rpb_rows = dram("rpb_rows", NA_HEADS * (2 * KH - 1), 2 * GRID_W - 1)
    na_bias = dram("na_bias", PAIRS, P, (2 * KH - 1) * GRID_W)
    o_cat = dram("o_cat", SEQ, D)
    h_res = dram("h_res", SEQ, D)
    hn_moe = dram("hn_moe", SEQ, D)
    project(nc, x, g_mix, w_in, feat_t, v_tok)
    tables(nc, na_rpb, alibi, rpb_rows, na_bias)
    neighbourhood(nc, feat_t, v_tok, na_bias, o_cat)
    differential(nc, feat_t, v_tok, alibi, (lam_q1, lam_k1, lam_q2, lam_k2), o_cat)
    with Parts(nc, "routes") as m:
        logits = m.sb("logits", [P, TILES, E])
        slot_token = m.sb("slot_token", [P, CAP // P, E], U32)
        slot_gate = m.sb("slot_gate", [P, CAP // P, E])
        mix_out(nc, x, o_cat, g_na_out, g_diff_out, w_out, g_moe, w_router, h_res, hn_moe, logits)
        route(nc, logits, slot_token, slot_gate)
        experts(nc, hn_moe, w_gate, w_up, w_down, slot_token, slot_gate, h_res)
    gated_ple(nc, h_res, p, g_ple, w_ple_gate, w_ple_proj, g_final, out)


def kernel(**inputs):
    import concourse.bacc as bacc
    import numpy as np
    from concourse.bass_utils import run_bass_kernel_spmd

    names = ["x", "p", "g_mix", "w_in", "na_rpb", "g_na_out", "lam_q1", "lam_k1", "lam_q2", "lam_k2", "g_diff_out",
             "w_out", "g_moe", "w_router", "w_gate", "w_up", "w_down", "g_ple", "w_ple_gate", "w_ple_proj", "g_final"]
    nc = bacc.Bacc("TRN2", target_bir_lowering=False, num_devices=1)
    arrays, args = {}, []
    for name in names:
        a = np.ascontiguousarray(inputs[name])
        arrays[f"in_{name}"] = a
        args.append(nc.dram_tensor(f"in_{name}", a.shape, mybir.dt.from_np(a.dtype), kind="ExternalInput").ap())
    out = nc.dram_tensor("out", (1, SEQ, D), F32, kind="ExternalOutput").ap()
    encoder_layer(nc, *args, out)
    r = run_bass_kernel_spmd(nc, [arrays], core_ids=[0])
    return r.results[0]["out"]
```

```python
from contextlib import ExitStack

import concourse.bass as bass
from concourse import mybir

F32 = mybir.dt.float32
F32R = mybir.dt.float32r
BF16 = mybir.dt.bfloat16
U32 = mybir.dt.uint32
I32 = mybir.dt.int32
ALU = mybir.AluOpType
ACT = mybir.ActivationFunctionType
AX = mybir.AxisListType

P = 128
BANK = 512
SEQ = 2048
D = 1024
KB = D // P
TILES = SEQ // P
EPS = 1e-6

GRID_W = 64
ROWS = SEQ // GRID_W
DH = 64
NA_HEADS = 8
PAIRS = NA_HEADS // 2
KH = 8
KW = 16
NA_KEYS = KH * GRID_W
DIFF_HEADS = 4
LAM_INIT = 0.8 - 0.6
NEG = -1e30

E = 16
CAP = 2 * SEQ // E
F = 1024
PLE = 256
EXP_SCALE = DH ** -0.5


class Parts:

    def __init__(self, nc, name):
        self.nc, self.name, self.stack, self.sems = nc, name, ExitStack(), []

    def __enter__(self):
        self.stack.__enter__()
        return self

    def __exit__(self, *a):
        self.stack.__exit__(*a)
        if self.sems:
            self.nc.clear_and_free_semaphores(self.sems)
            self.nc.all_engine_barrier()

    def sb(self, name, shape, dt=F32):
        return self.stack.enter_context(self.nc.sbuf_tensor(f"{self.name}_{name}", shape, dt))

    def psum(self, name, shape, dt=F32):
        return self.stack.enter_context(self.nc.psum_tensor(f"{self.name}_{name}", shape, dt))

    def sem(self, name):
        self.sems.append(self.nc.alloc_semaphore(name=f"{self.name}_{name}"))
        return self.sems[-1]

    def block(self):
        return self.stack.enter_context(self.nc.Block())


def first_apart(eng, count, fn):
    fn(0)
    with eng.Fori(1, count) as g:
        fn(g)


def numbered(g, k):
    return isinstance(g, int) and g == k


def credit(eng, sem, n):
    eng.nop().then_inc(sem, n)


def identity_steps(pool, ident, sem):
    pool.memset(ident[:, :], 0.0).then_inc(sem, 1)
    pool.wait_ge(sem, 1)
    pool.affine_select(out=ident[:, :], in_=ident[:, :], compare_op=ALU.not_equal, fill=1.0, base=0,
                       pattern=[[-1, P]], channel_multiplier=1).then_inc(sem, 1)


def project(nc, x, g_mix, w_in, feat_t, v_tok):
    CW = 256
    GRP = 4
    CHUNKS = 3 * D // CW
    HALF = 3 * D // 2
    UNITS = 8
    with Parts(nc, "pr") as m:
        xt = m.sb("xt", [P, GRP, D])
        junk = m.sb("junk", [P, D])
        ss = m.sb("ss", [P, GRP])
        ms = m.sb("ms", [P, GRP])
        rs = m.sb("rs", [P, GRP])
        mhalf = m.sb("mhalf", [P, GRP])
        gain = m.sb("gain", [P, KB])
        ident = m.sb("ident", [P, P])
        h_hi = m.sb("h_hi", [P, KB, SEQ], F32R)
        h_lo = m.sb("h_lo", [P, KB, SEQ], F32R)
        wst = [m.sb(f"wst{b}", [P, KB, CW]) for b in range(2)]
        w_hi = [m.sb(f"w_hi{b}", [P, KB, CW], F32R) for b in range(2)]
        w_lo = [m.sb(f"w_lo{b}", [P, KB, CW], F32R) for b in range(2)]
        stage = m.sb("stage", [P, 4, BANK])
        turned = m.psum("turned", [P, 4, BANK])
        out = m.psum("out", [P, 4, BANK])

        x_in = [m.sem(f"x_in{s}") for s in range(GRP)]
        gain_in = m.sem("gain_in")
        w_scaled = m.sem("w_scaled")
        ticks = m.sem("ticks")
        w_loaded = [m.sem(f"w_loaded{b}") for b in range(2)]
        consts = m.sem("consts")
        squares = m.sem("squares")
        pool_own = m.sem("pool_own")
        means = m.sem("means")
        rs_ready = m.sem("rs_ready")
        normed = m.sem("normed")
        turned_ready = m.sem("turned_ready")
        hi_ready = m.sem("hi_ready")
        lo_ready = m.sem("lo_ready")
        whi_ready = m.sem("whi_ready")
        wlo_ready = m.sem("wlo_ready")
        out_ready = m.sem("out_ready")
        out_free = m.sem("out_free")
        stored = [m.sem(f"stored{s}") for s in range(4)]

        x_v = x.rearrange("o (g s p) d -> (o g) s p d", s=GRP, p=P)
        w_v = w_in.rearrange("l (k p) c -> (l p) k c", p=P)
        block = m.block()

        @block.sync
        def _(sp):
            sp.dma_start(gain[:, :], g_mix.rearrange("l (k p) -> (l p) k", p=P),
                         allow_slow_non_contiguous=True).then_inc(gain_in, 16)
            for s in range(GRP):
                sp.dma_start(xt[:, s, :], x_v[0, s]).then_inc(x_in[s], 16)
            for b in range(2):
                sp.dma_start(wst[b][:, :, :], w_v[:, :, b * CW:(b + 1) * CW]).then_inc(w_loaded[b], 16)
            with sp.Fori(1, TILES // GRP) as g:
                for s in range(GRP):
                    sp.wait_ge(turned_ready, g * (2 * GRP) + (2 * s + 2 - 2 * GRP))
                    sp.dma_start(xt[:, s, :], x_v[g, s]).then_inc(x_in[s], 16)

            def store(src_unit, dst, u):
                sp.wait_ge(out_free, src_unit + 5)
                sp.dma_start(dst, stage[:, u % 4, :]).then_inc(stored[u % 4], 16)

            with sp.Fori(0, 2) as half:
                with sp.Fori(0, 2) as j:
                    for b in range(2):
                        sp.wait_ge(wlo_ready, half * 6 + j * 2 + b + 1)
                        sp.dma_start(wst[b][:, :, :], w_v[:, :, bass.ds(half * HALF + j * 2 * CW + (b + 2) * CW, CW)]
                                     ).then_inc(w_loaded[b], 16)
                        for u in range(UNITS):
                            ft, tg = u // 4, u % 4
                            store(half * 48 + j * 16 + b * 8 + u,
                                  feat_t[half, bass.ds(j * 2 * CW + b * CW + ft * P, P), tg * BANK:(tg + 1) * BANK], u)
                for b in range(2):
                    sp.wait_ge(wlo_ready, half * 6 + 4 + b + 1)
                    sp.dma_start(wst[b][:, :, :], w_v[:, :, b * CW + HALF:(b + 1) * CW + HALF]).then_inc(w_loaded[b], 16)
                    for u in range(UNITS):
                        store(half * 48 + 32 + b * 8 + u,
                              v_tok[half, u * 2 * P:(u + 1) * 2 * P, b * CW:(b + 1) * CW].rearrange(
                                  "(a p) c -> p a c", p=P), u)
            for s in range(4):
                sp.wait_ge(stored[s], 16 * 24)
            for b in range(2):
                sp.wait_ge(w_loaded[b], 16 * 7)

        @block.gpsimd
        def _(pool):
            identity_steps(pool, ident, consts)
            pool.memset(mhalf[:, :], -0.5).then_inc(pool_own, 1)
            pool.wait_ge(pool_own, 1)

            def group(g):
                for s in range(GRP):
                    n = g * GRP + s
                    pool.wait_ge(means, n + 1)
                    if not numbered(g, 0):
                        pool.wait_ge(normed, n + (1 - GRP))
                    pool.tensor_tensor(rs[:, s:s + 1], ms[:, s:s + 1], mhalf[:, s:s + 1], ALU.pow).then_inc(rs_ready, 1)

            first_apart(pool, TILES // GRP, group)

            def weights(c, b, turns):
                pool.wait_ge(w_loaded[b], turns * 16 + 16)
                pool.wait_ge(w_scaled, c)
                pool.sem_inc(ticks, 1)
                pool.tensor_tensor(wst[b][:, :, :], wst[b][:, :, :], gain[:, :].unsqueeze(2).to_broadcast([P, KB, CW]), ALU.mult
                                   ).then_inc(w_scaled, 1)
                pool.wait_ge(whi_ready, c + 1)
                pool.wait_ge(wlo_ready, c)
                pool.tensor_tensor(w_lo[b][:, :, :], wst[b][:, :, :], w_hi[b][:, :, :].bitcast(F32), ALU.subtract
                                   ).then_inc(wlo_ready, 1)

            pool.wait_ge(gain_in, 16)
            weights(1, 1, 0)
            with pool.Fori(1, CHUNKS // 2) as c2:
                for b in range(2):
                    weights(c2 * 2 + b, b, c2)

        @block.scalar
        def _(act):
            def high(n, s):
                for half in range(2):
                    act.wait_ge(turned_ready, n * 2 + (half + 1))
                    act.activation(h_hi[:, 4 * half:4 * half + 4, bass.ds(n * P, P)],
                                   turned[:, 2 * (s % 2) + half, :].rearrange("p (k t) -> p k t", t=P), ACT.Copy
                                   ).then_inc(hi_ready, 1)

            def chunk_high(c, b):
                act.wait_ge(w_scaled, c + 1)
                act.activation(w_hi[b][:, :, :], wst[b][:, :, :], ACT.Copy).then_inc(whi_ready, 1)

            def group(g):
                for s in range(GRP):
                    n = g * GRP + s
                    act.wait_ge(x_in[s], g * 16 + 16)
                    if not numbered(n, 0):
                        act.wait_ge(squares, n)
                    if not numbered(g, 0):
                        act.wait_ge(means, n + (1 - GRP))
                    act.activation(junk[:, :], xt[:, s, :], ACT.Square, accum_out=ss[:, s:s + 1]).then_inc(squares, 1)
                    if not numbered(n, 0):
                        high(n - 1, (s - 1) % GRP)
                if numbered(g, 0):
                    chunk_high(0, 0)

            first_apart(act, TILES // GRP, group)
            high(TILES - 1, GRP - 1)
            chunk_high(1, 1)
            with act.Fori(1, CHUNKS // 2) as c2:
                for b in range(2):
                    act.wait_ge(out_ready, (c2 * 2 + b - 1) * UNITS)
                    chunk_high(c2 * 2 + b, b)

        @block.vector
        def _(dve):
            credit(dve, out_free, 4)
            dve.wait_ge(gain_in, 16)

            def low(n, s):
                for half in range(2):
                    dve.wait_ge(hi_ready, n * 2 + (half + 1))
                    blocks = slice(4 * half, 4 * half + 4)
                    dve.tensor_tensor(h_lo[:, blocks, bass.ds(n * P, P)],
                                      turned[:, 2 * (s % 2) + half, :].rearrange("p (k t) -> p k t", t=P),
                                      h_hi[:, blocks, bass.ds(n * P, P)].bitcast(F32), ALU.subtract).then_inc(lo_ready, 1)

            def group(g):
                for s in range(GRP):
                    n = g * GRP + s
                    dve.wait_ge(squares, n + 1)
                    if not numbered(g, 0):
                        dve.wait_ge(rs_ready, n + (1 - GRP))
                    dve.tensor_scalar(ms[:, s:s + 1], ss[:, s:s + 1], 1.0 / D, EPS, ALU.mult, ALU.add).then_inc(means, 1)
                    if not (numbered(n, 0) or numbered(n, 1)):
                        low(n - 2, (s - 2) % GRP)
                    dve.wait_ge(rs_ready, n + 1)
                    dve.tensor_scalar(xt[:, s, :], xt[:, s, :], rs[:, s:s + 1], None, ALU.mult).then_inc(normed, 1)
                if numbered(g, 0):
                    dve.wait_ge(w_loaded[0], 16)
                    dve.tensor_tensor(wst[0][:, :, :], wst[0][:, :, :], gain[:, :].unsqueeze(2).to_broadcast([P, KB, CW]),
                                      ALU.mult).then_inc(w_scaled, 1)

            def results(v):
                for s in range(4):
                    dve.wait_ge(out_ready, v * 4 + s + 1)
                    if not numbered(v, 0):
                        dve.wait_ge(stored[s], v * 16)
                    dve.tensor_copy(stage[:, s, :], out[:, s, :]).then_inc(out_free, 1)

            first_apart(dve, TILES // GRP, group)
            low(TILES - 2, (TILES - 2) % GRP)
            dve.wait_ge(whi_ready, 1)
            dve.tensor_tensor(w_lo[0][:, :, :], wst[0][:, :, :], w_hi[0][:, :, :].bitcast(F32), ALU.subtract
                              ).then_inc(wlo_ready, 1)
            low(TILES - 1, GRP - 1)
            first_apart(dve, 24, results)

        @block.tensor
        def _(pe):
            pe.wait_ge(consts, 2)

            def group(g):
                for s in range(GRP):
                    n = g * GRP + s
                    pe.wait_ge(normed, n + 1)
                    for half in range(2):
                        if not (numbered(n, 0) or numbered(n, 1)):
                            pe.wait_ge(lo_ready, n * 2 + (half - 3))
                        for j in range(4):
                            k = 4 * half + j
                            t = pe.transpose(turned[:, 2 * (s % 2) + half, j * P:(j + 1) * P], xt[:, s, k * P:(k + 1) * P],
                                             ident[:, :])
                        t.then_inc(turned_ready, 1)

            first_apart(pe, TILES // GRP, group)
            pe.wait_ge(lo_ready, 2 * TILES)

            def unit(n, u):
                pe.wait_ge(out_free, n + u + 1)

            def products(dst, lhs, rhs):
                pairs = [(a, b) for a, b in ((0, 0), (0, 1), (1, 0))]
                for k in range(KB):
                    for a, b in pairs:
                        mm = pe.matmul(dst, lhs(a, k), rhs(b, k), start=(k == 0 and (a, b) == (0, 0)),
                                       stop=(k == KB - 1 and (a, b) == (1, 0)))
                return mm

            hs = (h_hi, h_lo)

            def features(n, b):
                ws = (w_hi[b], w_lo[b])
                for u in range(UNITS):
                    ft, tg = u // 4, u % 4
                    unit(n, u)
                    mm = products(out[:, u % 4, :], lambda a, k: ws[a][:, k, ft * P:(ft + 1) * P],
                                  lambda c, k: hs[c][:, k, tg * BANK:(tg + 1) * BANK])
                    mm.then_inc(out_ready, 1)

            def tokens(n, b):
                ws = (w_hi[b], w_lo[b])
                for u in range(UNITS):
                    unit(n, u)
                    for a2 in range(2):
                        t = 2 * u + a2
                        mm = products(out[:, u % 4, a2 * CW:(a2 + 1) * CW], lambda a, k: hs[a][:, k, t * P:(t + 1) * P],
                                      lambda c, k: ws[c][:, k, :])
                    mm.then_inc(out_ready, 1)

            with pe.Fori(0, 2) as half:
                with pe.Fori(0, 2) as j:
                    for b in range(2):
                        pe.wait_ge(wlo_ready, half * 6 + j * 2 + b + 1)
                        features(half * 48 + j * 16 + b * 8, b)
                for b in range(2):
                    pe.wait_ge(wlo_ready, half * 6 + 4 + b + 1)
                    tokens(half * 48 + 32 + b * 8, b)


def neighbourhood(nc, feat_t, v_tok, na_bias, alibi, o_cat):
    WIDE = 2 * SEQ - P
    PARTS = 8
    PART = WIDE // PARTS
    STEPS = PAIRS * ROWS
    UNROLL = 4
    LAG = 4
    with Parts(nc, "na") as m:
        ident = m.sb("ident", [P, P])
        own = m.sb("own", [P, 2, DH])
        q_raw = [m.sb(f"q_raw{i}", [P, SEQ]) for i in range(2)]
        k_st = m.sb("k_st", [P, SEQ])
        v_st = [m.sb(f"v_st{o}", [P, TILES, P]) for o in range(2)]
        k_hi = [m.sb(f"k_hi{i}", [P, SEQ], F32R) for i in range(2)]
        k_lo = [m.sb(f"k_lo{i}", [P, SEQ], F32R) for i in range(2)]
        v_parts = [[m.sb(f"v_parts{i}{o}", [P, TILES - o, 2, P], F32R) for o in range(2)] for i in range(2)]
        table = [m.sb(f"table{i}", [P, 2 * KH - 1, GRID_W]) for i in range(2)]
        q_own = [m.sb(f"q_own{b}", [P, P]) for b in range(2)]
        q_hi = [m.sb(f"q_hi{b}", [P, P], F32R) for b in range(2)]
        q_lo = [m.sb(f"q_lo{b}", [P, P], F32R) for b in range(2)]
        probs = [m.sb(f"probs{b}", [P, NA_KEYS]) for b in range(UNROLL)]
        nmax = [m.sb(f"nmax{b}", [P, 1]) for b in range(2)]
        sums = [m.sb(f"sums{b}", [P, 1]) for b in range(2)]
        recip = [m.sb(f"recip{b}", [P, 1]) for b in range(2)]
        t_hi = [m.sb(f"t_hi{b}", [P, BANK], F32R) for b in range(2)]
        t_lo = [m.sb(f"t_lo{b}", [P, BANK], F32R) for b in range(2)]
        o_part = [m.sb(f"o_part{b}", [P, P]) for b in range(2)]
        o_all = [m.sb(f"o_all{i}", [P, ROWS, DH]) for i in range(2)]
        dist = m.sb("dist", [P, WIDE])
        s_ps = m.psum("s_ps", [P, 2, BANK])
        t_ps = m.psum("t_ps", [P, 2, BANK])
        o_ps = m.psum("o_ps", [P, 2, BANK])

        consts = m.sem("consts")
        own_ready = m.sem("own_ready")
        q_loaded = m.sem("q_loaded")
        k_loaded = m.sem("k_loaded")
        v_loaded = m.sem("v_loaded")
        table_loaded = m.sem("table_loaded")
        k_hi_ready = m.sem("k_hi_ready")
        k_lo_ready = m.sem("k_lo_ready")
        v_hi_ready = m.sem("v_hi_ready")
        v_lo_ready = m.sem("v_lo_ready")
        q_own_ready = m.sem("q_own_ready")
        q_hi_ready = m.sem("q_hi_ready")
        q_lo_ready = m.sem("q_lo_ready")
        s_ready = m.sem("s_ready")
        biased = m.sem("biased")
        exped = m.sem("exped")
        recips = m.sem("recips")
        t_ready = m.sem("t_ready")
        thi_ready = m.sem("thi_ready")
        tlo_ready = m.sem("tlo_ready")
        pv_done = m.sem("pv_done")
        o_part_ready = m.sem("o_part_ready")
        o_ready = m.sem("o_ready")
        o_stored = m.sem("o_stored")
        dist_made = m.sem("dist_made")
        dist_abs = m.sem("dist_abs")
        alibi_ready = m.sem("alibi_ready")
        alibi_stored = m.sem("alibi_stored")
        ticks = m.sem("ticks")
        block = m.block()

        q_dram = feat_t[0, 0:BANK, :].rearrange("(h d) t -> h d t", d=P)
        k_dram = feat_t[0, BANK:2 * BANK, :].rearrange("(h d) t -> h d t", d=P)
        v_dram = v_tok[0].rearrange("t (h e) -> h t e", e=P)

        def run(eng, fn):
            for h in range(PAIRS):
                for i in range(2 * UNROLL):
                    fn(h * ROWS + i, i % UNROLL, h, i)
                with eng.Fori(2, ROWS // UNROLL - 1) as j:
                    for s in range(UNROLL):
                        fn(j * UNROLL + (h * ROWS + s), s, h, (j, s))
                for i in range(ROWS - UNROLL, ROWS):
                    fn(h * ROWS + i, i % UNROLL, h, i)
            for i in range(LAG):
                fn(STEPS + i, i, PAIRS, i)

        def inner(i):
            return isinstance(i, tuple)

        def window(i):
            return min(max(i - KH // 2, 0), ROWS - KH)

        def at(i, k):
            return not inner(i) and i == k

        def has(n, i, lag):
            return inner(i) or 0 <= n - lag < STEPS

        def place(h, i, lag):
            if inner(i):
                return h, (i[0], i[1] - lag)
            return h + (i - lag) // ROWS, (i - lag) % ROWS

        def columns(row, off=0):
            if isinstance(row, tuple):
                return row[0] * (UNROLL * GRID_W) + (row[1] + off) * GRID_W
            return (row + off) * GRID_W

        @block.sync
        def _(sp):
            def load(h):
                if h >= 1:
                    sp.wait_ge(k_lo_ready, h)
                    sp.wait_ge(v_lo_ready, 2 * h)
                if h >= 2:
                    sp.wait_ge(q_own_ready, (h - 1) * ROWS)
                    sp.wait_ge(biased, (h - 1) * ROWS)
                sp.dma_start(k_st[:, :], k_dram[h]).then_inc(k_loaded, 16)
                sp.dma_start(q_raw[h % 2][:, :], q_dram[h]).then_inc(q_loaded, 16)
                sp.dma_start(table[h % 2][:, :, :].rearrange("p r c -> p (r c)"), na_bias[h]).then_inc(table_loaded, 16)
                for o in range(2):
                    sp.dma_start(v_st[o][:, 0:TILES - o, :],
                                 v_dram[h, o * GRID_W:SEQ - o * GRID_W, :].rearrange("(j p) e -> p j e", p=P)
                                 ).then_inc(v_loaded, 16)

            load(0)
            for h in range(PAIRS):
                if h < PAIRS - 1:
                    load(h + 1)
                sp.wait_ge(alibi_ready, PARTS * (h + 1))
                sp.dma_start(alibi[h], dist[:, :]).then_inc(alibi_stored, 16)
                sp.wait_ge(o_ready, 2 * ROWS * (h + 1))
                for hh in range(2):
                    sp.dma_start(o_cat.rearrange("(r q) f -> q r f", q=GRID_W)[:, :, h * P + hh * DH:h * P + (hh + 1) * DH],
                                 o_all[h % 2][hh * DH:(hh + 1) * DH, :, :]).then_inc(o_stored, 16)
            sp.wait_ge(o_stored, 16 * NA_HEADS)
            sp.wait_ge(alibi_stored, 16 * DIFF_HEADS)

        @block.gpsimd
        def _(pool):
            identity_steps(pool, ident, consts)
            pool.memset(own[:, :, :], 1.0).then_inc(own_ready, 1)
            pool.wait_ge(own_ready, 1)
            pool.affine_select(out=own[:, 0, :], in_=own[:, 0, :], compare_op=ALU.is_gt, fill=0.0, base=DH,
                               pattern=[[0, DH]], channel_multiplier=-1).then_inc(own_ready, 1)
            pool.affine_select(out=own[:, 1, :], in_=own[:, 1, :], compare_op=ALU.is_ge, fill=0.0, base=-DH,
                               pattern=[[0, DH]], channel_multiplier=1).then_inc(own_ready, 1)
            pool.wait_ge(own_ready, 3)

            def own_queries(m, b, h, row):
                if not isinstance(m, int) or m >= 2:
                    pool.wait_ge(q_lo_ready, m - 1)
                pool.wait_ge(q_loaded, 16 * (h + 1))
                pool.sem_inc(ticks, 1)
                pool.tensor_tensor(q_own[b][:, :].rearrange("p (a q) -> p a q", a=2),
                                   q_raw[h % 2][:, bass.ds(columns(row), GRID_W)].unsqueeze(1).to_broadcast([P, 2, GRID_W]),
                                   own[:, :, :], ALU.mult).then_inc(q_own_ready, 1)

            def queries_lo(m, b):
                pool.wait_ge(q_hi_ready, m + 1)
                pool.tensor_tensor(q_lo[b][:, :], q_own[b][:, :], q_hi[b][:, :].bitcast(F32), ALU.subtract
                                   ).then_inc(q_lo_ready, 1)

            def step(n, s, h, i):
                if has(n, i, -1):
                    queries_lo(n + 1, (s + 1) % 2)
                if has(n, i, -2):
                    own_queries(n + 2, s % 2, *place(h, i, -2))
                if h == 0 and not inner(i) and i < PARTS:
                    pool.iota(dist[:, i * PART:(i + 1) * PART], pattern=[[-1, PART]], base=SEQ - P - i * PART,
                              channel_multiplier=1, allow_small_or_imprecise_dtypes=True).then_inc(dist_made, 1)
                    if i:
                        alibi_part(0, i - 1)
                if h == 0 and at(i, ROWS - UNROLL):
                    alibi_part(0, PARTS - 1)
                if 1 <= h < PAIRS and not inner(i) and i < PARTS:
                    alibi_part(h, i)

            def alibi_part(h, i):
                part = dist[:, i * PART:(i + 1) * PART]
                ratio = 2.0 ** (-8.0 / DIFF_HEADS)
                if h == 0:
                    pool.wait_ge(dist_abs, i + 1)
                elif i == 0:
                    pool.wait_ge(alibi_stored, 16 * h)
                pool.tensor_scalar(part, part, -ratio if h == 0 else ratio, 1.0, ALU.mult, ALU.mult).then_inc(alibi_ready, 1)

            for m in range(2):
                own_queries(m, m, 0, m)
            queries_lo(0, 0)
            run(pool, step)

        @block.scalar
        def _(act):
            def split_k(h):
                act.wait_ge(k_loaded, 16 * (h + 1))
                act.activation(k_hi[h % 2][:, :], k_st[:, :], ACT.Copy, scale=EXP_SCALE).then_inc(k_hi_ready, 1)

            def split_v(h, o):
                act.wait_ge(v_loaded, 32 * (h + 1))
                act.activation(v_parts[h % 2][o][:, :, 0, :], v_st[o][:, 0:TILES - o, :], ACT.Copy).then_inc(v_hi_ready, 1)

            def queries_hi(m, b):
                act.wait_ge(q_own_ready, m + 1)
                if not isinstance(m, int) or m >= 2:
                    act.wait_ge(s_ready, m - 1)
                act.activation(q_hi[b][:, :], q_own[b][:, :], ACT.Copy).then_inc(q_hi_ready, 1)

            queries_hi(0, 0)
            split_k(0)
            split_v(0, 0)
            split_v(0, 1)

            def step(n, s, h, i):
                b = s % 2
                if has(n, i, 4):
                    act.wait_ge(pv_done, n - 3)
                    act.wait_ge(recips, n - 3)
                    if inner(i) or n >= 6:
                        act.wait_ge(o_ready, 2 * n - 10)
                    act.activation(o_part[b][:, :], o_ps[:, b, P:2 * P], ACT.Copy, scale=recip[b][:, :]
                                   ).then_inc(o_part_ready, 1)
                if has(n, i, -1):
                    queries_hi(n + 1, 1 - b)
                if has(n, i, 1):
                    act.wait_ge(biased, n)
                    if inner(i) or n >= 3:
                        act.wait_ge(recips, n - 2)
                    act.activation(probs[(s + 3) % UNROLL][:, :], probs[(s + 3) % UNROLL][:, :], ACT.Exp, bias=nmax[1 - b][:, :],
                                   scale=-1.0, accum_out=sums[1 - b][:, :]).then_inc(exped, 1)
                if has(n, i, 2):
                    act.wait_ge(t_ready, n - 1)
                    if inner(i) or n >= 4:
                        act.wait_ge(pv_done, n - 3)
                    act.activation(t_hi[b][:, :], t_ps[:, b, :], ACT.Copy).then_inc(thi_ready, 1)
                if h == 0 and not inner(i) and i < PARTS:
                    part = dist[:, i * PART:(i + 1) * PART]
                    act.wait_ge(dist_made, i + 1)
                    act.activation(part, part, ACT.Abs).then_inc(dist_abs, 1)
                if h < PAIRS - 1:
                    if at(i, ROWS - 4):
                        split_k(h + 1)
                    if at(i, ROWS - 2):
                        split_v(h + 1, 0)
                if 1 <= h < PAIRS and at(i, 1):
                    split_v(h, 1)

            run(act, step)

        @block.vector
        def _(dve):
            def split_k(h):
                dve.wait_ge(k_hi_ready, h + 1)
                dve.scalar_tensor_tensor(out=k_lo[h % 2][:, :], in0=k_st[:, :], scalar=EXP_SCALE,
                                         in1=k_hi[h % 2][:, :].bitcast(F32), op0=ALU.mult, op1=ALU.subtract
                                         ).then_inc(k_lo_ready, 1)

            def split_v(h, o):
                dve.wait_ge(v_hi_ready, 2 * h + o + 1)
                dve.tensor_tensor(v_parts[h % 2][o][:, :, 1, :], v_st[o][:, 0:TILES - o, :],
                                  v_parts[h % 2][o][:, :, 0, :].bitcast(F32), ALU.subtract).then_inc(v_lo_ready, 1)

            split_k(0)
            split_v(0, 0)
            split_v(0, 1)

            def step(n, s, h, i):
                b = s % 2
                if has(n, i, 4):
                    ho, row = place(h, i, 4)
                    dve.wait_ge(o_part_ready, n - 3)
                    if ho >= 2 and at(row, 0):
                        dve.wait_ge(o_stored, 32 * (ho - 1))
                    row = row[0] * UNROLL + row[1] if isinstance(row, tuple) else row
                    for hh in range(2):
                        part = slice(hh * DH, (hh + 1) * DH)
                        dve.scalar_tensor_tensor(
                            out=o_all[ho % 2][part, bass.ds(row, 1), :].rearrange("p r d -> p (r d)"),
                            in0=o_ps[part, b, part], scalar=recip[b][part, :], in1=o_part[b][part, part],
                            op0=ALU.mult, op1=ALU.add).then_inc(o_ready, 1)
                if has(n, i, 0):
                    if at(i, 0):
                        dve.wait_ge(table_loaded, 16 * (h + 1))
                    dve.wait_ge(s_ready, n + 1)
                    if inner(i) or n >= 2:
                        dve.wait_ge(exped, n - 1)
                    if inner(i) or n >= 4:
                        dve.wait_ge(t_ready, n - 3)
                    dve.sem_inc(ticks, 1)
                    first = (KH - 1 - KH // 2 if inner(i) else window(i) - i + KH - 1) * GRID_W
                    dve.tensor_tensor_reduce(
                        probs[s][:, :], s_ps[:, b, :],
                        table[h % 2][:, :, :].rearrange("p r c -> p (r c)")[:, first:first + NA_KEYS],
                        -1.0, 3e38, ALU.add, ALU.min, nmax[b][:, :]).then_inc(biased, 1)
                if has(n, i, 2):
                    dve.wait_ge(exped, n - 1)
                    if inner(i) or n >= 4:
                        dve.wait_ge(o_ready, 2 * n - 6)
                    dve.reciprocal(recip[b][:, :], sums[b][:, :]).then_inc(recips, 1)
                    dve.wait_ge(thi_ready, n - 1)
                    dve.tensor_tensor(t_lo[b][:, :], t_ps[:, b, :], t_hi[b][:, :].bitcast(F32),
                                      ALU.subtract).then_inc(tlo_ready, 1)
                if h < PAIRS - 1:
                    if at(i, ROWS - 4):
                        split_k(h + 1)
                    if at(i, ROWS - 2):
                        split_v(h + 1, 0)
                if 1 <= h < PAIRS and at(i, 1):
                    split_v(h, 1)

            run(dve, step)

        @block.tensor
        def _(pe):
            pe.wait_ge(consts, 2)

            def scores(n, b, h, i):
                pe.wait_ge(q_lo_ready, n + 1)
                pe.wait_ge(k_lo_ready, h + 1)
                if inner(i) or n >= 2:
                    pe.wait_ge(biased, n - 1)
                cols = bass.ds(columns(i, -(KH // 2)) if inner(i) else columns(window(i)), NA_KEYS)
                pe.matmul(s_ps[:, b, :], q_hi[b][:, :], k_hi[h % 2][:, cols], start=True, stop=False)
                pe.matmul(s_ps[:, b, :], q_hi[b][:, :], k_lo[h % 2][:, cols], start=False, stop=False)
                pe.matmul(s_ps[:, b, :], q_lo[b][:, :], k_hi[h % 2][:, cols], start=False, stop=True).then_inc(s_ready, 1)

            def turn(n, s):
                b = s % 2
                pe.wait_ge(exped, n - 1)
                if not isinstance(n, int) or n >= 4:
                    pe.wait_ge(tlo_ready, n - 3)
                for k in range(4):
                    t = pe.transpose(t_ps[:, b, k * P:(k + 1) * P], probs[(s + 2) % UNROLL][:, k * P:(k + 1) * P], ident[:, :])
                t.then_inc(t_ready, 1)

            def values(n, s, h, i):
                c = 1 - s % 2
                hv, row = place(h, i, 3)
                pe.wait_ge(tlo_ready, n - 2)
                pe.wait_ge(v_lo_ready, 2 * hv + 2)
                if inner(i) or n >= 5:
                    pe.wait_ge(o_ready, 2 * n - 8)
                if inner(i):
                    off = row[1] - KH // 2
                    odd, first = off % 2, row[0] * (UNROLL // 2) + (off - off % 2) // 2
                else:
                    w = window(row)
                    odd, first = w % 2, w // 2
                for k in range(4):
                    blk = slice(k * P, (k + 1) * P)
                    pe.matmul(o_ps[:, c, 0:2 * P], t_hi[c][:, blk],
                              v_parts[hv % 2][odd][:, bass.ds(first + k, 1), :, :].rearrange("p r a e -> p (r a e)"),
                              start=(k == 0), stop=False, skip_group_check=True)
                    mm = pe.matmul(o_ps[:, c, 0:P], t_lo[c][:, blk],
                                   v_parts[hv % 2][odd][:, bass.ds(first + k, 1), 0, :].rearrange("p r e -> p (r e)"),
                                   start=False, stop=(k == 3), skip_group_check=True)
                mm.then_inc(pv_done, 1)

            def step(n, s, h, i):
                if has(n, i, 0):
                    scores(n, s % 2, h, i)
                if has(n, i, 2):
                    turn(n, s)
                if has(n, i, 3):
                    values(n, s, h, i)

            run(pe, step)


def bias_tables(nc, na_rpb, rpb_rows, na_bias):
    NR = 2 * KH - 1
    NC = 2 * KW - 1
    NPAD = 2 * GRID_W - 1
    with Parts(nc, "tb") as m:
        pad = m.sb("pad", [NA_HEADS * NR, NPAD])
        mirrored = m.sb("mirrored", [P, PAIRS, NR * GRID_W])
        mirror = m.sb("mirror", [P, P])
        outside = m.sb("outside", [P, GRID_W])
        tab = m.sb("tab", [P, PAIRS, NR, GRID_W])
        tab_ps = m.psum("tab_ps", [P, PAIRS, 2 * BANK])
        pad_zero = m.sem("pad_zero")
        pad_in = m.sem("pad_in")
        pad_out = m.sem("pad_out")
        tab_in = m.sem("tab_in")
        mirror_ready = m.sem("mirror_ready")
        turned_round = m.sem("turned_round")
        tab_ready = m.sem("tab_ready")
        masked = m.sem("masked")
        tab_out = m.sem("tab_out")
        block = m.block()

        @block.gpsimd
        def _(pool):
            pool.memset(pad[:, :], 0.0).then_inc(pad_zero, 1)
            pool.memset(outside[:, :], 0.0).then_inc(masked, 1)
            pool.memset(mirror[:, :], 0.0).then_inc(mirror_ready, 1)
            for hh in range(2):
                pool.wait_ge(mirror_ready, hh + 1)
                pool.affine_select(out=mirror[:, :], in_=mirror[:, :], compare_op=ALU.not_equal, fill=1.0,
                                   base=1 - GRID_W - 2 * hh * GRID_W, pattern=[[1, P]], channel_multiplier=1
                                   ).then_inc(mirror_ready, 1)
            n = 1
            for hh in range(2):
                part = outside[hh * GRID_W:(hh + 1) * GRID_W, :]
                pool.wait_ge(masked, n)
                low = part[:, 0:GRID_W - KW]
                pool.affine_select(out=low, in_=low, compare_op=ALU.is_ge, fill=NEG, base=KW // 2,
                                   pattern=[[1, GRID_W - KW]], channel_multiplier=-1).then_inc(masked, 1)
                pool.wait_ge(masked, n + 1)
                high = part[:, KW:GRID_W]
                pool.affine_select(out=high, in_=high, compare_op=ALU.is_gt, fill=NEG, base=KW // 2 - KW,
                                   pattern=[[-1, GRID_W - KW]], channel_multiplier=1).then_inc(masked, 1)
                n += 2

        @block.tensor
        def _(pe):
            pe.wait_ge(mirror_ready, 3)
            pe.wait_ge(tab_in, 16 * NA_HEADS)
            for a in range(PAIRS):
                for first in range(0, NR * GRID_W, BANK):
                    last = min(first + BANK, NR * GRID_W)
                    mm = pe.matmul(tab_ps[:, a, first:last], mirror[:, :], mirrored[:, a, first:last], start=True, stop=True)
                mm.then_inc(turned_round, 1)

        @block.vector
        def _(dve):
            dve.wait_ge(masked, 5)
            for a in range(PAIRS):
                dve.wait_ge(turned_round, a + 1)
                dve.tensor_tensor(tab[:, a, :, :], tab_ps[:, a, 0:NR * GRID_W].rearrange("p (r c) -> p r c", c=GRID_W),
                                  outside[:, :].unsqueeze(1).to_broadcast([P, NR, GRID_W]), ALU.add).then_inc(tab_ready, 1)

        @block.sync
        def _(sp):
            sp.wait_ge(pad_zero, 1)
            sp.dma_start(pad[:, GRID_W - KW:GRID_W - KW + NC], na_rpb.rearrange("l h r c -> (l h r) c")).then_inc(pad_in, 16)
            sp.wait_ge(pad_in, 16)
            sp.dma_start(rpb_rows, pad[:, :]).then_inc(pad_out, 16)
            sp.wait_ge(pad_out, 16)
            for h in range(NA_HEADS):
                src = bass.AP(rpb_rows.tensor, h * NR * NPAD, [[1, GRID_W], [NPAD, NR], [1, GRID_W]])
                hh = h % 2
                sp.dma_start(mirrored[hh * GRID_W:(hh + 1) * GRID_W, h // 2, :].rearrange("p (r c) -> p r c", c=GRID_W), src
                             ).then_inc(tab_in, 16)
            for a in range(PAIRS):
                sp.wait_ge(tab_ready, a + 1)
                sp.dma_start(na_bias[a], tab[:, a, :, :].rearrange("p r c -> p (r c)")).then_inc(tab_out, 16)
            sp.wait_ge(tab_out, 16 * PAIRS)


def differential(nc, feat_t, v_tok, alibi, lams, o_cat):
    QB = SEQ // P
    STEPS = DIFF_HEADS * QB
    CH = SEQ // BANK
    PCH = CH - 1
    with Parts(nc, "df") as m:
        ident = m.sb("ident", [P, P])
        q_raw = [m.sb(f"q_raw{b}", [P, 2, P]) for b in range(2)]
        k_st = m.sb("k_st", [P, SEQ])
        v_st = m.sb("v_st", [P, TILES, P])
        k_hi = [m.sb(f"k_hi{i}", [P, 2, SEQ], F32R) for i in range(2)]
        k_lo = [m.sb(f"k_lo{i}", [P, 2, SEQ], F32R) for i in range(2)]
        v_parts = [m.sb(f"v_parts{i}", [P, TILES, 2, P], F32R) for i in range(2)]
        q_high = [m.sb(f"q_high{b}", [P, 2, P]) for b in range(2)]
        q_parts = [m.sb(f"q_parts{b}", [P, 2, P], F32R) for b in range(2)]
        bias = [m.sb(f"bias{b}", [P, SEQ]) for b in range(2)]
        probs = [m.sb(f"probs{b}", [P, 2, SEQ]) for b in range(2)]
        amap = [m.sb(f"amap{b}", [P, SEQ]) for b in range(2)]
        t_hi = [m.sb(f"t_hi{g}", [P, BANK], F32R) for g in range(CH)]
        t_lo = [m.sb(f"t_lo{g}", [P, BANK], F32R) for g in range(CH)]
        nmax = [m.sb(f"nmax{b}", [P, 2, CH]) for b in range(2)]
        sums = [m.sb(f"sums{b}", [P, 2]) for b in range(2)]
        recip = [m.sb(f"recip{b}", [P, 2]) for b in range(2)]
        ratio = [m.sb(f"ratio{b}", [P, 1]) for b in range(2)]
        o_part = m.sb("o_part", [P, P])
        o_sb = [m.sb(f"o_sb{b}", [P, P]) for b in range(2)]
        lam_sb = m.sb("lam_sb", [P, 4, DH])
        lam_exp = m.sb("lam_exp", [P, 2])
        lam_dot = m.sb("lam_dot", [P, 2])
        nlam = m.sb("nlam", [P, 1])
        s_ps = m.psum("s_ps", [P, 4, BANK])
        t_ps = m.psum("t_ps", [P, 2, BANK])
        o_ps = m.psum("o_ps", [P, 2, BANK])

        consts = m.sem("consts")
        lam_loaded = m.sem("lam_loaded")
        lam_steps = m.sem("lam_steps")
        q_loaded = [m.sem(f"q_loaded{b}") for b in range(2)]
        k_loaded = m.sem("k_loaded")
        v_loaded = m.sem("v_loaded")
        k_hi_ready = m.sem("k_hi_ready")
        k_lo_ready = m.sem("k_lo_ready")
        v_hi_ready = m.sem("v_hi_ready")
        v_lo_ready = m.sem("v_lo_ready")
        q_hi_ready = m.sem("q_hi_ready")
        q_ready = m.sem("q_ready")
        q_zeros = m.sem("q_zeros")
        bias_loaded = [m.sem(f"bias_loaded{b}") for b in range(2)]
        s_ready = m.sem("s_ready")
        biased = m.sem("biased")
        exped = m.sem("exped")
        recips = m.sem("recips")
        ratios = m.sem("ratios")
        p1_scaled = m.sem("p1_scaled")
        a_ready = m.sem("a_ready")
        a0_ready = m.sem("a0_ready")
        t_ready = m.sem("t_ready")
        thi_ready = m.sem("thi_ready")
        tlo_ready = m.sem("tlo_ready")
        pv_groups = m.sem("pv_groups")
        o_part_ready = m.sem("o_part_ready")
        o_ready = m.sem("o_ready")
        o_stored = [m.sem(f"o_stored{b}") for b in range(2)]
        ticks = m.sem("ticks")
        k_first_loaded = m.sem("k_first_loaded")
        block = m.block()

        k_first = v_st[:, :, :].rearrange("p t e -> p (t e)")
        q_dram = feat_t[1, 0:BANK, :].rearrange("(h c d) t -> h d c t", c=2, d=DH)
        k_dram = feat_t[1, BANK:2 * BANK, :].rearrange("(h c d) t -> h c d t", c=2, d=DH)
        v_dram = v_tok[1].rearrange("(j p) (h e) -> h p j e", p=P, e=P)

        def run(eng, fn):
            for h in range(DIFF_HEADS):
                for i in range(4):
                    fn(h * QB + i, i % 2, h, i)
                last = h == DIFF_HEADS - 1
                with eng.Fori(2, QB // 2 - last) as j:
                    for b in range(2):
                        fn(j * 2 + (h * QB + b), b, h, j * 2 + b)
                if last:
                    for i in range(QB - 2, QB):
                        fn(h * QB + i, i % 2, h, i)
            for i in range(4):
                fn(STEPS + i, i % 2, DIFF_HEADS, i)

        def inner(i):
            return not isinstance(i, int)

        def at(i, k):
            return isinstance(i, int) and i == k

        def has(n, i, lag):
            return inner(i) or 0 <= n - lag < STEPS

        def turn_of(n, b):
            return n * 8 + (16 - 8 * b)

        def head_of(n, h, i, lag):
            return h if inner(i) or i >= lag else h - 1

        @block.sync
        def _(sp):
            for i, lam in enumerate(lams):
                sp.dma_start(lam_sb[:, i, :], lam.partition_broadcast(P).rearrange("p l n -> p (l n)")
                             ).then_inc(lam_loaded, 16)

            def load_k(h, c):
                for half in range(2):
                    sp.dma_start(k_st[half * DH:(half + 1) * DH, :], k_dram[h, c]).then_inc(k_loaded, 16)

            def load_v(h):
                sp.dma_start(v_st[:, :, :], v_dram[h]).then_inc(v_loaded, 16)

            load_k(0, 0)
            for half in range(2):
                sp.dma_start(k_first[half * DH:(half + 1) * DH, :], k_dram[0, 1]).then_inc(k_first_loaded, 16)

            def step(n, b, h, i):
                if h < DIFF_HEADS:
                    if inner(i) or n >= 2:
                        sp.wait_ge(q_ready, n - 1)
                        sp.sem_inc(ticks, 1)
                    for half in range(2):
                        sp.dma_start(q_raw[b][half * DH:(half + 1) * DH, :, :], q_dram[h, :, :, bass.ds(i * P, P)]
                                     ).then_inc(q_loaded[b], 16)
                    if inner(i) or n >= 2:
                        sp.wait_ge(biased, n * 8 - 8)
                        sp.sem_inc(ticks, 1)
                    start = (SEQ - P) - i * P
                    sp.dma_start(bias[b][:, :], alibi[h, :, bass.ds(start, SEQ)]).then_inc(bias_loaded[b], 16)
                    if numbered(n, 0):
                        sp.wait_ge(k_lo_ready, 2)
                        load_v(0)
                    if at(i, 0) and h < DIFF_HEADS - 1:
                        sp.wait_ge(k_lo_ready, 2 * h + 2)
                        load_k(h + 1, 0)
                    if at(i, 2) and h < DIFF_HEADS - 1:
                        sp.wait_ge(v_lo_ready, h + 1)
                        load_v(h + 1)
                    if at(i, 3) and h < DIFF_HEADS - 1:
                        sp.wait_ge(k_lo_ready, 2 * h + 3)
                        load_k(h + 1, 1)
            run(sp, step)
            for b in range(2):
                sp.wait_ge(o_stored[b], 16 * STEPS // 2 + 16 * b)

        @block.gpsimd
        def _(pool):
            identity_steps(pool, ident, consts)

            pool.memset(q_high[0][0:DH, :, :], 0.0).then_inc(q_zeros, 1)
            pool.memset(q_high[1][0:DH, :, :], 0.0).then_inc(q_zeros, 1)
            pool.wait_ge(q_zeros, 2)

            def queries(m, b):
                pool.wait_ge(q_hi_ready, m + 1)
                if not isinstance(m, int) or m >= 2:
                    pool.wait_ge(s_ready, m * 8 - 8)
                pool.tensor_tensor(q_parts[b][:, :, :], q_raw[b][:, :, :], q_high[b][:, :, :],
                                   ALU.subtract).then_inc(q_ready, 1)

            def step(n, b, h, i):
                if has(n, i, -1):
                    queries(n + 1, 1 - b)
                if has(n, i, 1):
                    pool.wait_ge(ratios, n)
                    pool.sem_inc(ticks, 1)
                for g in range(1, CH):
                    if has(n, i, 1):
                        cols = slice(g * BANK, (g + 1) * BANK)
                        pool.tensor_scalar(probs[1 - b][:, 1, cols], probs[1 - b][:, 1, cols], ratio[1 - b][:, 0:1], 1.0,
                                           ALU.mult, ALU.mult).then_inc(p1_scaled, 1)
                        if inner(i) or n >= 3:
                            pool.wait_ge(t_ready, n * CH + (g + 1 - 3 * CH))
                        pool.wait_ge(p1_scaled, n * PCH + (g - PCH))
                        pool.tensor_tensor(amap[1 - b][:, cols], probs[1 - b][:, 0, cols], probs[1 - b][:, 1, cols],
                                           ALU.add).then_inc(a_ready, 1)

            queries(0, 0)
            run(pool, step)

        @block.scalar
        def _(act):
            def split_k(h, c):
                n = 2 * h + c
                if n == 1:
                    act.wait_ge(k_first_loaded, 32)
                else:
                    act.wait_ge(k_loaded, 32 * max(n, 1))
                act.activation(k_hi[h % 2][:, c, :], k_first if n == 1 else k_st[:, :], ACT.Copy, scale=EXP_SCALE
                               ).then_inc(k_hi_ready, 1)

            act.wait_ge(lam_steps, 2)
            act.activation(lam_exp[:, :], lam_dot[:, :], ACT.Exp).then_inc(lam_steps, 1)
            split_k(0, 0)
            split_k(0, 1)

            def queries_high(m, b):
                act.wait_ge(q_loaded[b], 2 * turn_of(m, b))
                if not isinstance(m, int) or m >= 2:
                    act.wait_ge(q_ready, m - 1)
                act.activation(q_high[b][DH:P, :, :].bitcast(F32R), q_raw[b][DH:P, :, :], ACT.Copy).then_inc(q_hi_ready, 1)

            def exponentials(n, b, c):
                act.wait_ge(biased, n * 8 + (c - 1))
                if c == 0 and not (isinstance(n, int) and n < 3):
                    act.wait_ge(ratios, n - 2)
                act.activation(probs[1 - b][:, c, :], probs[1 - b][:, c, :], ACT.Exp, bias=nmax[1 - b][:, c, CH - 1:CH],
                               scale=-1.0, accum_out=sums[1 - b][:, c:c + 1]).then_inc(exped, 1)

            def turned_high(n, g):
                act.wait_ge(t_ready, n * CH + (g + 1 - 2 * CH))
                if not (isinstance(n, int) and n < 3):
                    act.wait_ge(pv_groups, n * CH + (g + 1 - 3 * CH))
                act.activation(t_hi[g][:, :], t_ps[:, g % 2, :], ACT.Copy).then_inc(thi_ready, 1)

            queries_high(0, 0)

            def step(n, b, h, i):
                if has(n, i, -1):
                    queries_high(n + 1, 1 - b)
                if has(n, i, 1):
                    exponentials(n, b, 0)
                if has(n, i, 2):
                    turned_high(n, 0)
                if has(n, i, 1):
                    exponentials(n, b, 1)
                if has(n, i, 2):
                    turned_high(n, 1)
                if has(n, i, 3):
                    act.wait_ge(pv_groups, n * CH - 2 * CH)
                    if inner(i) or n >= 4:
                        act.wait_ge(o_ready, n - 3)
                    act.activation(o_part[:, :], o_ps[:, 1 - b, P:2 * P], ACT.Copy, scale=recip[1 - b][:, 0:1]
                                   ).then_inc(o_part_ready, 1)
                if has(n, i, 4):
                    act.wait_ge(o_ready, n - 3)
                    act.sem_inc(ticks, 1)
                    if inner(i):
                        rows, hh = bass.ds((i - 4) * P, P), h
                    else:
                        hh, ii = (n - 4) // QB, (n - 4) % QB
                        rows = bass.ds(ii * P, P)
                    act.dma_start(o_cat[rows, NA_HEADS * DH + hh * P:NA_HEADS * DH + (hh + 1) * P], o_sb[b][:, :]
                                 ).then_inc(o_stored[b], 16)
                if has(n, i, 2):
                    turned_high(n, 2)
                    turned_high(n, 3)
                if h < DIFF_HEADS - 1 and (at(i, 1) or at(i, 3)):
                    if h >= 1 and at(i, 1):
                        act.wait_ge(s_ready, h * QB * 8)
                    split_k(h + 1, i // 2)
                if h < DIFF_HEADS and at(i, 0):
                    act.wait_ge(v_loaded, 16 * (h + 1))
                    if h >= 2:
                        act.wait_ge(pv_groups, (h - 1) * QB * CH)
                    act.activation(v_parts[h % 2][:, :, 0, :], v_st[:, :, :], ACT.Copy).then_inc(v_hi_ready, 1)

            run(act, step)

        @block.vector
        def _(dve):
            def split_k(h, c):
                n = 2 * h + c
                dve.wait_ge(k_hi_ready, n + 1)
                dve.scalar_tensor_tensor(out=k_lo[h % 2][:, c, :], in0=k_first if n == 1 else k_st[:, :], scalar=EXP_SCALE,
                                         in1=k_hi[h % 2][:, c, :].bitcast(F32), op0=ALU.mult, op1=ALU.subtract
                                         ).then_inc(k_lo_ready, 1)

            credit(dve, o_stored[1], 16)
            dve.wait_ge(lam_loaded, 16 * 4)
            dve.tensor_tensor(lam_sb[:, 0::2, :], lam_sb[:, 0::2, :], lam_sb[:, 1::2, :], ALU.mult).then_inc(lam_steps, 1)
            dve.wait_ge(lam_steps, 1)
            dve.tensor_reduce(lam_dot[:, :], lam_sb[:, 0::2, :], AX.X, ALU.add).then_inc(lam_steps, 1)
            dve.wait_ge(lam_steps, 3)
            dve.scalar_tensor_tensor(out=nlam[:, :], in0=lam_exp[:, 1:2], scalar=-LAM_INIT, in1=lam_exp[:, 0:1],
                                     op0=ALU.add, op1=ALU.subtract).then_inc(lam_steps, 1)
            split_k(0, 0)
            split_k(0, 1)

            def bias_scores(n, b, g):
                for c in range(2):
                    u = n * 8 + (2 * g + c)
                    if g == 0 and c == 0:
                        dve.wait_ge(bias_loaded[b], turn_of(n, b))
                    dve.wait_ge(s_ready, u + 1)
                    if g >= 1:
                        dve.wait_ge(biased, u - 1)
                    dve.sem_inc(ticks, 1)
                    dve.tensor_tensor_reduce(
                        probs[b][:, c, g * BANK:(g + 1) * BANK], s_ps[:, 2 * (g % 2) + c, :],
                        bias[b][:, g * BANK:(g + 1) * BANK], -1.0,
                        3e38 if g == 0 else nmax[b][:, c, g - 1:g], ALU.add, ALU.min, nmax[b][:, c, g:g + 1]
                    ).then_inc(biased, 1)

            def step(n, b, h, i):
                for g in range(CH):
                    if has(n, i, 0):
                        if inner(i) or n >= 2:
                            if g:
                                dve.wait_ge(a_ready, n * PCH + (g - 2 * PCH))
                            else:
                                dve.wait_ge(a0_ready, n - 1)
                                dve.wait_ge(exped, n * 2 - 2)
                        bias_scores(n, b, g)
                    if has(n, i, 3) and g == 2:
                        dve.wait_ge(o_part_ready, n - 2)
                        if inner(i) or n >= 5:
                            dve.wait_ge(o_stored[1 - b], o_turn(n, b))
                        dve.scalar_tensor_tensor(out=o_sb[1 - b][:, :], in0=o_ps[:, 1 - b, 0:P], scalar=recip[1 - b][:, 0:1],
                                                 in1=o_part[:, :], op0=ALU.mult, op1=ALU.add).then_inc(o_ready, 1)
                    if has(n, i, 1) and g == 3:
                        dve.wait_ge(exped, n * 2)
                        if inner(i) or n >= 3:
                            dve.wait_ge(o_ready, n - 2)
                            dve.wait_ge(a_ready, n * PCH - 2 * PCH)
                            dve.wait_ge(a0_ready, n - 2)
                        dve.reciprocal(recip[1 - b][:, :], sums[1 - b][:, :]).then_inc(recips, 1)
                        dve.wait_ge(recips, n)
                        dve.tensor_scalar(ratio[1 - b][:, :], recip[1 - b][:, 1:2], sums[1 - b][:, 0:1], nlam[:, 0:1],
                                          ALU.mult, ALU.mult).then_inc(ratios, 1)
                        dve.wait_ge(ratios, n)
                        if inner(i) or n >= 3:
                            dve.wait_ge(t_ready, n * CH + (1 - 3 * CH))
                        dve.scalar_tensor_tensor(out=amap[1 - b][:, 0:BANK], in0=probs[1 - b][:, 1, 0:BANK],
                                                 scalar=ratio[1 - b][:, 0:1], in1=probs[1 - b][:, 0, 0:BANK],
                                                 op0=ALU.mult, op1=ALU.add).then_inc(a0_ready, 1)
                    if has(n, i, 2):
                        dve.wait_ge(thi_ready, n * CH + (g + 1 - 2 * CH))
                        dve.tensor_tensor(t_lo[g][:, :], t_ps[:, g % 2, :], t_hi[g][:, :].bitcast(F32),
                                          ALU.subtract).then_inc(tlo_ready, 1)
                if h < DIFF_HEADS and at(i, 0):
                    dve.wait_ge(v_hi_ready, h + 1)
                    dve.tensor_tensor(v_parts[h % 2][:, :, 1, :], v_st[:, :, :],
                                      v_parts[h % 2][:, :, 0, :].bitcast(F32), ALU.subtract).then_inc(v_lo_ready, 1)
                if h + 1 < DIFF_HEADS and (at(i, 1) or at(i, 3)):
                    split_k(h + 1, i // 2)

            def o_turn(n, b):
                if isinstance(n, int):
                    return 16 * ((n - 5) // 2 + 1 + (1 - b))
                return n * 8 + (-24 if b else -16)

            dve.wait_ge(lam_steps, 4)
            run(dve, step)

        @block.tensor
        def _(pe):
            pe.wait_ge(consts, 2)

            def scores(n, b, h, g):
                for c in range(2):
                    u = n * 8 + (2 * g + c)
                    if g == 0 and c == 0:
                        pe.wait_ge(q_ready, n + 1)
                        pe.wait_ge(k_lo_ready, 2 * h + 2)
                    if not isinstance(n, int) or u >= 4:
                        pe.wait_ge(biased, u - 3)
                    rows = slice(g * BANK, (g + 1) * BANK)
                    pe.matmul(s_ps[:, 2 * (g % 2) + c, :], q_parts[b][:, c, :], k_hi[h % 2][:, c, rows],
                              start=True, stop=False)
                    pe.matmul(s_ps[:, 2 * (g % 2) + c, :], q_parts[b][:, c, :], k_lo[h % 2][:, c, rows],
                              start=False, stop=True).then_inc(s_ready, 1)

            def turn(n, b, g):
                if g:
                    pe.wait_ge(a_ready, n * PCH + (g - 2 * PCH))
                else:
                    pe.wait_ge(a0_ready, n - 1)
                if not isinstance(n, int) or n >= 3 or g >= 2:
                    pe.wait_ge(tlo_ready, n * CH + (g - 1 - 2 * CH))
                for j in range(4):
                    t = pe.transpose(t_ps[:, g % 2, j * P:(j + 1) * P], amap[b][:, (4 * g + j) * P:(4 * g + j + 1) * P],
                                     ident[:, :])
                t.then_inc(t_ready, 1)

            def values(n, b, m_lag, hv, g):
                c = (b + m_lag) % 2
                pe.wait_ge(tlo_ready, n * CH + (g + 1 - m_lag * CH))
                if g == 0:
                    pe.wait_ge(v_lo_ready, hv + 1)
                    if not isinstance(n, int) or n >= 4:
                        pe.wait_ge(o_ready, n - 3)
                for j in range(4):
                    k = 4 * g + j
                    blk = slice(j * P, (j + 1) * P)
                    pe.matmul(o_ps[:, c, 0:2 * P], t_hi[g][:, blk], v_parts[hv % 2][:, k, :, :],
                              start=(k == 0), stop=False, skip_group_check=True)
                    mm = pe.matmul(o_ps[:, c, 0:P], t_lo[g][:, blk], v_parts[hv % 2][:, k, 0, :],
                                   start=False, stop=(k == TILES - 1), skip_group_check=True)
                mm.then_inc(pv_groups, 1)

            def step(n, b, h, i):
                for g in range(CH):
                    if has(n, i, 0):
                        scores(n, b, h, g)
                    if has(n, i, 2):
                        turn(n, b, g)
                    if g == 0 and has(n, i, 3):
                        values(n, b, 3, head_of(n, h, i, 3), CH - 1)
                    if g >= 1 and has(n, i, 2):
                        values(n, b, 2, head_of(n, h, i, 2), g - 1)

            run(pe, step)


def mix_out(nc, x, o_cat, g_na_out, g_diff_out, w_out, g_moe, w_router, h_res, hn_moe, logits):
    EARLY = 4
    WS = 4
    NG = D // DH
    NA_W = NA_HEADS * DH
    with Parts(nc, "mo") as m:
        ident = m.sb("ident", [P, P])
        w_st = [m.sb(f"w_st{r}", [P, D]) for r in range(WS)]
        w_hi = m.sb("w_hi", [P, KB, D], F32R)
        w_lo = m.sb("w_lo", [P, KB, D], F32R)
        w_r = m.sb("w_r", [P, KB, E])
        g_heads = m.sb("g_heads", [P, D])
        g_next = m.sb("g_next", [P, D])
        mhalf = m.sb("mhalf", [P, NG])
        o_in = [m.sb(f"o_in{b}", [P, D]) for b in range(2)]
        x_in = [m.sb(f"x_in{b}", [P, D]) for b in range(2)]
        o_sq = m.sb("o_sq", [P, D])
        o_ss = m.sb("o_ss", [P, NG])
        o_pair = m.sb("o_pair", [P, NG // 4])
        o_ms = m.sb("o_ms", [P, NG])
        o_rs = m.sb("o_rs", [P, NG])
        ot_hi = [m.sb(f"ot_hi{b}", [P, KB, P], F32R) for b in range(2)]
        ot_lo = [m.sb(f"ot_lo{b}", [P, KB, P], F32R) for b in range(2)]
        h_sb = [m.sb(f"h_sb{b}", [P, D]) for b in range(2)]
        h_sq = m.sb("h_sq", [P, D])
        h_ss = m.sb("h_ss", [P, 1])
        h_ms = m.sb("h_ms", [P, 1])
        h_rs = m.sb("h_rs", [P, 1])
        hn_sb = [m.sb(f"hn_sb{b}", [P, D]) for b in range(2)]
        hnt = [m.sb(f"hnt{b}", [P, KB, P]) for b in range(2)]
        t_ps = m.psum("t_ps", [P, 2, BANK])
        out_ps = m.psum("out_ps", [P, 2, D])
        l_ps = m.psum("l_ps", [P, 2, BANK])

        sem = m.sem
        consts, mhalf_ready = sem("consts"), sem("mhalf_ready")
        gains_loaded, gains_ready = sem("gains_loaded"), sem("gains_ready")
        w_loaded = [sem(f"w_loaded{r}") for r in range(WS)]
        whi_ready, wlo_ready, wr_loaded = sem("whi_ready"), sem("wlo_ready"), sem("wr_loaded")
        o_loaded = [sem(f"o_loaded{b}") for b in range(2)]
        x_loaded = [sem(f"x_loaded{b}") for b in range(2)]
        o_squared, o_summed, o_steps, o_means, o_rsqrt = (sem(n) for n in ("o_squared", "o_summed", "o_steps", "o_means", "o_rsqrt"))
        o_scaled, o_normed, turned = sem("o_scaled"), sem("o_normed"), sem("turned")
        othi_ready, otlo_ready, out_ready = sem("othi_ready"), sem("otlo_ready"), sem("out_ready")
        h_ready, h_squared, h_means, h_rsqrt, hn_ready = (sem(n) for n in ("h_ready", "h_squared", "h_means", "h_rsqrt", "hn_ready"))
        hnt_ready, l_ready, l_copied = sem("hnt_ready"), sem("l_ready"), sem("l_copied")
        h_stored = [sem(f"h_stored{b}") for b in range(2)]
        hn_stored = [sem(f"hn_stored{b}") for b in range(2)]
        block = m.block()

        def run(eng, fn, start=0):
            for n in range(start, 4):
                fn(n, n % 2, n)
            with eng.Fori(2, TILES // 2 - 1) as j:
                for b in range(2):
                    fn(j * 2 + b, b, None)
            for n in range(TILES - 2, TILES + 4):
                fn(n, n % 2, n)

        def has(i, lag):
            return i is None or 0 <= i - lag < TILES

        def turns(n, b, lag=0):
            return n * 8 + (16 - 8 * ((b - lag) % 2) - 8 * lag)

        def turned_o(n, g):
            return 4 * n + (g + 1 - 6) if not isinstance(n, int) or n >= 3 else 2 * n + g + 1

        def turned_hn(n, g):
            return 4 * n + (g + 3 - 6) if not isinstance(n, int) or n < TILES else 2 * n + (2 * TILES - 6) + g + 1

        @block.sync
        def _(sp):
            sp.dma_start(g_heads[:, 0:NA_W], g_na_out.rearrange("l h d -> l (h d)").partition_broadcast(P).rearrange(
                "p l n -> p (l n)")).then_inc(gains_loaded, 16)
            for h in range(DIFF_HEADS):
                sp.dma_start(g_heads[:, NA_W + h * P:NA_W + (h + 1) * P], g_diff_out.partition_broadcast(P).rearrange(
                    "p l n -> p (l n)")).then_inc(gains_loaded, 16)
            sp.dma_start(g_next[:, :], g_moe.partition_broadcast(P).rearrange("p l n -> p (l n)")).then_inc(gains_loaded, 16)
            for b in range(2):
                sp.dma_start(o_in[b][:, :], o_cat[b * P:(b + 1) * P, :]).then_inc(o_loaded[b], 16)
            for k in range(KB):
                if k >= WS:
                    sp.wait_ge(wlo_ready, k - WS + 1)
                sp.dma_start(w_st[k % WS][:, :], w_out[0, k * P:(k + 1) * P, :]).then_inc(w_loaded[k % WS], 16)
            sp.dma_start(w_r[:, :, :], w_router.rearrange("l (k p) e -> (l p) k e", p=P)).then_inc(wr_loaded, 16)

            def step(n, b, i):
                if has(i, -1) and (i is None or i >= 1):
                    sp.wait_ge(turned, turned_o(n - 1, 1))
                    sp.dma_start(o_in[1 - b][:, :], o_cat[bass.ds((n + 1) * P, P), :]).then_inc(o_loaded[1 - b], 16)
                if has(i, 0):
                    if i is None or i >= 2:
                        sp.wait_ge(h_ready, n - 1)
                    sp.dma_start(x_in[b][:, :], x[0, bass.ds(n * P, P), :]).then_inc(x_loaded[b], 16)
                if has(i, 3):
                    c = 1 - b
                    sp.wait_ge(hn_ready, n - 2)
                    sp.dma_start(h_res[bass.ds((n - 3) * P, P), :], h_sb[c][:, :]).then_inc(h_stored[c], 16)
                    sp.dma_start(hn_moe[bass.ds((n - 3) * P, P), :], hn_sb[c][:, :]).then_inc(hn_stored[c], 16)

            run(sp, step)
            for b in range(2):
                sp.wait_ge(h_stored[b], 8 * TILES)
                sp.wait_ge(hn_stored[b], 8 * TILES)

        @block.gpsimd
        def _(pool):
            identity_steps(pool, ident, consts)
            pool.memset(mhalf[:, :], -0.5).then_inc(mhalf_ready, 1)
            pool.wait_ge(mhalf_ready, 1)

            def norm_o(n):
                pool.wait_ge(o_means, n + 1)
                pool.tensor_tensor(o_rs[:, :], o_ms[:, :], mhalf[:, :], ALU.pow).then_inc(o_rsqrt, 1)

            def step(n, b, i):
                if i is None or i < TILES - 1:
                    norm_o(n + 1)
                if has(i, 2):
                    pool.wait_ge(h_means, n - 1)
                    pool.tensor_tensor(h_rs[:, :], h_ms[:, :], mhalf[:, 0:1], ALU.pow).then_inc(h_rsqrt, 1)

            norm_o(0)
            run(pool, step)

        @block.scalar
        def _(act):
            def square_o(n, b):
                act.wait_ge(o_loaded[b], turns(n, b))
                if not isinstance(n, int) or n >= 1:
                    act.wait_ge(o_summed, n)
                act.activation(o_sq[:, :], o_in[b][:, :], ACT.Square).then_inc(o_squared, 1)

            square_o(0, 0)
            def split_w(k):
                act.wait_ge(w_loaded[k % WS], 16 * (k // WS + 1))
                act.activation(w_hi[:, k, :], w_st[k % WS][:, :], ACT.Copy).then_inc(whi_ready, 1)

            def step(n, b, i):
                if has(i, 0):
                    for g in range(2):
                        act.wait_ge(turned, turned_o(n, g))
                        if g == 0 and (i is None or i >= 2):
                            act.wait_ge(out_ready, n - 1)
                        act.activation(ot_hi[b][:, 4 * g:4 * g + 4, :], t_ps[:, g, :].rearrange("p (k t) -> p k t", t=P),
                                       ACT.Copy).then_inc(othi_ready, 1)
                if has(i, 3):
                    c = 1 - b
                    for g in range(2):
                        act.wait_ge(turned, turned_hn(n, g))
                        if g == 0 and (i is None or i >= 5):
                            act.wait_ge(l_ready, n - 3)
                        act.activation(hnt[c][:, 4 * g:4 * g + 4, :], t_ps[:, g, :].rearrange("p (k t) -> p k t", t=P),
                                       ACT.Copy).then_inc(hnt_ready, 1)
                if i is None or i < TILES - 1:
                    square_o(n + 1, 1 - b)
                if has(i, 2):
                    act.wait_ge(h_ready, n - 1)
                    if i is None or i >= 3:
                        act.wait_ge(h_means, n - 2)
                        act.wait_ge(h_squared, n - 2)
                    act.activation(h_sq[:, :], h_sb[b][:, :], ACT.Square, accum_out=h_ss[:, :]).then_inc(h_squared, 1)

            for k in range(KB):
                if k == EARLY:
                    step(0, 0, 0)
                split_w(k)
            run(act, step, 1)

        @block.vector
        def _(dve):
            credit(dve, l_copied, 1)
            dve.wait_ge(gains_loaded, 16 * (2 + DIFF_HEADS))
            dve.tensor_scalar(g_heads[:, NA_W:D], g_heads[:, NA_W:D], 1.0 - LAM_INIT, None, ALU.mult).then_inc(gains_ready, 1)

            def norm_o(n, b):
                dve.wait_ge(o_squared, n + 1)
                if not isinstance(n, int) or n >= 1:
                    dve.wait_ge(o_means, n)
                dve.tensor_reduce(o_ss[:, :], o_sq[:, :].rearrange("p (g d) -> p g d", d=DH), AX.X, ALU.add
                                  ).then_inc(o_summed, 1)
                dve.wait_ge(o_summed, n + 1)
                dve.tensor_tensor(o_pair[:, :], o_ss[:, NG // 2::2], o_ss[:, NG // 2 + 1::2], ALU.add).then_inc(o_steps, 1)
                if not isinstance(n, int) or n >= 1:
                    dve.wait_ge(o_rsqrt, n)
                dve.tensor_scalar(o_ms[:, 0:NG // 2], o_ss[:, 0:NG // 2], 1.0 / DH, EPS, ALU.mult, ALU.add).then_inc(o_steps, 1)
                dve.wait_ge(o_steps, 2 * n + 2)
                dve.tensor_scalar(o_ms[:, NG // 2:NG].rearrange("p (h a) -> p h a", a=2),
                                  o_pair[:, :].unsqueeze(2).to_broadcast([P, NG // 4, 2]), 0.5 / DH, EPS, ALU.mult, ALU.add
                                  ).then_inc(o_means, 1)
                dve.wait_ge(o_rsqrt, n + 1)
                dve.tensor_tensor(o_in[b][:, :].rearrange("p (g d) -> p g d", d=DH),
                                  o_in[b][:, :].rearrange("p (g d) -> p g d", d=DH),
                                  o_rs[:, :].unsqueeze(2).to_broadcast([P, NG, DH]), ALU.mult).then_inc(o_scaled, 1)
                dve.wait_ge(o_scaled, n + 1)
                dve.tensor_tensor(o_in[b][:, :], o_in[b][:, :], g_heads[:, :], ALU.mult).then_inc(o_normed, 1)

            dve.wait_ge(gains_ready, 1)
            norm_o(0, 0)
            def split_w(k):
                dve.wait_ge(whi_ready, k + 1)
                dve.tensor_tensor(w_lo[:, k, :], w_st[k % WS][:, :], w_hi[:, k, :].bitcast(F32), ALU.subtract
                                  ).then_inc(wlo_ready, 1)

            def step(n, b, i):
                if has(i, 0):
                    for g in range(2):
                        dve.wait_ge(othi_ready, 2 * n + (g + 1))
                        dve.tensor_tensor(ot_lo[b][:, 4 * g:4 * g + 4, :], t_ps[:, g, :].rearrange("p (k t) -> p k t", t=P),
                                          ot_hi[b][:, 4 * g:4 * g + 4, :].bitcast(F32), ALU.subtract).then_inc(otlo_ready, 1)
                if has(i, 2):
                    dve.wait_ge(out_ready, n - 1)
                    dve.wait_ge(x_loaded[b], turns(n, b, 2))
                    if i is None or i >= 4:
                        dve.wait_ge(h_stored[b], turns(n, b, 4))
                        dve.wait_ge(hn_stored[b], turns(n, b, 4))
                    dve.tensor_tensor(h_sb[b][:, :], out_ps[:, b, :], x_in[b][:, :], ALU.add).then_inc(h_ready, 1)
                if i is None or i < TILES - 1:
                    norm_o(n + 1, 1 - b)
                if has(i, 2):
                    dve.wait_ge(h_squared, n - 1)
                    if i is None or i >= 3:
                        dve.wait_ge(h_rsqrt, n - 2)
                    dve.tensor_scalar(h_ms[:, :], h_ss[:, :], 1.0 / D, EPS, ALU.mult, ALU.add).then_inc(h_means, 1)
                    dve.wait_ge(h_rsqrt, n - 1)
                    if i is None or i >= 4:
                        dve.wait_ge(turned, turned_hn(n - 1, 1))
                    dve.scalar_tensor_tensor(out=hn_sb[b][:, :], in0=h_sb[b][:, :], scalar=h_rs[:, 0:1], in1=g_next[:, :],
                                             op0=ALU.mult, op1=ALU.mult).then_inc(hn_ready, 1)
                if has(i, 4):
                    dve.wait_ge(l_ready, n - 2)
                    dve.tensor_copy(logits[:, bass.ds(n - 4, 1), :].rearrange("p a e -> p (a e)"), l_ps[:, b, 0:E]
                                    ).then_inc(l_copied, 1)

            for k in range(KB):
                if k == EARLY:
                    step(0, 0, 0)
                split_w(k)
            run(dve, step, 1)
            dve.wait_ge(l_copied, TILES + 1)

        @block.tensor
        def _(pe):
            credit(pe, l_ready, 1)
            pe.wait_ge(consts, 2)

            def products(n, b, i):
                c = 1 - b
                pe.wait_ge(otlo_ready, 2 * n)
                if i is not None and i == 1:
                    pe.wait_ge(wlo_ready, KB)
                if i is None or i >= 3:
                    pe.wait_ge(h_ready, n - 2)
                for half in range(2):
                    cols = slice(half * BANK, (half + 1) * BANK)
                    for k in range(KB):
                        pe.matmul(out_ps[:, c, cols], ot_hi[c][:, k, :], w_hi[:, k, cols], start=(k == 0), stop=False)
                        pe.matmul(out_ps[:, c, cols], ot_hi[c][:, k, :], w_lo[:, k, cols], start=False, stop=False)
                        mm = pe.matmul(out_ps[:, c, cols], ot_lo[c][:, k, :], w_hi[:, k, cols], start=False,
                                       stop=(k == KB - 1))
                mm.then_inc(out_ready, 1)

            def step(n, b, i):
                if has(i, 0):
                    pe.wait_ge(o_normed, n + 1)
                    for g in range(2):
                        if g == 0 and (i is None or i >= 4):
                            pe.wait_ge(hnt_ready, 2 * n - 6)
                        elif g == 0 and i >= 1:
                            pe.wait_ge(otlo_ready, 2 * n)
                        for k in range(4 * g, 4 * g + 4):
                            t = pe.transpose(t_ps[:, g, (k % 4) * P:(k % 4 + 1) * P], o_in[b][:, k * P:(k + 1) * P], ident[:, :])
                        t.then_inc(turned, 1)
                if has(i, 3):
                    c = 1 - b
                    pe.wait_ge(hn_ready, n - 2)
                    for g in range(2):
                        if has(i, 0):
                            pe.wait_ge(otlo_ready, 2 * n + (g + 1))
                        else:
                            pe.wait_ge(hnt_ready, 2 * n - 6)
                            pe.wait_ge(otlo_ready, 2 * TILES)
                        for k in range(4 * g, 4 * g + 4):
                            t = pe.transpose(t_ps[:, g, (k % 4) * P:(k % 4 + 1) * P], hn_sb[c][:, k * P:(k + 1) * P], ident[:, :])
                        t.then_inc(turned, 1)
                if has(i, 1):
                    products(n, b, i)
                if has(i, 3):
                    c = 1 - b
                    pe.wait_ge(hnt_ready, 2 * n - 4)
                    if i is not None and i == 3:
                        pe.wait_ge(wr_loaded, 16)
                    if i is None or i >= 5:
                        pe.wait_ge(l_copied, n - 3)
                    for k in range(KB):
                        mm = pe.matmul(l_ps[:, c, 0:E], hnt[c][:, k, :], w_r[:, k, :], start=(k == 0), stop=(k == KB - 1))
                    mm.then_inc(l_ready, 1)

            run(pe, step)


def route(nc, logits, slot_token, slot_gate):
    TE = TILES * E
    BITS = 30
    HALVES = CAP // P
    NPAY = 6
    STEP = 2
    TRIES = 2 ** STEP - 1
    BY_POOL = [t for t in range(TILES) if t % 5 == 2]
    BY_DVE = [t for t in range(TILES) if t not in BY_POOL]
    RING_POOL, RING_DVE = len(BY_POOL), len(BY_DVE)
    with Parts(nc, "ro") as m:
        aff = m.sb("aff", [P, TILES, E])
        per_tile = m.sb("per_tile", [P, TILES])
        thresh = m.sb("thresh", [P, E])
        cand = m.sb("cand", [P, TRIES, E])
        kept = m.sb("kept", [P, TRIES, E])
        best = m.sb("best", [P, E])
        bits = m.sb("bits", [P, TRIES, E], I32)
        tried = m.sb("tried", [P, TRIES, TILES, E])
        tried_count = m.sb("tried_count", [P, TRIES, E])
        flags = m.sb("flags", [P, TILES, E])
        count = m.sb("count", [P, E])
        ones = m.sb("ones", [P, P])
        before = m.sb("before", [P, P])
        above = m.sb("above", [P, TILES, E])
        equal = m.sb("equal", [P, TILES, E])
        rank = m.sb("rank", [P, TILES, E])
        tiles_before = m.sb("tiles_before", [P, TILES, E])
        need = m.sb("need", [P, E])
        slot = m.sb("slot", [P, TILES, E])
        rest = m.sb("rest", [P, TILES, E])
        iota_s = m.sb("iota_s", [P, CAP], BF16)
        payload = m.sb("payload", [P, TILES, E, NPAY], BF16)
        slot_e = [m.sb(f"slot_e{b}", [P, TILES]) for b in range(2)]
        hot_d = [m.sb(f"hot_d{r}", [P, CAP], BF16) for r in range(RING_DVE)]
        hot_p = [m.sb(f"hot_p{r}", [P, CAP], BF16) for r in range(RING_POOL)]
        got = m.sb("got", [P, HALVES, E, NPAY])
        gate_part = m.sb("gate_part", [P, HALVES, E])
        token_f = m.sb("token_f", [P, HALVES, E])
        c_ps = m.psum("c_ps", [P, BANK])
        r_ps = m.psum("r_ps", [P, BANK])
        tot_ps = m.psum("tot_ps", [P, BANK])
        s_ps = m.psum("s_ps", [P, HALVES, BANK])

        consts = m.sem("consts")
        steps = m.sem("steps")
        exped = m.sem("exped")
        counted = m.sem("counted")
        counts_ready = m.sem("counts_ready")
        flags_ready = m.sem("flags_ready")
        sums_ready = m.sem("sums_ready")
        pay_ready = m.sem("pay_ready")
        slot_e_ready = m.sem("slot_e_ready")
        hot_d_ready, hot_d_used = m.sem("hot_d_ready"), m.sem("hot_d_used")
        hot_p_ready, hot_p_used = m.sem("hot_p_ready"), m.sem("hot_p_used")
        ticks = m.sem("ticks")
        block = m.block()

        @block.gpsimd
        def _(pool):
            pool.memset(ones[:, :], 1.0).then_inc(consts, 1)
            pool.memset(before[:, :], 1.0).then_inc(consts, 1)
            pool.wait_ge(consts, 2)
            pool.affine_select(out=before[:, :], in_=before[:, :], compare_op=ALU.is_gt, fill=0.0, base=0,
                               pattern=[[1, P]], channel_multiplier=-1).then_inc(consts, 1)
            pool.iota(iota_s[:, :], pattern=[[1, CAP]], base=0, channel_multiplier=0,
                      allow_small_or_imprecise_dtypes=True).then_inc(consts, 1)
            pool.memset(payload[:, :, :, :], 0.0).then_inc(consts, 1)
            pool.wait_ge(consts, 5)
            pool.iota(payload[:, :, :, 0], pattern=[[0, TILES], [0, E]], base=0, channel_multiplier=1,
                      allow_small_or_imprecise_dtypes=True).then_inc(consts, 1)
            pool.iota(payload[:, :, :, 1], pattern=[[1, TILES], [0, E]], base=0, channel_multiplier=0,
                      allow_small_or_imprecise_dtypes=True).then_inc(consts, 1)
            pool.wait_ge(consts, 7)
            with pool.Fori(0, E // 2) as e2:
                for b in range(2):
                    pool.wait_ge(slot_e_ready, e2 * 2 + (b + 1))
                    pool.sem_inc(ticks, 1)
                    for i, t in enumerate(BY_POOL):
                        pool.wait_ge(hot_p_used, e2 * (2 * len(BY_POOL)) + (b * len(BY_POOL) + i + 1))
                        pool.sem_inc(ticks, 1)
                        pool.tensor_scalar(hot_p[i % RING_POOL][:, :], iota_s[:, :], slot_e[b][:, t:t + 1], None, ALU.is_equal
                                           ).then_inc(hot_p_ready, 1)

        @block.scalar
        def _(act):
            act.wait_ge(steps, 2)
            act.activation(aff[:, :, :], aff[:, :, :], ACT.Exp).then_inc(exped, 1)

        @block.vector
        def _(dve):
            done = [0]

            def own(ins):
                done[0] += 1
                ins.then_inc(steps, 1)
                dve.wait_ge(steps, done[0])

            def over_tiles(a):
                return a.unsqueeze(1).to_broadcast([P, TILES, E])

            def over_experts(a):
                return a.unsqueeze(2).to_broadcast([P, TILES, E])

            own(dve.tensor_reduce(per_tile[:, :], logits[:, :, :], AX.X, ALU.max))
            own(dve.tensor_tensor(aff[:, :, :], logits[:, :, :], over_experts(per_tile[:, :]), ALU.subtract))
            dve.wait_ge(exped, 1)
            own(dve.tensor_reduce(per_tile[:, :], aff[:, :, :], AX.X, ALU.add))
            own(dve.reciprocal(per_tile[:, :], per_tile[:, :]))
            own(dve.tensor_tensor(aff[:, :, :], aff[:, :, :], over_experts(per_tile[:, :]), ALU.mult))
            own(dve.memset(thresh[:, :], 0.0))
            for c in range(TRIES):
                own(dve.memset(bits[:, c, :], (c + 1) << (BITS - STEP)))
            dve.wait_ge(consts, 7)
            base = done[0]
            with dve.Fori(0, BITS // STEP) as i:
                def mine(ins, k):
                    ins.then_inc(steps, 1)
                    dve.wait_ge(steps, i * 6 + (base + k))
                mine(dve.tensor_tensor(cand[:, :, :].bitcast(I32), thresh[:, :].bitcast(I32).unsqueeze(1).to_broadcast([P, TRIES, E]),
                                       bits[:, :, :], ALU.bitwise_or), 1)
                mine(dve.tensor_tensor(tried[:, :, :, :], aff[:, :, :].unsqueeze(1).to_broadcast([P, TRIES, TILES, E]),
                                       cand[:, :, :].unsqueeze(2).to_broadcast([P, TRIES, TILES, E]), ALU.is_ge), 2)
                dve.tensor_reduce(tried_count[:, :, :], tried[:, :, :, :].rearrange("p c t e -> p c e t"), AX.X, ALU.add
                                  ).then_inc(counted, 1)
                mine(dve.tensor_scalar(bits[:, :, :], bits[:, :, :], STEP, None, ALU.logical_shift_right), 3)
                dve.wait_ge(counts_ready, i + 1)
                mine(dve.scalar_tensor_tensor(out=kept[:, :, :], in0=c_ps[:, 0:TRIES * E].rearrange("p (c e) -> p c e", e=E),
                                              scalar=CAP - 0.5, in1=cand[:, :, :], op0=ALU.is_ge, op1=ALU.mult), 4)
                mine(dve.tensor_reduce(best[:, :], kept[:, :, :].rearrange("p c e -> p e c"), AX.X, ALU.max), 5)
                mine(dve.tensor_tensor(thresh[:, :], thresh[:, :], best[:, :], ALU.max), 6)
            done[0] = base + 6 * (BITS // STEP)

            def ranks(of, k):
                dve.nop().then_inc(flags_ready, 1)
                dve.wait_ge(sums_ready, k + 1)
                own(dve.memset(tiles_before[:, 0, :], 0.0))
                for t in range(1, TILES):
                    own(dve.tensor_tensor(tiles_before[:, t, :], tiles_before[:, t - 1, :],
                                          tot_ps[:, (t - 1) * E:t * E], ALU.add))
                own(dve.tensor_tensor(rank[:, :, :], r_ps[:, 0:TE].rearrange("p (t e) -> p t e", e=E),
                                      tiles_before[:, :, :], ALU.add))

            own(dve.tensor_tensor(above[:, :, :], aff[:, :, :], over_tiles(thresh[:, :]), ALU.is_gt))
            own(dve.tensor_tensor(equal[:, :, :], aff[:, :, :], over_tiles(thresh[:, :]), ALU.is_equal))
            dve.wait_ge(counts_ready, BITS // STEP)
            dve.tensor_reduce(count[:, :], above[:, :, :].rearrange("p t e -> p e t"), AX.X, ALU.add).then_inc(counted, 1)
            dve.wait_ge(counts_ready, BITS // STEP + 1)
            own(dve.tensor_scalar(need[:, :], c_ps[:, 0:E], -1.0, float(CAP), ALU.mult, ALU.add))
            ranks(equal, 0)
            own(dve.tensor_tensor(flags[:, :, :], rank[:, :, :], over_tiles(need[:, :]), ALU.is_lt))
            own(dve.tensor_tensor(equal[:, :, :], equal[:, :, :], flags[:, :, :], ALU.mult))
            own(dve.tensor_tensor(equal[:, :, :], equal[:, :, :], above[:, :, :], ALU.add))
            ranks(equal, 1)
            own(dve.scalar_tensor_tensor(out=slot[:, :, :], in0=rank[:, :, :], scalar=1.0, in1=equal[:, :, :],
                                         op0=ALU.add, op1=ALU.mult))
            own(dve.tensor_scalar(slot[:, :, :], slot[:, :, :], -1.0, None, ALU.add))
            own(dve.tensor_copy(payload[:, :, :, 2], aff[:, :, :]))
            own(dve.tensor_tensor(rest[:, :, :], aff[:, :, :], payload[:, :, :, 2], ALU.subtract))
            own(dve.tensor_copy(payload[:, :, :, 3], rest[:, :, :]))
            own(dve.tensor_tensor(rest[:, :, :], rest[:, :, :], payload[:, :, :, 3], ALU.subtract))
            own(dve.tensor_copy(payload[:, :, :, 4], rest[:, :, :]))
            credit(dve, pay_ready, 1)
            ND, NP = len(BY_DVE), len(BY_POOL)

            def two_experts(e2):
                for b in range(2):
                    if not numbered(e2, 0):
                        dve.wait_ge(hot_p_ready, e2 * (2 * NP) + (b * NP - NP))
                    dve.tensor_copy(slot_e[b][:, :], slot[:, :, bass.ds(e2 * 2 + b, 1)].rearrange("p t e -> p (t e)")
                                    ).then_inc(slot_e_ready, 1)
                    dve.wait_ge(slot_e_ready, e2 * 2 + (b + 1))
                    for i, t in enumerate(BY_DVE):
                        dve.wait_ge(hot_d_used, e2 * (2 * ND) + (b * ND + i + 1))
                        dve.tensor_scalar(hot_d[i % RING_DVE][:, :], iota_s[:, :], slot_e[b][:, t:t + 1], None, ALU.is_equal
                                          ).then_inc(hot_d_ready, 1)

            first_apart(dve, E // 2, two_experts)
            dve.wait_ge(hot_d_used, E * ND + RING_DVE)
            dve.wait_ge(hot_p_used, E * NP + RING_POOL)
            own(dve.tensor_copy(got[:, :, :, :], s_ps[:, :, 0:E * NPAY].rearrange("p a (e n) -> p a e n", n=NPAY)))
            own(dve.scalar_tensor_tensor(out=token_f[:, :, :], in0=got[:, :, :, 1], scalar=float(P), in1=got[:, :, :, 0],
                                         op0=ALU.mult, op1=ALU.add))
            own(dve.tensor_copy(slot_token[:, :, :], token_f[:, :, :]))
            own(dve.tensor_tensor(gate_part[:, :, :], got[:, :, :, 3], got[:, :, :, 4], ALU.add))
            own(dve.tensor_tensor(slot_gate[:, :, :], gate_part[:, :, :], got[:, :, :, 2], ALU.add))

        @block.tensor
        def _(pe):
            credit(pe, hot_d_used, RING_DVE)
            credit(pe, hot_p_used, RING_POOL)
            pe.wait_ge(consts, 7)
            with pe.Fori(0, BITS // STEP) as i:
                pe.wait_ge(counted, i + 1)
                pe.matmul(c_ps[:, 0:TRIES * E], ones[:, :], tried_count[:, :, :].rearrange("p c e -> p (c e)"),
                          start=True, stop=True).then_inc(counts_ready, 1)
            pe.wait_ge(counted, BITS // STEP + 1)
            pe.matmul(c_ps[:, 0:E], ones[:, :], count[:, :], start=True, stop=True).then_inc(counts_ready, 1)
            for k in range(2):
                pe.wait_ge(flags_ready, k + 1)
                flat = equal[:, :, :].rearrange("p t e -> p (t e)")
                pe.matmul(r_ps[:, 0:TE], before[:, :], flat, start=True, stop=True)
                pe.matmul(tot_ps[:, 0:TE], ones[:, :], flat, start=True, stop=True).then_inc(sums_ready, 1)
            pe.wait_ge(pay_ready, 1)
            with pe.Fori(0, E) as e:
                for t in range(TILES):
                    if t in BY_POOL:
                        i, tiles, ring, ready, used = BY_POOL.index(t), BY_POOL, hot_p, hot_p_ready, hot_p_used
                    else:
                        i, tiles, ring, ready, used = BY_DVE.index(t), BY_DVE, hot_d, hot_d_ready, hot_d_used
                    pe.wait_ge(ready, e * len(tiles) + (i + 1))
                    for a in range(HALVES):
                        mm = pe.matmul(s_ps[:, a, bass.ds(e * NPAY, NPAY)], ring[i % len(ring)][:, a * P:(a + 1) * P],
                                       payload[:, t, bass.ds(e, 1), :].rearrange("p a n -> p (a n)"),
                                       start=(t == 0), stop=(t == TILES - 1))
                    mm.then_inc(used, 1)


def experts(nc, hn_moe, w_gate, w_up, w_down, slot_token, slot_gate, h_res):
    CH = 2 * P
    NC = F // CH
    PER = 3 * NC
    RING = 3
    HALVES = CAP // P
    FB = CH // P
    with Parts(nc, "ex") as m:
        ident = m.sb("ident", [P, P])
        w_st = [m.sb(f"w_st{r}", [P, KB * CH]) for r in range(RING)]
        w_hi = [m.sb(f"w_hi{r}", [P, KB * CH], F32R) for r in range(RING)]
        w_lo = [m.sb(f"w_lo{r}", [P, KB * CH], F32R) for r in range(RING)]
        tokens = m.sb("tokens", [P, HALVES], U32)
        tokens_out = m.sb("tokens_out", [P, HALVES], U32)
        rows = m.sb("rows", [P, HALVES, D])
        xt_hi = m.sb("xt_hi", [P, KB, CAP], F32R)
        xt_lo = m.sb("xt_lo", [P, KB, CAP], F32R)
        silu = [m.sb(f"silu{b}", [P, FB * CAP]) for b in range(2)]
        hid = [m.sb(f"hid{b}", [P, FB * CAP]) for b in range(2)]
        hid_hi = m.sb("hid_hi", [P, NC, FB * CAP], F32R)
        hid_lo = m.sb("hid_lo", [P, NC, FB * CAP], F32R)
        y = m.sb("y", [P, HALVES, D])
        gu_ps = m.psum("gu_ps", [P, 4, BANK])
        y_ps = m.psum("y_ps", [P, HALVES, D])

        sem = m.sem
        consts = sem("consts")
        w_loaded = [sem(f"w_loaded{r}") for r in range(RING)]
        whi_ready, wlo_ready, w_used = sem("whi_ready"), sem("wlo_ready"), sem("w_used")
        tokens_ready, tokens_out_ready = sem("tokens_ready"), sem("tokens_out_ready")
        gathered, turned, xthi_ready, xtlo_ready = sem("gathered"), sem("turned"), sem("xthi_ready"), sem("xtlo_ready")
        silu_ready, hid_ready, hidhi_ready, hidlo_ready = sem("silu_ready"), sem("hid_ready"), sem("hidhi_ready"), sem("hidlo_ready")
        y_ready, y_scaled, y_free, added, ticks = sem("y_ready"), sem("y_scaled"), sem("y_free"), sem("added"), sem("ticks")
        block = m.block()

        def wide(t):
            return t[:, :].rearrange("p (k c) -> p k c", c=CH)

        def tall(t):
            return t[:, :].rearrange("p (k c) -> p k c", c=D)

        def all_experts(eng, fn):
            fn(0)
            with eng.Fori(1, E - 1) as e:
                fn(e)
            fn(E - 1)

        @block.sync
        def _(sp):
            def expert(e):
                for c in range(PER):
                    r = c % RING
                    first = isinstance(e, int) and e == 0 and c < RING
                    if not first:
                        sp.wait_ge(wlo_ready, e * PER + (c - RING + 1))
                    q, kind = (c // 2, c % 2) if c < 2 * NC else (c - 2 * NC, 2)
                    if kind < 2:
                        src = (w_gate, w_up)[kind][0].rearrange("e (k p) c -> e p k c", p=P)[
                            bass.ds(e, 1), :, :, q * CH:(q + 1) * CH].rearrange("e p k c -> (e p) k c")
                        dst = wide(w_st[r])
                    else:
                        src = w_down[0].rearrange("e (k p) c -> e p k c", p=P)[
                            bass.ds(e, 1), :, FB * q:FB * (q + 1), :].rearrange("e p k c -> (e p) k c")
                        dst = tall(w_st[r])
                    sp.dma_start(dst, src).then_inc(w_loaded[r], 16)

            all_experts(sp, expert)

        @block.gpsimd
        def _(pool):
            identity_steps(pool, ident, consts)
            credit(pool, y_free, 1)

            def gather(e):
                pool.tensor_copy(tokens[:, :], slot_token[:, :, bass.ds(e, 1)].rearrange("p a e -> p (a e)")
                                 ).then_inc(tokens_ready, 1)
                pool.wait_ge(tokens_ready, e + 1)
                pool.sem_inc(ticks, 1)
                for a in range(HALVES):
                    pool.indirect_dma_start(out=rows[:, a, :], out_offset=None, in_=hn_moe,
                                            in_offset=bass.IndirectOffsetOnAxis(ap=tokens[:, a:a + 1], axis=0)
                                            ).then_inc(gathered, 16)

            def expert(e):
                if not (isinstance(e, int) and e == E - 1):
                    pool.wait_ge(turned, e * 4 + 4)
                    pool.sem_inc(ticks, 1)
                    gather(e + 1)
                if not (isinstance(e, int) and e == 0):
                    pool.wait_ge(added, e * 32)
                    pool.sem_inc(y_free, 1)
                pool.tensor_copy(tokens_out[:, :], slot_token[:, :, bass.ds(e, 1)].rearrange("p a e -> p (a e)")
                                 ).then_inc(tokens_out_ready, 1)
                pool.wait_ge(tokens_out_ready, e + 1)
                pool.wait_ge(y_scaled, e * 2 + 2)
                pool.sem_inc(ticks, 1)
                for a in range(HALVES):
                    pool.indirect_dma_start(out=h_res, out_offset=bass.IndirectOffsetOnAxis(ap=tokens_out[:, a:a + 1], axis=0),
                                            in_=y[:, a, :], in_offset=None, compute_op=ALU.add).then_inc(added, 16)

            gather(0)
            all_experts(pool, expert)
            pool.wait_ge(added, 32 * E)

        @block.scalar
        def _(act):
            def split_w(e, c):
                r = c % RING
                act.wait_ge(w_loaded[r], (e * (PER // RING) + (c // RING + 1)) * 16)
                if not (isinstance(e, int) and e == 0 and c < RING):
                    act.wait_ge(w_used, e * PER + (c - RING + 1))
                act.activation(w_hi[r][:, :], w_st[r][:, :], ACT.Copy).then_inc(whi_ready, 1)

            def split_x(e, g):
                act.wait_ge(turned, e * 4 + (g + 1))
                act.activation(xt_hi[:, 2 * g:2 * g + 2, :], gu_ps[:, g, :].rearrange("p (k s) -> p k s", s=CAP), ACT.Copy
                               ).then_inc(xthi_ready, 1)

            def hidden(e, q):
                b = q % 2
                act.wait_ge(w_used, e * PER + (2 * q + 1))
                if not (isinstance(e, int) and e == 0 and q < 2):
                    act.wait_ge(hid_ready, e * NC + (q - 1))
                act.activation(silu[b][:, :], gu_ps[:, 2 * b, :], ACT.Silu).then_inc(silu_ready, 1)

            def hidden_hi(e, q):
                act.wait_ge(hid_ready, e * NC + (q + 1))
                if q == 0 and not (isinstance(e, int) and e == 0):
                    act.wait_ge(w_used, e * PER)
                act.activation(hid_hi[:, q, :], hid[q % 2][:, :], ACT.Copy).then_inc(hidhi_ready, 1)

            def expert(e):
                for q in range(NC):
                    for c in (2 * q, 2 * q + 1):
                        if not (isinstance(e, int) and e == 0 and c < 2):
                            split_w(e, c)
                    if q:
                        hidden(e, q - 1)
                        hidden_hi(e, q - 1)
                split_w(e, 2 * NC)
                hidden(e, NC - 1)
                hidden_hi(e, NC - 1)
                last = isinstance(e, int) and e == E - 1
                for q in range(1, NC):
                    split_w(e, 2 * NC + q)
                    if not last:
                        if q == 1:
                            for g in range(2):
                                split_x(e + 1, g)
                        if q == 2:
                            for g in range(2, 4):
                                split_x(e + 1, g)

            for c in range(2):
                split_w(0, c)
            for g in range(4):
                split_x(0, g)
            all_experts(act, expert)

        @block.vector
        def _(dve):
            def split_w(e, c):
                r = c % RING
                dve.wait_ge(whi_ready, e * PER + (c + 1))
                dve.tensor_tensor(w_lo[r][:, :], w_st[r][:, :], w_hi[r][:, :].bitcast(F32), ALU.subtract
                                  ).then_inc(wlo_ready, 1)

            def split_x(e, g):
                dve.wait_ge(xthi_ready, e * 4 + (g + 1))
                dve.tensor_tensor(xt_lo[:, 2 * g:2 * g + 2, :], gu_ps[:, g, :].rearrange("p (k s) -> p k s", s=CAP),
                                  xt_hi[:, 2 * g:2 * g + 2, :].bitcast(F32), ALU.subtract).then_inc(xtlo_ready, 1)

            def hidden(e, q):
                b = q % 2
                dve.wait_ge(w_used, e * PER + (2 * q + 2))
                dve.wait_ge(silu_ready, e * NC + (q + 1))
                if not (isinstance(e, int) and e == 0 and q < 2):
                    dve.wait_ge(hidlo_ready, e * NC + (q - 1))
                dve.tensor_tensor(hid[b][:, :], silu[b][:, :], gu_ps[:, 2 * b + 1, :], ALU.mult).then_inc(hid_ready, 1)

            def hidden_lo(e, q):
                dve.wait_ge(hidhi_ready, e * NC + (q + 1))
                dve.tensor_tensor(hid_lo[:, q, :], hid[q % 2][:, :], hid_hi[:, q, :].bitcast(F32), ALU.subtract
                                  ).then_inc(hidlo_ready, 1)

            def scale_y(e):
                dve.wait_ge(y_ready, e + 1)
                dve.wait_ge(y_free, e + 1)
                for a in range(HALVES):
                    dve.tensor_scalar(y[:, a, :], y_ps[:, a, :], slot_gate[:, a, bass.ds(e, 1)], None, ALU.mult
                                      ).then_inc(y_scaled, 1)

            def expert(e):
                for q in range(NC):
                    for c in (2 * q, 2 * q + 1):
                        if not (isinstance(e, int) and e == 0 and c < 2):
                            split_w(e, c)
                    if q == 1 and not (isinstance(e, int) and e == 0):
                        scale_y(e - 1)
                    if q:
                        hidden(e, q - 1)
                        hidden_lo(e, q - 1)
                split_w(e, 2 * NC)
                hidden(e, NC - 1)
                hidden_lo(e, NC - 1)
                last = isinstance(e, int) and e == E - 1
                for q in range(1, NC):
                    split_w(e, 2 * NC + q)
                    if not last:
                        if q == 1:
                            for g in range(2):
                                split_x(e + 1, g)
                        if q == 2:
                            for g in range(2, 4):
                                split_x(e + 1, g)

            for c in range(2):
                split_w(0, c)
            for g in range(4):
                split_x(0, g)
            all_experts(dve, expert)
            scale_y(E - 1)

        @block.tensor
        def _(pe):
            pe.wait_ge(consts, 2)

            def turn(e):
                pe.wait_ge(gathered, e * 32 + 32)
                if not (isinstance(e, int) and e == 0):
                    pe.wait_ge(hid_ready, e * NC - 1)
                for g in range(4):
                    if g == 2 and not (isinstance(e, int) and e == 0):
                        pe.wait_ge(hid_ready, e * NC)
                    for k in range(2 * g, 2 * g + 2):
                        for a in range(HALVES):
                            t = pe.transpose(gu_ps[:, g, (k % 2) * CAP + a * P:(k % 2) * CAP + (a + 1) * P],
                                             rows[:, a, k * P:(k + 1) * P], ident[:, :])
                    t.then_inc(turned, 1)

            def gate_up(e, c):
                r, q, kind = c % RING, c // 2, c % 2
                bank = 2 * (q % 2) + kind
                pe.wait_ge(wlo_ready, e * PER + (c + 1))
                if c == 0:
                    pe.wait_ge(xtlo_ready, e * 4 + 4)
                elif c >= 4:
                    pe.wait_ge(hid_ready, e * NC + (q - 1))
                hi, lo = wide(w_hi[r]), wide(w_lo[r])
                for f in range(FB):
                    dst, cols = gu_ps[:, bank, f * CAP:(f + 1) * CAP], slice(f * P, (f + 1) * P)
                    for k in range(KB):
                        pe.matmul(dst, hi[:, k, cols], xt_hi[:, k, :], start=(k == 0), stop=False)
                        pe.matmul(dst, hi[:, k, cols], xt_lo[:, k, :], start=False, stop=False)
                        mm = pe.matmul(dst, lo[:, k, cols], xt_hi[:, k, :], start=False, stop=(k == KB - 1))
                mm.then_inc(w_used, 1)

            def down(e, q):
                c = 2 * NC + q
                r = c % RING
                pe.wait_ge(wlo_ready, e * PER + (c + 1))
                pe.wait_ge(hidlo_ready, e * NC + (q + 1))
                if q == 0 and not (isinstance(e, int) and e == 0):
                    pe.wait_ge(y_scaled, e * 2)
                hi, lo = tall(w_hi[r]), tall(w_lo[r])
                for f in range(FB):
                    for a in range(HALVES):
                        slots = slice(f * CAP + a * P, f * CAP + (a + 1) * P)
                        for n in range(D // BANK):
                            cols = slice(n * BANK, (n + 1) * BANK)
                            dst = y_ps[:, a, cols]
                            first, last = q == 0 and f == 0, q == NC - 1 and f == FB - 1
                            pe.matmul(dst, hid_hi[:, q, slots], hi[:, f, cols], start=first, stop=False)
                            pe.matmul(dst, hid_hi[:, q, slots], lo[:, f, cols], start=False, stop=False)
                            mm = pe.matmul(dst, hid_lo[:, q, slots], hi[:, f, cols], start=False, stop=last)
                mm.then_inc(w_used, 1)
                if q == NC - 1:
                    pe.wait_ge(w_used, e * PER + PER)
                    pe.nop().then_inc(y_ready, 1)

            def expert(e):
                for c in range(2 * NC):
                    gate_up(e, c)
                if not (isinstance(e, int) and e == E - 1):
                    turn(e + 1)
                for q in range(NC):
                    down(e, q)

            turn(0)
            all_experts(pe, expert)


def gated_ple(nc, h_res, p_emb, g_ple, w_ple_gate, w_ple_proj, g_final, out):
    PB = PLE // P
    EARLY = 4
    WS = 4
    KT = KB + PB
    GROUPS = [(0, 4), (4, 8), (8, 10)]
    with Parts(nc, "pl") as m:
        ident = m.sb("ident", [P, P])
        w_st = [m.sb(f"w_st{r}", [P, D]) for r in range(WS)]
        w_hi = m.sb("w_hi", [P, KT, D], F32R)
        w_lo = m.sb("w_lo", [P, KT, D], F32R)
        g_in = m.sb("g_in", [P, D])
        g_out = m.sb("g_out", [P, D])
        mhalf = m.sb("mhalf", [P, 1])
        h_in = [m.sb(f"h_in{i}", [P, D]) for i in range(4)]
        p_in = [m.sb(f"p_in{b}", [P, PLE]) for b in range(2)]
        sq = m.sb("sq", [P, D])
        ss, ms, rs = (m.sb(n, [P, 1]) for n in ("ss", "ms", "rs"))
        ss2, ms2, rs2 = (m.sb(n, [P, 1]) for n in ("ss2", "ms2", "rs2"))
        hn = [m.sb(f"hn{b}", [P, D]) for b in range(2)]
        t_hi = [m.sb(f"t_hi{b}", [P, KT, P], F32R) for b in range(2)]
        t_lo = [m.sb(f"t_lo{b}", [P, KT, P], F32R) for b in range(2)]
        gate = m.sb("gate", [P, D])
        mixed = m.sb("mixed", [P, D])
        out_sb = [m.sb(f"out_sb{b}", [P, D]) for b in range(2)]
        t_ps = m.psum("t_ps", [P, 3, BANK])
        g_ps = m.psum("g_ps", [P, D])
        p_ps = m.psum("p_ps", [P, D])

        sem = m.sem
        consts, mhalf_ready, gains_loaded = sem("consts"), sem("mhalf_ready"), sem("gains_loaded")
        w_loaded = [sem(f"w_loaded{r}") for r in range(WS)]
        whi_ready, wlo_ready = sem("whi_ready"), sem("wlo_ready")
        h_loaded = [sem(f"h_loaded{i}") for i in range(4)]
        p_loaded = [sem(f"p_loaded{b}") for b in range(2)]
        squared, means, rsqrt, normed, turned, thi_ready, tlo_ready = (
            sem(n) for n in ("squared", "means", "rsqrt", "normed", "turned", "thi_ready", "tlo_ready"))
        g_ready, p_ready, gated, mixed_ready, h_ready, squared2, means2, rsqrt2, out_ready = (
            sem(n) for n in ("g_ready", "p_ready", "gated", "mixed_ready", "h_ready", "squared2", "means2", "rsqrt2", "out_ready"))
        out_stored = [sem(f"out_stored{b}") for b in range(2)]
        block = m.block()

        def run(eng, fn, start=0):
            for n in range(start, 4):
                fn(n, n, n)
            with eng.Fori(1, TILES // 4 - 1) as j:
                for s in range(4):
                    fn(j * 4 + s, s, None)
            for n in range(TILES - 4, TILES + 2):
                fn(n, n % 4, n)

        def has(i, lag):
            return i is None or 0 <= i - lag < TILES

        def h_turns(n, s):
            return n * 4 + (16 - 4 * s)

        @block.sync
        def _(sp):
            for g, dst in ((g_ple, g_in), (g_final.rearrange("(l n) -> l n", l=1), g_out)):
                sp.dma_start(dst[:, :], g.partition_broadcast(P).rearrange("p l n -> p (l n)")).then_inc(gains_loaded, 16)
            for n in range(2):
                sp.dma_start(h_in[n][:, :], h_res[n * P:(n + 1) * P, :]).then_inc(h_loaded[n], 16)
                sp.dma_start(p_in[n][:, :], p_emb[0, 0, n * P:(n + 1) * P, :]).then_inc(p_loaded[n], 16)
            for k in range(KT):
                if k >= WS:
                    sp.wait_ge(wlo_ready, k - WS + 1)
                src = w_ple_gate[0, k * P:(k + 1) * P, :] if k < KB else w_ple_proj[0, (k - KB) * P:(k - KB + 1) * P, :]
                sp.dma_start(w_st[k % WS][:, :], src).then_inc(w_loaded[k % WS], 16)

            def step(n, s, i):
                b = s % 2
                if i is None or 2 <= i < TILES:
                    if i is None or i >= 4:
                        sp.wait_ge(h_ready, n - 3)
                        sp.wait_ge(out_ready, n - 3)
                    sp.dma_start(h_in[s][:, :], h_res[bass.ds(n * P, P), :]).then_inc(h_loaded[s], 16)
                    sp.wait_ge(turned, 3 * (n - 1))
                    sp.dma_start(p_in[b][:, :], p_emb[0, 0, bass.ds(n * P, P), :]).then_inc(p_loaded[b], 16)
                if has(i, 2):
                    sp.wait_ge(out_ready, n - 1)
                    sp.dma_start(out[0, bass.ds((n - 2) * P, P), :], out_sb[b][:, :]).then_inc(out_stored[b], 16)

            run(sp, step)
            for b in range(2):
                sp.wait_ge(out_stored[b], 8 * TILES)

        @block.gpsimd
        def _(pool):
            identity_steps(pool, ident, consts)
            pool.memset(mhalf[:, :], -0.5).then_inc(mhalf_ready, 1)
            pool.wait_ge(mhalf_ready, 1)

            def norm(n):
                pool.wait_ge(means, n + 1)
                pool.tensor_tensor(rs[:, :], ms[:, :], mhalf[:, :], ALU.pow).then_inc(rsqrt, 1)

            def step(n, s, i):
                if i is None or i < TILES - 1:
                    norm(n + 1)
                if has(i, 1):
                    pool.wait_ge(means2, n)
                    pool.tensor_tensor(rs2[:, :], ms2[:, :], mhalf[:, :], ALU.pow).then_inc(rsqrt2, 1)

            norm(0)
            run(pool, step)

        @block.scalar
        def _(act):
            def square(n, s):
                act.wait_ge(h_loaded[s], h_turns(n, s))
                if not isinstance(n, int) or n >= 1:
                    act.wait_ge(means, n)
                    act.wait_ge(squared, n)
                if not isinstance(n, int) or n >= 3:
                    act.wait_ge(squared2, n - 2)
                act.activation(sq[:, :], h_in[s][:, :], ACT.Square, accum_out=ss[:, :]).then_inc(squared, 1)

            square(0, 0)
            def split_w(k):
                act.wait_ge(w_loaded[k % WS], 16 * (k // WS + 1))
                act.activation(w_hi[:, k, :], w_st[k % WS][:, :], ACT.Copy).then_inc(whi_ready, 1)

            def step(n, s, i):
                b = s % 2
                if has(i, 0):
                    for g, (lo, hi) in enumerate(GROUPS):
                        act.wait_ge(turned, 3 * n + (g + 1))
                        if g == 0 and (i is None or i >= 2):
                            act.wait_ge(p_ready, n - 1)
                        act.activation(t_hi[b][:, lo:hi, :], t_ps[:, g, 0:(hi - lo) * P].rearrange("p (k t) -> p k t", t=P),
                                       ACT.Copy).then_inc(thi_ready, 1)
                if i is None or i < TILES - 1:
                    square(n + 1, (s + 1) % 4)
                if has(i, 1):
                    act.wait_ge(g_ready, n)
                    if i is None or i >= 2:
                        act.wait_ge(mixed_ready, n - 1)
                    act.activation(gate[:, :], g_ps[:, :], ACT.Sigmoid).then_inc(gated, 1)
                    act.wait_ge(h_ready, n)
                    if i is None or i >= 2:
                        act.wait_ge(means2, n - 1)
                    if i is None or i < TILES - 1:
                        act.wait_ge(squared, n + 2)
                    else:
                        act.wait_ge(squared, TILES)
                    act.activation(sq[:, :], h_in[(s + 3) % 4][:, :], ACT.Square, accum_out=ss2[:, :]).then_inc(squared2, 1)

            for k in range(KT):
                if k == EARLY:
                    step(0, 0, 0)
                split_w(k)
            run(act, step, 1)

        @block.vector
        def _(dve):
            dve.wait_ge(gains_loaded, 32)

            def norm(n, s):
                b = s % 2
                dve.wait_ge(squared, n + 1)
                if not isinstance(n, int) or n >= 1:
                    dve.wait_ge(rsqrt, n)
                dve.tensor_scalar(ms[:, :], ss[:, :], 1.0 / D, EPS, ALU.mult, ALU.add).then_inc(means, 1)
                dve.wait_ge(rsqrt, n + 1)
                if not isinstance(n, int) or n >= 2:
                    dve.wait_ge(turned, 3 * n - 3)
                dve.scalar_tensor_tensor(out=hn[b][:, :], in0=h_in[s][:, :], scalar=rs[:, 0:1], in1=g_in[:, :],
                                         op0=ALU.mult, op1=ALU.mult).then_inc(normed, 1)

            norm(0, 0)
            def split_w(k):
                dve.wait_ge(whi_ready, k + 1)
                dve.tensor_tensor(w_lo[:, k, :], w_st[k % WS][:, :], w_hi[:, k, :].bitcast(F32), ALU.subtract
                                  ).then_inc(wlo_ready, 1)

            def step(n, s, i):
                b = s % 2
                if has(i, 0):
                    for g, (lo, hi) in enumerate(GROUPS):
                        dve.wait_ge(thi_ready, 3 * n + (g + 1))
                        dve.tensor_tensor(t_lo[b][:, lo:hi, :], t_ps[:, g, 0:(hi - lo) * P].rearrange("p (k t) -> p k t", t=P),
                                          t_hi[b][:, lo:hi, :].bitcast(F32), ALU.subtract).then_inc(tlo_ready, 1)
                if i is None or i < TILES - 1:
                    norm(n + 1, (s + 1) % 4)
                if has(i, 1):
                    h = h_in[(s + 3) % 4]
                    dve.wait_ge(gated, n)
                    dve.wait_ge(p_ready, n)
                    dve.tensor_tensor(mixed[:, :], p_ps[:, :], gate[:, :], ALU.mult).then_inc(mixed_ready, 1)
                    dve.wait_ge(mixed_ready, n)
                    dve.tensor_tensor(h[:, :], h[:, :], mixed[:, :], ALU.add).then_inc(h_ready, 1)
                    dve.wait_ge(squared2, n)
                    if i is None or i >= 2:
                        dve.wait_ge(rsqrt2, n - 1)
                    dve.tensor_scalar(ms2[:, :], ss2[:, :], 1.0 / D, EPS, ALU.mult, ALU.add).then_inc(means2, 1)
                    dve.wait_ge(rsqrt2, n)
                    if i is None or i >= 3:
                        dve.wait_ge(out_stored[1 - b], n * 8 + (-16 if b == 0 else -8))
                    dve.scalar_tensor_tensor(out=out_sb[1 - b][:, :], in0=h[:, :], scalar=rs2[:, 0:1], in1=g_out[:, :],
                                             op0=ALU.mult, op1=ALU.mult).then_inc(out_ready, 1)

            for k in range(KT):
                if k == EARLY:
                    step(0, 0, 0)
                split_w(k)
            run(dve, step, 1)

        @block.tensor
        def _(pe):
            pe.wait_ge(consts, 2)

            def products(n, b, i):
                c = 1 - b
                pe.wait_ge(tlo_ready, 3 * n)
                if i is not None and i == 1:
                    pe.wait_ge(wlo_ready, KT)
                for dst, lo, hi, done in ((g_ps, 0, KB, g_ready), (p_ps, KB, KT, p_ready)):
                    if i is None or i >= 2:
                        pe.wait_ge(gated if lo == 0 else mixed_ready, n - 1)
                    for half in range(2):
                        cols = slice(half * BANK, (half + 1) * BANK)
                        for k in range(lo, hi):
                            pe.matmul(dst[:, cols], t_hi[c][:, k, :], w_hi[:, k, cols], start=(k == lo), stop=False)
                            pe.matmul(dst[:, cols], t_hi[c][:, k, :], w_lo[:, k, cols], start=False, stop=False)
                            mm = pe.matmul(dst[:, cols], t_lo[c][:, k, :], w_hi[:, k, cols], start=False, stop=(k == hi - 1))
                    mm.then_inc(done, 1)

            def step(n, s, i):
                b = s % 2
                if has(i, 0):
                    pe.wait_ge(normed, n + 1)
                    pe.wait_ge(p_loaded[b], n * 8 + (16 - 8 * b))
                    for g, (lo, hi) in enumerate(GROUPS):
                        if i is None or i >= 1:
                            pe.wait_ge(tlo_ready, 3 * n + (g - 2))
                        for k in range(lo, hi):
                            src = hn[b][:, k * P:(k + 1) * P] if k < KB else p_in[b][:, (k - KB) * P:(k - KB + 1) * P]
                            t = pe.transpose(t_ps[:, g, (k - lo) * P:(k - lo + 1) * P], src, ident[:, :])
                        t.then_inc(turned, 1)
                if has(i, 1):
                    products(n, b, i)

            run(pe, step)


def encoder_layer(nc, x, p, g_mix, w_in, na_rpb, g_na_out, lam_q1, lam_k1, lam_q2, lam_k2, g_diff_out, w_out, g_moe,
                  w_router, w_gate, w_up, w_down, g_ple, w_ple_gate, w_ple_proj, g_final, out):
    def dram(name, *shape):
        return nc.dram_tensor(name, shape, F32).ap()

    feat_t = dram("feat_t", 2, D, SEQ)
    v_tok = dram("v_tok", 2, SEQ, D // 2)
    alibi = dram("alibi", DIFF_HEADS, P, 2 * SEQ - P)
    rpb_rows = dram("rpb_rows", NA_HEADS * (2 * KH - 1), 2 * GRID_W - 1)
    na_bias = dram("na_bias", PAIRS, P, (2 * KH - 1) * GRID_W)
    o_cat = dram("o_cat", SEQ, D)
    h_res = dram("h_res", SEQ, D)
    hn_moe = dram("hn_moe", SEQ, D)
    project(nc, x, g_mix, w_in, feat_t, v_tok)
    bias_tables(nc, na_rpb, rpb_rows, na_bias)
    neighbourhood(nc, feat_t, v_tok, na_bias, alibi, o_cat)
    differential(nc, feat_t, v_tok, alibi, (lam_q1, lam_k1, lam_q2, lam_k2), o_cat)
    with Parts(nc, "routes") as m:
        logits = m.sb("logits", [P, TILES, E])
        slot_token = m.sb("slot_token", [P, CAP // P, E], U32)
        slot_gate = m.sb("slot_gate", [P, CAP // P, E])
        mix_out(nc, x, o_cat, g_na_out, g_diff_out, w_out, g_moe, w_router, h_res, hn_moe, logits)
        route(nc, logits, slot_token, slot_gate)
        experts(nc, hn_moe, w_gate, w_up, w_down, slot_token, slot_gate, h_res)
    gated_ple(nc, h_res, p, g_ple, w_ple_gate, w_ple_proj, g_final, out)


def kernel(**inputs):
    import concourse.bacc as bacc
    import numpy as np
    from concourse.bass_utils import run_bass_kernel_spmd

    names = ["x", "p", "g_mix", "w_in", "na_rpb", "g_na_out", "lam_q1", "lam_k1", "lam_q2", "lam_k2", "g_diff_out",
             "w_out", "g_moe", "w_router", "w_gate", "w_up", "w_down", "g_ple", "w_ple_gate", "w_ple_proj", "g_final"]
    nc = bacc.Bacc("TRN2", target_bir_lowering=False, num_devices=1)
    arrays, args = {}, []
    for name in names:
        a = np.ascontiguousarray(inputs[name])
        arrays[f"in_{name}"] = a
        args.append(nc.dram_tensor(f"in_{name}", a.shape, mybir.dt.from_np(a.dtype), kind="ExternalInput").ap())
    out = nc.dram_tensor("out", (1, SEQ, D), F32, kind="ExternalOutput").ap()
    encoder_layer(nc, *args, out)
    r = run_bass_kernel_spmd(nc, [arrays], core_ids=[0])
    return r.results[0]["out"]
```
